# Optimizing a Trainium2 kernel written in Bass

```python
import math
import jax, jax.numpy as jnp
from jax import lax
import numpy as np

D_MODEL = 1024
BATCH = 1
SEQ = 256
DEPTH = 1

D_PLE = 256
M_HEADS = 4
M_QK = 128
M_V = 256
M_WIDTH = M_HEADS * M_V
M_CHUNK = 64
CONV_W = 4
A_HEADS = 8
A_DH = 64
A_WIDTH = A_HEADS * A_DH
IDX_HEADS = 8
IDX_DH = 64
TOPK_MAX = 256
Q_BLOCK = 128
REL_BUCKETS = 32
REL_MAX_DIST = 128
D_MIX = M_WIDTH + A_WIDTH
EPS = 1e-6

PROJ_SIZES = [
    M_HEADS * M_QK,
    M_HEADS * M_QK,
    M_WIDTH,
    M_WIDTH,
    M_WIDTH,
    2 * M_HEADS,
    A_WIDTH,
    A_WIDTH,
    A_WIDTH,
    A_WIDTH,
    IDX_HEADS * IDX_DH,
    IDX_DH,
    IDX_HEADS,
]
PROJ_TOTAL = int(sum(PROJ_SIZES))
SPLIT_POINTS = [int(v) for v in np.cumsum(PROJ_SIZES)[:-1]]


def rmsnorm(x, g):
    xf = x.astype(jnp.float32)
    y = xf * lax.rsqrt(jnp.mean(xf * xf, axis=-1, keepdims=True) + EPS)
    return (y * g.astype(jnp.float32)).astype(x.dtype)

def causal_dwconv(x, w):
    S = x.shape[1]
    xp = jnp.pad(x, ((0, 0), (CONV_W - 1, 0), (0, 0)))
    y = xp[:, 0:S] * w[0]
    for j in range(1, CONV_W):
        y = y + xp[:, j:j + S] * w[j]
    return y

def mlstm_chunkwise(q, k, v, log_i, log_f):
    f32 = jnp.float32
    B, S, H, Dk = q.shape
    Dv = v.shape[-1]
    L = M_CHUNK
    NC = S // L

    def to_chunks(a):
        return a.reshape((B, NC, L) + a.shape[2:]).swapaxes(0, 1)

    qc = to_chunks(q.astype(f32))
    kc = to_chunks(k.astype(f32) * (Dk ** -0.5))
    vc = to_chunks(v.astype(f32))
    ic = to_chunks(log_i.astype(f32))
    fc = to_chunks(log_f.astype(f32))
    causal = jnp.tril(jnp.ones((L, L), dtype=bool))

    def step(carry, inp):
        C, n, m = carry
        q_, k_, v_, li, lf = inp
        b = jnp.cumsum(lf, axis=1).transpose(0, 2, 1)
        li_h = li.transpose(0, 2, 1)
        D = b[:, :, :, None] - b[:, :, None, :] + li_h[:, :, None, :]
        D = jnp.where(causal, D, -jnp.inf)
        inter = b + m[:, :, None]
        m_t = jnp.maximum(inter, D.max(-1))
        s = jnp.einsum('blhd,bshd->bhls', q_, k_) * jnp.exp(D - m_t[..., None])
        w_inter = jnp.exp(inter - m_t)
        num = (jnp.einsum('bhls,bshv->blhv', s, v_)
               + w_inter.transpose(0, 2, 1)[..., None] * jnp.einsum('blhd,bhdv->blhv', q_, C))
        den = s.sum(-1) + w_inter * jnp.einsum('blhd,bhd->bhl', q_, n)
        den = jnp.maximum(jnp.abs(den), jnp.exp(-m_t))
        h = num / den.transpose(0, 2, 1)[..., None]
        b_L = b[:, :, -1]
        g = b_L[:, :, None] - b + li_h
        m_new = jnp.maximum(b_L + m, g.max(-1))
        wk = jnp.exp(g - m_new[..., None])
        decay = jnp.exp(b_L + m - m_new)
        C_new = decay[..., None, None] * C + jnp.einsum('bhs,bshd,bshv->bhdv', wk, k_, v_)
        n_new = decay[..., None] * n + jnp.einsum('bhs,bshd->bhd', wk, k_)
        return (C_new, n_new, m_new), h

    init = (jnp.zeros((B, H, Dk, Dv), f32), jnp.zeros((B, H, Dk), f32), jnp.zeros((B, H), f32))
    _, hs = lax.scan(step, init, (qc, kc, vc, ic, fc))
    return hs.swapaxes(0, 1).reshape(B, S, H, Dv)

def t5_bucket(dist):
    max_exact = REL_BUCKETS // 2
    large = max_exact + (jnp.log(jnp.maximum(dist, 1).astype(jnp.float32) / max_exact)
                         / math.log(REL_MAX_DIST / max_exact) * (REL_BUCKETS - max_exact)).astype(jnp.int32)
    large = jnp.minimum(large, REL_BUCKETS - 1)
    return jnp.where(dist < max_exact, dist, large)

def dsa_attention(q, k, v, iq, ik, iw, rel_bias):
    B, S, H, dh = q.shape
    topk = min(TOPK_MAX, S // 4)
    NB = S // Q_BLOCK
    key_pos = jnp.arange(S)
    iq = iq * (IDX_DH ** -0.5)
    iw = iw * (IDX_HEADS ** -0.5)

    def blockify(a):
        return a.reshape((B, NB, Q_BLOCK) + a.shape[2:]).swapaxes(0, 1)

    def one_block(args):
        qb, iqb, iwb, bi = args
        t = bi * Q_BLOCK + jnp.arange(Q_BLOCK)
        sc = jax.nn.relu(jnp.einsum('bthd,bsd->bths', iqb, ik))
        score = jnp.einsum('bths,bth->bts', sc, iwb).astype(jnp.float32)
        causal = key_pos[None, :] <= t[:, None]
        score = jnp.where(causal[None], score, -jnp.inf)
        _, idx = lax.top_k(score, topk)
        k_sel = jax.vmap(lambda kb, ib: kb[ib])(k, idx)
        v_sel = jax.vmap(lambda vb, ib: vb[ib])(v, idx)
        valid = idx <= t[None, :, None]
        bucket = t5_bucket(jnp.maximum(t[None, :, None] - idx, 0))
        bias = rel_bias[bucket].astype(jnp.float32).transpose(0, 1, 3, 2)
        logits = jnp.einsum('bthd,btkhd->bthk', qb, k_sel).astype(jnp.float32) * (dh ** -0.5) + bias
        logits = jnp.where(valid[:, :, None, :], logits, -jnp.inf)
        probs = jax.nn.softmax(logits, axis=-1).astype(v.dtype)
        return jnp.einsum('bthk,btkhd->bthd', probs, v_sel)

    out = lax.map(one_block, (blockify(q), blockify(iq), blockify(iw), jnp.arange(NB)))
    return out.swapaxes(0, 1).reshape(B, S, H, dh)

def first_inputs(seed: int = 0) -> dict:
    key = jax.random.key(seed)
    ks = jax.random.split(key, 16)
    f32 = jnp.float32
    x = jax.random.normal(ks[0], (BATCH, SEQ, D_MODEL), f32)
    p = jax.random.normal(ks[1], (DEPTH, BATCH, SEQ, D_PLE), f32)
    w_in = jax.random.normal(ks[2], (DEPTH, D_MODEL, PROJ_TOTAL), f32) * D_MODEL ** -0.5
    i_bias = 0.1 * jax.random.normal(ks[3], (DEPTH, M_HEADS), f32)
    f_bias = jnp.linspace(3.0, 6.0, M_HEADS, dtype=f32)[None] + 0.1 * jax.random.normal(ks[4], (DEPTH, M_HEADS), f32)
    b_gate = jnp.concatenate([i_bias, f_bias], axis=-1)
    conv_w = jax.random.normal(ks[5], (DEPTH, CONV_W, 2 * M_HEADS * M_QK), f32) * CONV_W ** -0.5
    w_out = jax.random.normal(ks[6], (DEPTH, D_MIX, D_MODEL), f32) * D_MIX ** -0.5
    norm_in = 1.0 + 0.1 * jax.random.normal(ks[7], (DEPTH, D_MODEL), f32)
    m_norm = 1.0 + 0.1 * jax.random.normal(ks[8], (DEPTH, M_WIDTH), f32)
    rel_bias = 0.5 * jax.random.normal(ks[9], (REL_BUCKETS, A_HEADS), f32)
    w_ple = jax.random.normal(ks[10], (DEPTH, D_PLE, D_MODEL), f32) * D_PLE ** -0.5
    w_ple_gate = jax.random.normal(ks[11], (DEPTH, D_MODEL, D_MODEL), f32) * D_MODEL ** -0.5
    norm_final = 1.0 + 0.1 * jax.random.normal(ks[12], (D_MODEL,), f32)
    return {"x": x, "p": p, "w_in": w_in, "b_gate": b_gate, "conv_w": conv_w, "w_out": w_out,
            "norm_in": norm_in, "m_norm": m_norm, "rel_bias": rel_bias, "w_ple": w_ple,
            "w_ple_gate": w_ple_gate, "norm_final": norm_final}

def first_block(x, p, w_in, b_gate, conv_w, w_out, norm_in, m_norm, rel_bias, w_ple, w_ple_gate, norm_final):
    B, S, _ = x.shape
    h = x
    for i in range(DEPTH):
        u = rmsnorm(h, norm_in[i])
        proj = u @ w_in[i]
        (m_q, m_k, m_v, m_o, m_z, m_if, a_q, a_k, a_v, a_z,
         ix_q, ix_k, ix_w) = jnp.split(proj, SPLIT_POINTS, axis=-1)

        qk = jax.nn.silu(causal_dwconv(jnp.concatenate([m_q, m_k], axis=-1), conv_w[i]))
        mq, mk = jnp.split(qk, 2, axis=-1)
        gates = (m_if + b_gate[i]).astype(jnp.float32)
        log_i = gates[..., :M_HEADS]
        log_f = jax.nn.log_sigmoid(gates[..., M_HEADS:])
        hm = mlstm_chunkwise(mq.reshape(B, S, M_HEADS, M_QK), mk.reshape(B, S, M_HEADS, M_QK),
                             m_v.reshape(B, S, M_HEADS, M_V), log_i, log_f)
        hm = hm * lax.rsqrt(jnp.mean(hm * hm, axis=-1, keepdims=True) + EPS)
        hm = hm.reshape(B, S, M_WIDTH) * m_norm[i].astype(jnp.float32)
        hm = jax.nn.sigmoid(m_o) * hm.astype(x.dtype) * jax.nn.silu(m_z)

        ha = dsa_attention(a_q.reshape(B, S, A_HEADS, A_DH), a_k.reshape(B, S, A_HEADS, A_DH),
                           a_v.reshape(B, S, A_HEADS, A_DH), ix_q.reshape(B, S, IDX_HEADS, IDX_DH),
                           ix_k, ix_w, rel_bias)
        ha = ha.reshape(B, S, A_WIDTH) * jax.nn.silu(a_z)

        h = h + jnp.concatenate([hm, ha], axis=-1) @ w_out[i]

        h = h + (p[i] @ w_ple[i]) * jax.nn.sigmoid(h @ w_ple_gate[i])
    return rmsnorm(h, norm_final)


DEPTH_2 = 2

N_MIXERS = 4
GATHER_CHUNK = 16
MAX_POS_OFFSET = 4096

MLA_HEADS = 8
MLA_NOPE = 128
MLA_ROPE = 64
MLA_V = 128
MLA_Q_RANK = 256
MLA_KV_RANK = 256
ROPE_BASE = 10000.0

MOBA_HEADS = 8
MOBA_HD = 128
MOBA_BLOCK = 256
MOBA_TOPK = 3

NSA_HEADS = 8
NSA_GROUPS = 2
NSA_HD = 128
NSA_CMP_LEN = 32
NSA_CMP_STRIDE = 16
NSA_SEL_BLOCK = 64
NSA_SEL_TOPN = 16
NSA_WINDOW = 512
NSA_FORCE_BONUS = 100.0

SB_HEADS = 8
SB_HD = 128

D_FF = 2816
CONV_W_2 = 3
LN_EPS = 1e-5
RMS_EPS = 1e-6
NEG = -1e30
TINY = 1e-30
DEEPNORM_ALPHA = (2 * DEPTH_2) ** 0.25
DEEPNORM_BETA = (8 * DEPTH_2) ** -0.25


def _count(kind):
    return len(range(kind, DEPTH_2, N_MIXERS))

def layer_norm(x, g, b):
    xf = x.astype(jnp.float32)
    mu = jnp.mean(xf, -1, keepdims=True)
    var = jnp.mean(jnp.square(xf - mu), -1, keepdims=True)
    return ((xf - mu) * lax.rsqrt(var + LN_EPS) * g.astype(jnp.float32) + b.astype(jnp.float32)).astype(x.dtype)

def rms_norm(x, g):
    xf = x.astype(jnp.float32)
    return (xf * lax.rsqrt(jnp.mean(jnp.square(xf), -1, keepdims=True) + RMS_EPS) * g.astype(jnp.float32)).astype(x.dtype)

def apply_rope(x, cos, sin):
    half = x.shape[-1] // 2
    x1 = x[..., :half].astype(jnp.float32)
    x2 = x[..., half:].astype(jnp.float32)
    return jnp.concatenate([x1 * cos - x2 * sin, x2 * cos + x1 * sin], -1).astype(x.dtype)

def alibi_slopes(n):
    return 2.0 ** (-8.0 * jnp.arange(1, n + 1, dtype=jnp.float32) / n)

def masked_softmax(s, mask):
    s = jnp.where(mask, s, NEG)
    p = jnp.where(mask, jnp.exp(s - jnp.max(s, -1, keepdims=True)), 0.0)
    return p / jnp.maximum(jnp.sum(p, -1, keepdims=True), TINY)

def split_heads3(proj, n_heads, hd):
    B, S, _ = proj.shape
    t = proj.reshape(B, S, 3, n_heads, hd).transpose(2, 0, 3, 1, 4)
    return t[0], t[1], t[2]

def merge_heads(o):
    B, H, S, D = o.shape
    return o.transpose(0, 2, 1, 3).reshape(B, S, H * D)

def causal_softmax_attention(q, k, v, scale):
    B, H, S, Dk = q.shape
    nqb = S // Q_BLOCK
    q_blocks = q.reshape(B, H, nqb, Q_BLOCK, Dk).transpose(2, 0, 1, 3, 4)
    k_idx = jnp.arange(S)

    def block(args):
        q_b, bi = args
        s = jnp.einsum('bhqd,bhkd->bhqk', q_b, k, preferred_element_type=jnp.float32) * scale
        q_idx = bi * Q_BLOCK + jnp.arange(Q_BLOCK)
        p = masked_softmax(s, k_idx[None, :] <= q_idx[:, None])
        return jnp.einsum('bhqk,bhkd->bhqd', p.astype(v.dtype), v)

    o = lax.map(block, (q_blocks, jnp.arange(nqb)))
    return o.transpose(1, 2, 0, 3, 4).reshape(B, H, S, v.shape[-1])

def mla_mixer(h, cos, sin, w_in, q_norm, w_uq, kv_norm, w_ukv, w_o):
    B, S, _ = h.shape
    H, DN, DR, DV = MLA_HEADS, MLA_NOPE, MLA_ROPE, MLA_V
    proj = h @ w_in
    c_q = rms_norm(proj[..., :MLA_Q_RANK], q_norm)
    c_kv = rms_norm(proj[..., MLA_Q_RANK:MLA_Q_RANK + MLA_KV_RANK], kv_norm)
    k_rope = apply_rope(proj[..., MLA_Q_RANK + MLA_KV_RANK:], cos, sin)
    q = (c_q @ w_uq).reshape(B, S, H, DN + DR).transpose(0, 2, 1, 3)
    q = jnp.concatenate([q[..., :DN], apply_rope(q[..., DN:], cos[:, None], sin[:, None])], -1)
    kv = (c_kv @ w_ukv).reshape(B, S, H, DN + DV).transpose(0, 2, 1, 3)
    k = jnp.concatenate([kv[..., :DN], jnp.broadcast_to(k_rope[:, None], (B, H, S, DR))], -1)
    v = kv[..., DN:]
    o = causal_softmax_attention(q, k, v, (DN + DR) ** -0.5)
    return merge_heads(o) @ w_o

def moba_mixer(h, positions, w_in, w_o):
    B, S, _ = h.shape
    H, D, BLK, C = MOBA_HEADS, MOBA_HD, MOBA_BLOCK, GATHER_CHUNK
    q, k, v = split_heads3(h @ w_in, H, D)
    nb = -(-S // BLK)
    pad = nb * BLK - S
    posf = positions.astype(jnp.float32)
    k_p = jnp.pad(k, ((0, 0), (0, 0), (0, pad), (0, 0)))
    v_p = jnp.pad(v, ((0, 0), (0, 0), (0, pad), (0, 0)))
    pos_p = jnp.pad(posf, ((0, 0), (0, pad)))
    k_blk = k_p.reshape(B, H, nb, BLK, D)
    v_blk = v_p.reshape(B, H, nb, BLK, D)
    pos_blk = pos_p.reshape(B, nb, BLK)
    k_mean = jnp.mean(k_blk.astype(jnp.float32), axis=3)
    slope = alibi_slopes(H)[None, :, None, None]
    kk = min(MOBA_TOPK, nb)
    nch = S // C
    scale = D ** -0.5
    b_ix = jnp.arange(B)[:, None, None, None]
    h_ix = jnp.arange(H)[None, :, None, None]
    blk_off = jnp.arange(BLK)
    sel_rank = jnp.arange(kk)

    def chunk(args):
        q_c, pq, ci = args
        start = ci * C
        q_idx = start + jnp.arange(C)
        own = start // BLK
        gate = jnp.einsum('bhqd,bhnd->bhqn', q_c.astype(jnp.float32), k_mean)
        gate = jnp.where(jnp.arange(nb) < own, gate, NEG)
        _, sel = lax.top_k(gate, kk)
        sel_valid = sel_rank < own
        k_sel = k_blk[b_ix, h_ix, sel]
        v_sel = v_blk[b_ix, h_ix, sel]
        kpos_sel = pos_blk[b_ix, sel]
        s_sel = jnp.einsum('bhqd,bhqnkd->bhqnk', q_c, k_sel, preferred_element_type=jnp.float32) * scale
        s_sel = s_sel - slope[..., None] * jnp.abs(pq[:, None, :, None, None] - kpos_sel)
        k_own = lax.dynamic_slice_in_dim(k_p, own * BLK, BLK, axis=2)
        v_own = lax.dynamic_slice_in_dim(v_p, own * BLK, BLK, axis=2)
        kpos_own = lax.dynamic_slice_in_dim(pos_p, own * BLK, BLK, axis=1)
        s_own = jnp.einsum('bhqd,bhkd->bhqk', q_c, k_own, preferred_element_type=jnp.float32) * scale
        s_own = s_own - slope * jnp.abs(pq[:, None, :, None] - kpos_own[:, None, None, :])
        mask_own = (own * BLK + blk_off)[None, :] <= q_idx[:, None]
        mask_sel = jnp.broadcast_to(jnp.repeat(sel_valid, BLK)[None, :], (C, kk * BLK))
        s = jnp.concatenate([s_sel.reshape(B, H, C, kk * BLK), s_own], -1)
        p = masked_softmax(s, jnp.concatenate([mask_sel, mask_own], -1))
        p_sel = p[..., :kk * BLK].reshape(B, H, C, kk, BLK).astype(v.dtype)
        p_own = p[..., kk * BLK:].astype(v.dtype)
        return (jnp.einsum('bhqnk,bhqnkd->bhqd', p_sel, v_sel)
                + jnp.einsum('bhqk,bhkd->bhqd', p_own, v_own))

    q_chunks = q.reshape(B, H, nch, C, D).transpose(2, 0, 1, 3, 4)
    pq_chunks = posf.reshape(B, nch, C).transpose(1, 0, 2)
    o = lax.map(chunk, (q_chunks, pq_chunks, jnp.arange(nch)))
    o = o.transpose(1, 2, 0, 3, 4).reshape(B, H, S, D)
    return merge_heads(o) @ w_o

def nsa_mixer(h, positions, w_in, cmp_pos, cmp_w1, cmp_w2, w_o):
    B, S, _ = h.shape
    H, G, D = NSA_HEADS, NSA_GROUPS, NSA_HD
    R = H // G
    L, ST, SB, W = NSA_CMP_LEN, NSA_CMP_STRIDE, NSA_SEL_BLOCK, NSA_WINDOW
    proj = h @ w_in
    q = proj[..., :H * D].reshape(B, S, G, R, D).transpose(0, 2, 3, 1, 4)
    kv = proj[..., H * D:H * D + 6 * G * D].reshape(B, S, 6, G, D).transpose(2, 0, 3, 1, 4)
    k_cmp_raw, v_cmp_raw, k_slc, v_slc, k_win, v_win = kv[0], kv[1], kv[2], kv[3], kv[4], kv[5]
    gates = jax.nn.sigmoid(proj[..., H * D + 6 * G * D:].astype(jnp.float32))
    gates = gates.reshape(B, S, 3, G, R).transpose(2, 0, 3, 4, 1)[..., None]
    posf = positions.astype(jnp.float32)
    slope = alibi_slopes(H).reshape(G, R)[None, :, :, None, None]
    scale = D ** -0.5
    q_idx_all = jnp.arange(S)

    nc = (S - L) // ST + 1
    c_start = jnp.arange(nc) * ST
    c_idx = c_start[:, None] + jnp.arange(L)[None, :]
    c_end = c_start + L - 1

    def compress(t, pe, w1, w2):
        blocks = t[:, :, c_idx] + pe
        return jax.nn.gelu(blocks.reshape(B, G, nc, L * D) @ w1) @ w2

    k_c = compress(k_cmp_raw, cmp_pos[0], cmp_w1[0], cmp_w2[0])
    v_c = compress(v_cmp_raw, cmp_pos[1], cmp_w1[1], cmp_w2[1])
    s_c = jnp.einsum('bgrqd,bgnd->bgrqn', q, k_c, preferred_element_type=jnp.float32) * scale
    s_c = s_c - slope * jnp.abs(posf[:, None, None, :, None] - posf[:, c_end][:, None, None, None, :])
    p_c = masked_softmax(s_c, c_end[None, :] <= q_idx_all[:, None])
    o_cmp = jnp.einsum('bgrqn,bgnd->bgrqd', p_c.astype(v_c.dtype), v_c)

    ns = S // SB
    j_start = jnp.arange(ns) * SB
    overlap = ((c_start[:, None] < j_start[None, :] + SB) & (c_end[:, None] >= j_start[None, :])).astype(jnp.float32)
    imp = jnp.einsum('bgrqn,nj->bgqj', p_c, overlap)
    q_blk = q_idx_all // SB
    jj = jnp.arange(ns)
    forced = ((jj[None, :] == 0) | (jj[None, :] == q_blk[:, None]) | (jj[None, :] == q_blk[:, None] - 1)).astype(jnp.float32)
    imp = jnp.where(jj[None, :] <= q_blk[:, None], imp + NSA_FORCE_BONUS * forced, NEG)
    topn = min(NSA_SEL_TOPN, ns)
    _, sel = lax.top_k(imp, topn)
    sel_valid = jnp.arange(topn)[None, :] <= q_blk[:, None]

    k_sb = k_slc.reshape(B, G, ns, SB, D)
    v_sb = v_slc.reshape(B, G, ns, SB, D)
    pos_sb = posf.reshape(B, ns, SB)
    C = GATHER_CHUNK
    nch = S // C
    b_ix = jnp.arange(B)[:, None, None, None]
    g_ix = jnp.arange(G)[None, :, None, None]
    sb_off = jnp.arange(SB)

    def sel_chunk(args):
        q_c, pq, sel_c, valid_c, ci = args
        q_i = ci * C + jnp.arange(C)
        k_g = k_sb[b_ix, g_ix, sel_c]
        v_g = v_sb[b_ix, g_ix, sel_c]
        kpos = pos_sb[b_ix, sel_c]
        k_i = sel_c[..., None] * SB + sb_off
        s = jnp.einsum('bgrqd,bgqnkd->bgrqnk', q_c, k_g, preferred_element_type=jnp.float32) * scale
        s = s - slope[..., None] * jnp.abs(pq[:, None, None, :, None, None] - kpos[:, :, None])
        mask = valid_c[None, None, :, :, None] & (k_i <= q_i[None, None, :, None, None])
        p = masked_softmax(s.reshape(B, G, R, C, topn * SB), mask.reshape(B, G, 1, C, topn * SB))
        return jnp.einsum('bgrqnk,bgqnkd->bgrqd', p.reshape(B, G, R, C, topn, SB).astype(v_g.dtype), v_g)

    o_sel = lax.map(sel_chunk, (
        q.reshape(B, G, R, nch, C, D).transpose(3, 0, 1, 2, 4, 5),
        posf.reshape(B, nch, C).transpose(1, 0, 2),
        sel.reshape(B, G, nch, C, topn).transpose(2, 0, 1, 3, 4),
        sel_valid.reshape(nch, C, topn),
        jnp.arange(nch)))
    o_sel = o_sel.transpose(1, 2, 3, 0, 4, 5).reshape(B, G, R, S, D)

    QB = Q_BLOCK
    nqb = S // QB
    span = W + QB
    band = jnp.arange(nqb)[:, None] * QB + jnp.arange(span)[None, :]
    k_w = jnp.pad(k_win, ((0, 0), (0, 0), (W, 0), (0, 0)))[:, :, band]
    v_w = jnp.pad(v_win, ((0, 0), (0, 0), (W, 0), (0, 0)))[:, :, band]
    kpos_w = jnp.pad(posf, ((0, 0), (W, 0)))[:, band]
    k_i = (band - W)[:, None, :]
    q_i = (jnp.arange(nqb)[:, None] * QB + jnp.arange(QB)[None, :])[:, :, None]
    mask_w = (k_i >= 0) & (k_i <= q_i) & (q_i - k_i < W)
    q_w = q.reshape(B, G, R, nqb, QB, D)
    s_w = jnp.einsum('bgriqd,bgikd->bgriqk', q_w, k_w, preferred_element_type=jnp.float32) * scale
    s_w = s_w - slope[..., None] * jnp.abs(posf.reshape(B, nqb, QB)[:, None, None, :, :, None] - kpos_w[:, None, None, :, None, :])
    p_w = masked_softmax(s_w, mask_w)
    o_win = jnp.einsum('bgriqk,bgikd->bgriqd', p_w.astype(v_w.dtype), v_w).reshape(B, G, R, S, D)

    o = gates[0] * o_cmp + gates[1] * o_sel + gates[2] * o_win
    o = o.transpose(0, 3, 1, 2, 4).reshape(B, S, H * D).astype(h.dtype)
    return o @ w_o

def stick_breaking_mixer(h, w_in, w_o):
    B, S, _ = h.shape
    H, D = SB_HEADS, SB_HD
    q, k, v = split_heads3(h @ w_in, H, D)
    scale = D ** -0.5
    nqb = S // Q_BLOCK
    k_idx = jnp.arange(S)

    def block(args):
        q_b, bi = args
        z = jnp.einsum('bhqd,bhkd->bhqk', q_b, k, preferred_element_type=jnp.float32) * scale
        q_idx = bi * Q_BLOCK + jnp.arange(Q_BLOCK)
        mask = k_idx[None, :] < q_idx[:, None]
        log_beta = jax.nn.log_sigmoid(z)
        log_1mb = jnp.where(mask, jax.nn.log_sigmoid(-z), 0.0)
        tail = lax.cumsum(log_1mb, axis=3, reverse=True) - log_1mb
        a = jnp.where(mask, jnp.exp(log_beta + tail), 0.0)
        return jnp.einsum('bhqk,bhkd->bhqd', a.astype(v.dtype), v)

    q_blocks = q.reshape(B, H, nqb, Q_BLOCK, D).transpose(2, 0, 1, 3, 4)
    o = lax.map(block, (q_blocks, jnp.arange(nqb)))
    o = o.transpose(1, 2, 0, 3, 4).reshape(B, H, S, D)
    return merge_heads(o) @ w_o

def conv_ffn(h, w_in, conv_w, conv_b, w_out):
    u = h @ w_in
    a, b = u[..., :D_FF], u[..., D_FF:]
    a = lax.conv_general_dilated(a, conv_w[:, None, :].astype(a.dtype), window_strides=(1,),
                                 padding=[(CONV_W_2 - 1, 0)], dimension_numbers=('NWC', 'WIO', 'NWC'),
                                 feature_group_count=D_FF) + conv_b
    return (jax.nn.gelu(a) * b) @ w_out

def _w(key, shape, fan_in, scale=1.0):
    return jax.random.normal(key, shape, jnp.float32) * (scale * fan_in ** -0.5)

def _gain(key, shape):
    return 1.0 + 0.02 * jax.random.normal(key, shape, jnp.float32)

def _small(key, shape):
    return 0.02 * jax.random.normal(key, shape, jnp.float32)

def second_inputs(seed: int = 0) -> dict:
    key = jax.random.key(seed)
    ks = jax.random.split(key, 32)
    D = D_MODEL
    nA, nB, nC, nD = _count(0), _count(1), _count(2), _count(3)
    mla_out = MLA_Q_RANK + MLA_KV_RANK + MLA_ROPE
    nsa_out = NSA_HEADS * NSA_HD + 6 * NSA_GROUPS * NSA_HD + 3 * NSA_HEADS
    mod_base = jnp.repeat(jnp.array([0.0, 0.0, 1.0, 0.0, 0.0, 1.0], jnp.float32), D)
    offset = jax.random.randint(ks[2], (BATCH, 1), 0, MAX_POS_OFFSET, dtype=jnp.int32)
    return {
        'x': jax.random.normal(ks[0], (BATCH, SEQ, D), jnp.float32),
        'c': jax.random.normal(ks[1], (BATCH, D), jnp.float32),
        'positions': offset + jnp.arange(SEQ, dtype=jnp.int32)[None, :],
        'mod_w': _w(ks[3], (DEPTH_2, D, 6 * D), D, 0.1),
        'mod_b': mod_base + _small(ks[4], (DEPTH_2, 6 * D)),
        'ln_g': _gain(ks[5], (DEPTH_2, 2, D)),
        'ln_b': _small(ks[6], (DEPTH_2, 2, D)),
        'ffn_w_in': _w(ks[7], (DEPTH_2, D, 2 * D_FF), D),
        'ffn_conv_w': _w(ks[8], (DEPTH_2, CONV_W_2, D_FF), CONV_W_2),
        'ffn_conv_b': _small(ks[9], (DEPTH_2, D_FF)),
        'ffn_w_out': _w(ks[10], (DEPTH_2, D_FF, D), D_FF, DEEPNORM_BETA),
        'mla_w_in': _w(ks[11], (nA, D, mla_out), D),
        'mla_q_norm': _gain(ks[12], (nA, MLA_Q_RANK)),
        'mla_w_uq': _w(ks[13], (nA, MLA_Q_RANK, MLA_HEADS * (MLA_NOPE + MLA_ROPE)), MLA_Q_RANK),
        'mla_kv_norm': _gain(ks[14], (nA, MLA_KV_RANK)),
        'mla_w_ukv': _w(ks[15], (nA, MLA_KV_RANK, MLA_HEADS * (MLA_NOPE + MLA_V)), MLA_KV_RANK),
        'mla_w_o': _w(ks[16], (nA, MLA_HEADS * MLA_V, D), MLA_HEADS * MLA_V, DEEPNORM_BETA),
        'moba_w_in': _w(ks[17], (nB, D, 3 * MOBA_HEADS * MOBA_HD), D),
        'moba_w_o': _w(ks[18], (nB, MOBA_HEADS * MOBA_HD, D), MOBA_HEADS * MOBA_HD, DEEPNORM_BETA),
        'nsa_w_in': _w(ks[19], (nC, D, nsa_out), D),
        'nsa_cmp_pos': _small(ks[20], (nC, 2, NSA_CMP_LEN, NSA_HD)),
        'nsa_cmp_w1': _w(ks[21], (nC, 2, NSA_CMP_LEN * NSA_HD, NSA_HD), NSA_CMP_LEN * NSA_HD),
        'nsa_cmp_w2': _w(ks[22], (nC, 2, NSA_HD, NSA_HD), NSA_HD),
        'nsa_w_o': _w(ks[23], (nC, NSA_HEADS * NSA_HD, D), NSA_HEADS * NSA_HD, DEEPNORM_BETA),
        'sb_w_in': _w(ks[24], (nD, D, 3 * SB_HEADS * SB_HD), D),
        'sb_w_o': _w(ks[25], (nD, SB_HEADS * SB_HD, D), SB_HEADS * SB_HD, DEEPNORM_BETA),
    }

def second_block(x, c, positions, mod_w, mod_b, ln_g, ln_b, ffn_w_in, ffn_conv_w, ffn_conv_b, ffn_w_out,
              mla_w_in, mla_q_norm, mla_w_uq, mla_kv_norm, mla_w_ukv, mla_w_o,
              moba_w_in, moba_w_o, nsa_w_in, nsa_cmp_pos, nsa_cmp_w1, nsa_cmp_w2, nsa_w_o,
              sb_w_in, sb_w_o):
    B, S, D = x.shape
    half = MLA_ROPE // 2
    inv_freq = ROPE_BASE ** (-jnp.arange(half, dtype=jnp.float32) / half)
    ang = positions.astype(jnp.float32)[..., None] * inv_freq
    cos, sin = jnp.cos(ang), jnp.sin(ang)
    c_act = jax.nn.silu(c)
    for i in range(DEPTH_2):
        kind, j = i % N_MIXERS, i // N_MIXERS
        mod = (c_act @ mod_w[i] + mod_b[i]).reshape(B, 6, D)[:, :, None, :]
        hin = x * (1.0 + mod[:, 1]) + mod[:, 0]
        if kind == 0:
            y = mla_mixer(hin, cos, sin, mla_w_in[j], mla_q_norm[j], mla_w_uq[j], mla_kv_norm[j], mla_w_ukv[j], mla_w_o[j])
        elif kind == 1:
            y = moba_mixer(hin, positions, moba_w_in[j], moba_w_o[j])
        elif kind == 2:
            y = nsa_mixer(hin, positions, nsa_w_in[j], nsa_cmp_pos[j], nsa_cmp_w1[j], nsa_cmp_w2[j], nsa_w_o[j])
        else:
            y = stick_breaking_mixer(hin, sb_w_in[j], sb_w_o[j])
        x = layer_norm(DEEPNORM_ALPHA * x + mod[:, 2] * y, ln_g[i, 0], ln_b[i, 0])
        hin = x * (1.0 + mod[:, 4]) + mod[:, 3]
        y = conv_ffn(hin, ffn_w_in[i], ffn_conv_w[i], ffn_conv_b[i], ffn_w_out[i])
        x = layer_norm(DEEPNORM_ALPHA * x + mod[:, 5] * y, ln_g[i, 1], ln_b[i, 1])
    return x


def setup_inputs(seed=0):
    out = dict(first_inputs(seed))
    for name, value in second_inputs(seed + 1).items():
        if name != "x":
            out[name + "_2"] = value
    return out


def reference(
    x, p, w_in, b_gate, conv_w, w_out, norm_in, m_norm, rel_bias, w_ple, w_ple_gate, norm_final,
    c_2, positions_2, mod_w_2, mod_b_2, ln_g_2, ln_b_2, ffn_w_in_2, ffn_conv_w_2, ffn_conv_b_2,
    ffn_w_out_2, mla_w_in_2, mla_q_norm_2, mla_w_uq_2, mla_kv_norm_2, mla_w_ukv_2, mla_w_o_2,
    moba_w_in_2, moba_w_o_2, nsa_w_in_2, nsa_cmp_pos_2, nsa_cmp_w1_2, nsa_cmp_w2_2, nsa_w_o_2,
    sb_w_in_2, sb_w_o_2,
):
    x = first_block(
        x, p, w_in, b_gate, conv_w, w_out, norm_in, m_norm, rel_bias, w_ple, w_ple_gate,
        norm_final,
    )
    return second_block(
        x, c_2, positions_2, mod_w_2, mod_b_2, ln_g_2, ln_b_2, ffn_w_in_2, ffn_conv_w_2,
        ffn_conv_b_2, ffn_w_out_2, mla_w_in_2, mla_q_norm_2, mla_w_uq_2, mla_kv_norm_2,
        mla_w_ukv_2, mla_w_o_2, moba_w_in_2, moba_w_o_2, nsa_w_in_2, nsa_cmp_pos_2,
        nsa_cmp_w1_2, nsa_cmp_w2_2, nsa_w_o_2, sb_w_in_2, sb_w_o_2,
    )


_drawn_inputs = setup_inputs


def setup_inputs(seed=0):
    import zlib

    import numpy as np

    out = dict(_drawn_inputs(seed))
    spreads = {}
    factors = {'ffn_conv_b_2': 8.0, 'mla_q_norm_2': 8.0, 'mla_kv_norm_2': 8.0}
    for name, (base, spread) in spreads.items():
        noise = np.random.default_rng([zlib.crc32(name.encode()), seed]).standard_normal(out[name].shape)
        drawn = base * np.exp(spread * noise) if base else spread * noise
        out[name] = __import__('jax').numpy.asarray(drawn.astype(out[name].dtype))
    for name, factor in factors.items():
        out[name] = (out[name] * factor).astype(out[name].dtype)
    return out
```

```python
import numpy as np
import concourse.bass as bass
from concourse import mybir
from contextlib import ExitStack

BIG = 1e30
COLS = [("norm_in", 8), ("conv_w", 32), ("fconv_w", 132), ("fconv_b", 44), ("q_norm", 2), ("kv_norm", 2),
        ("mod_b", 96), ("c", 8), ("b_gate", 2), ("inv_freq", 1), ("sign", 1)]
CONSTS = [("ident", 128), ("ones", 256), ("sel", 512), ("onehot", 384), ("cm", 256), ("cmT", 256)]


def spans(table):
    out, at = {}, 0
    for name, n in table:
        out[name] = (at, at + n)
        at += n
    return out, at


COL_AT, NCOL = spans(COLS)
CONST_AT, NCONST = spans(CONSTS)


class Queue:

    def __init__(self, sem):
        self.sem, self.count, self.items, self.seen = sem, 0, [], {}

    def wait(self, tokens):
        for t in tokens:
            if t is None:
                continue
            if isinstance(t, list):
                self.wait(t)
                continue
            sem, value = t
            if self.seen.get(sem.name, 0) < value:
                self.seen[sem.name] = value
                self.items.append((None, (sem, value), None, None, 0))

    def op(self, tokens, fn, *args, **kw):
        self.wait(tokens)
        self.count += 1
        self.items.append((fn, args, kw, self.sem, 1))
        return self.sem, self.count

    def quiet(self, tokens, fn, *args, **kw):
        self.wait(tokens)
        self.items.append((fn, args, kw, None, 0))

    def dma(self, tokens, sem, value, fn, *args, **kw):
        self.wait(tokens)
        self.items.append((fn, args, kw, sem, 16))
        return sem, value

    def emit(self, eng):
        for fn, args, kw, sem, by in self.items:
            if fn is None:
                eng.wait_ge(*args)
            elif sem is None:
                fn(*args, **kw)
            else:
                fn(*args, **kw).then_inc(sem, by)


class Spot:

    def __init__(self, ap):
        self.ap, self.free = ap, []


class Turn:

    def __init__(self, aps):
        self.spots, self.n = [Spot(a) for a in aps], 0

    def get(self):
        s = self.spots[self.n % len(self.spots)]
        self.n += 1
        return s


def build(nc, D, out):
    f32, i32 = mybir.dt.float32, mybir.dt.int32
    ALU, ACT, AX = mybir.AluOpType, mybir.ActivationFunctionType, mybir.AxisListType
    MUL, ADD, SUB, MAX, MIN = ALU.mult, ALU.add, ALU.subtract, ALU.max, ALU.min
    ctx = ExitStack()
    with ctx:
        def sb(name, cols, dt=f32):
            return ctx.enter_context(nc.sbuf_tensor(name, [128, cols], dt))

        def sem(name):
            return ctx.enter_context(nc.semaphore(name))

        P, V, A, G, S = (Queue(sem(n)) for n in ("s_pe", "s_dve", "s_act", "s_pool", "s_sp"))
        ve, ac, po, pe = nc.vector, nc.scalar, nc.gpsimd, nc.tensor

        NR = 8
        ring_t = sb("ring", NR * 2048)
        ring = Turn([ring_t[:, i * 2048:(i + 1) * 2048] for i in range(NR)])
        ring_sem = [sem(f"s_w{i}") for i in range(NR)]

        def load(src, cols=2048):
            i, turn = ring.n % NR, ring.n // NR
            s = ring.get()
            assert s.free is not None
            tok = S.dma(s.free, ring_sem[i], 16 * (turn + 1), nc.sync.dma_start, s.ap[:, 0:cols], src[:, 0:cols])
            s.free = None
            return s, tok

        def rows(names):
            i, turn = ring.n % NR, ring.n // NR
            s = ring.get()
            assert s.free is not None
            src = D[names[0]].tensor
            off, n = names[1], names[2]
            tok = S.dma(s.free, ring_sem[i], 16 * (turn + 1), nc.sync.dma_start, s.ap[:, 0:n],
                        bass.AP(src, off, [[0, 128], [1, n]]))
            s.free = None
            return s, tok

        psum = Turn([ctx.enter_context(nc.psum_tensor(f"ps{i}", [128, 512], f32))[:, :] for i in range(8)])

        cst = sb("cst", NCONST)
        cols = sb("cols", NCOL)
        X = sb("X", 2048)[:, :].rearrange("p (t n) -> p t n", t=2)
        Y = sb("Y", 2048)[:, :].rearrange("p (t n) -> p t n", t=2)
        XT = sb("XT", 2048)[:, :].rearrange("p (k n) -> p k n", k=8)
        R2 = sb("R2", 2048)[:, :].rearrange("p (m n) -> p m n", m=2)
        MC = sb("MC", 64)
        MC2 = [MC[:, 0:32], MC[:, 32:64]]
        acc = sb("acc", 2048)
        small = sb("small", 512)
        arena = sb("arena", 19456)
        wk = Turn([sb(f"wk{i}", 512)[:, :] for i in range(4)])
        pt = Turn([sb(f"pt{i}", 256)[:, :] for i in range(4)])
        posi = sb("posi", 258, i32)
        gscr = nc.dram_tensor("gscr", [8, 128, 383], f32, kind="Internal").ap()

        def C(name, a=0, b=None):
            lo, hi = CONST_AT[name]
            return cst[:, lo + a:(hi if b is None else lo + b)]

        def K(name, i=0, n=1):
            lo = COL_AT[name][0]
            return cols[:, lo + i:lo + i + n]

        at = [0]

        def take(n):
            at[0] += n
            assert at[0] <= 19456, at[0]
            return arena[:, at[0] - n:at[0]]

        sm_at = [0]

        def tiny(n):
            sm_at[0] += n
            assert sm_at[0] <= 512
            return small[:, sm_at[0] - n:sm_at[0]]

        s_in = [sem(f"s_in{i}") for i in range(5)]
        s_rb = sem("s_rb")
        t_cst = S.dma([], s_in[0], 16, nc.sync.dma_start, cst[:, :], D["consts"])
        t_cols = S.dma([], s_in[1], 16, nc.sync.dma_start, cols[:, :], D["cols"])
        t_x = S.dma([], s_in[2], 16, nc.sync.dma_start, X, D["x"].rearrange("(t p) n -> p t n", t=2))
        relb = tiny(8)
        pT = take(512).rearrange("p (k n) -> p k n", k=2)
        S.dma([], s_in[3], 16, nc.sync.dma_start, relb[0:32, :], D["rel_bias"])
        S.dma([], s_in[3], 32, nc.sync.dma_start, posi[:, 0:256],
              bass.AP(D["pos_r"].tensor, 0, [[0, 128], [1, 256]]))
        S.dma([], s_in[3], 48, nc.sync.dma_start, posi[:, 256:258], D["pos_c"])
        t_misc = S.dma([], s_in[3], 64, nc.sync.dma_start, pT, D["pT"].rearrange("(k p) n -> p k n", k=2))
        ID = C("ident")

        def mm(tokens, o, l, r, start, stop, mark=False):
            if mark:
                return P.op(tokens, pe.matmul, o, l, r, start=start, stop=stop)
            P.quiet(tokens, pe.matmul, o, l, r, start=start, stop=stop)

        def proj_b(xT, deps, nk, src, blocks, evac):
            per = 2048 // (128 * nk)
            for u in range((blocks + per - 1) // per):
                nb = min(per, blocks - u * per)
                w, tw = load(src[u], nb * nk * 128)
                for j in range(0, nb, 2):
                    b = psum.get()
                    m = min(2, nb - j)
                    for i in range(m):
                        for k in range(nk):
                            c = ((j + i) * nk + k) * 128
                            last = mm([tw, deps[k], b.free], b.ap[:, i * 256:(i + 1) * 256], w.ap[:, c:c + 128],
                                      xT[:, k, :], k == 0, k == nk - 1, k == nk - 1 and i == m - 1)
                    b.free = evac(u * per + j, m, b, last)
                w.free = [last]

        def proj_a(xT, deps, nk, src, blocks, evac):
            nq = (nk + 3) // 4
            for cb in range(blocks):
                bs = [psum.get(), psum.get()]
                for q in range(nq):
                    kk = min(4, nk - 4 * q)
                    w, tw = load(src[cb * nq + q], kk * 512)
                    ends = []
                    for t in range(2):
                        for k in range(kk):
                            kg = 4 * q + k
                            last = mm([tw, deps[kg], bs[t].free], bs[t].ap, xT[:, kg, t * 128:(t + 1) * 128],
                                      w.ap[:, k * 512:(k + 1) * 512], kg == 0, kg == nk - 1, k == kk - 1)
                        ends.append(last)
                    w.free = [last]
                for t in range(2):
                    bs[t].free = evac(t, cb, bs[t], ends[t])

        def proj_a2(xT, deps, src, evac):
            w, tw = load(src[0])
            for cb in range(2):
                for t in range(2):
                    b = psum.get()
                    for k in range(2):
                        last = mm([tw, deps[k], b.free], b.ap, xT[:, k, t * 128:(t + 1) * 128],
                                  w.ap[:, (cb * 2 + k) * 512:(cb * 2 + k + 1) * 512], k == 0, k == 1, k == 1)
                    b.free = evac(t, cb, b, last)
            w.free = [last]

        def transposed(src, deps, dst, nk, evac):
            out_t = [None] * nk
            for k in range(0, nk, 2):
                b = psum.get()
                for i in range(2):
                    for t in range(2):
                        o = b.ap[:, i * 256 + t * 128:i * 256 + (t + 1) * 128]
                        if i == 1 and t == 1:
                            last = P.op([deps[t], b.free, t_cst], pe.transpose, o, src(t, k + i), ID)
                        else:
                            P.quiet([deps[t], b.free, t_cst], pe.transpose, o, src(t, k + i), ID)
                b.free = []
                for i in range(2):
                    out_t[k + i] = evac(k + i, b.ap[:, i * 256:(i + 1) * 256], dst[:, k + i, :], last)
                    b.free.append(out_t[k + i])
            return out_t

        def rsqrt(src, o, scale, eps, tokens):
            t = V.op(tokens, ve.tensor_scalar, o, src, scale, eps, MUL, ADD)
            t = A.op([t], ac.activation, o, o, ACT.Sqrt)
            return V.op([t], ve.reciprocal, o, o)

        turn = [0]

        def copy(o, i, tokens):
            turn[0] += 1
            if turn[0] % 2:
                return V.op(tokens, ve.tensor_copy, o, i)
            return A.op(tokens, ac.copy, o, i)

        ones = C("ones")

        cact = tiny(8)
        ct = A.op([t_cols], ac.activation, cact, K("c", 0, 8), ACT.Sigmoid)
        ct = V.op([ct], ve.tensor_tensor, cact, cact, K("c", 0, 8), MUL)
        t_mod = {}
        acc_free = [[]]
        r2_free = [[]]
        mc_free = [[], []]

        def modulation(i):
            toks = []
            tb_free = []
            for c in range(3):
                prev = ct
                for k in range(8):
                    w, tw = load(D["mod_w"][(i * 3 + c) * 8 + k])
                    for q in range(2):
                        a_, w_ = acc[:, q * 1024:(q + 1) * 1024], w.ap[:, q * 1024:(q + 1) * 1024]
                        if k == 0:
                            t = V.op([tw, ct, acc_free[0]], ve.tensor_scalar, a_, w_, cact[:, k:k + 1], None, MUL)
                            if q == 0:
                                t0 = t
                        else:
                            t = V.op([tw, prev[q]], ve.scalar_tensor_tensor, a_, w_, cact[:, k:k + 1],
                                     a_, MUL, ADD)
                        if q == 0:
                            ta = t
                    prev = [ta, t]
                    w.free = [t]
                    yield
                done = []
                for half in range(2):
                    m = 2 * c + half
                    a_ = acc[:, half * 1024:(half + 1) * 1024]
                    if m in (2, 5):
                        r = 0 if m == 2 else 1
                        if half == 0 or c == 2:
                            br, tb = rows(("mod_b", i * 6144 + m * 1024, 1024))
                        for cb in range(2):
                            b = psum.get()
                            last = mm([prev, b.free, t_cst], b.ap, ones[:, 0:128],
                                      a_[:, cb * 512:(cb + 1) * 512], True, True, True)
                            t = V.op([last, tb, r2_free[0]], ve.tensor_tensor, R2[:, r, cb * 512:(cb + 1) * 512],
                                     b.ap, br.ap[:, cb * 512:(cb + 1) * 512], ADD)
                            b.free = [t]
                            toks.append(t)
                        br.free = [t]
                        done.append(last)
                    else:
                        x = {0: 0, 1: 8, 3: 16, 4: 24}[m]
                        b = psum.get()
                        for k in range(8):
                            last = mm([prev, b.free, t_cst], b.ap[:, k:k + 1], a_[:, k * 128:(k + 1) * 128],
                                      ones[:, 0:1], True, True, k == 7)
                        t = V.op([last, t_cols, mc_free[i]], ve.tensor_tensor, MC2[i][:, x:x + 8], b.ap[:, 0:8],
                                 K("mod_b", i * 48 + m * 8, 8), ADD)
                        b.free = [t]
                        if m in (1, 4):
                            t = V.op([t], ve.tensor_scalar, MC2[i][:, x:x + 8], MC2[i][:, x:x + 8], 1.0, None, ADD)
                        toks.append(t)
                        done.append(last)
                acc_free[0] = done
                t_mod[i] = toks
                yield

        class Beside:
            def __init__(self, gen):
                self.gen = gen

            def step(self, n=1):
                for _ in range(n):
                    if next(self.gen, 1) == 1:
                        return

            def finish(self):
                self.step(1000)

        ss = tiny(2)
        toks = []
        for t in range(2):
            toks.append(A.op([t_x], ac.activation, Y[:, t, :], X[:, t, :], ACT.Square, accum_out=ss[:, t:t + 1]))
        tr = rsqrt(ss, ss, 1.0 / 1024, 1e-6, toks)
        dU = [V.op([tr], ve.tensor_scalar, Y[:, t, :], X[:, t, :], ss[:, t:t + 1], None, MUL) for t in range(2)]

        def ev(k, b, d, t):
            return V.op([t, t_cols], ve.tensor_scalar, d, b, K("norm_in", k), None, MUL)

        tU = transposed(lambda t, k: Y[:, t, k * 128:(k + 1) * 128], dU, XT, 8, ev)

        mod0 = Beside(modulation(0))

        mix = take(3072)
        mixT = mix.rearrange("p (k n) -> p k n", k=12)
        srow = mix[:, 0:2304]

        b = psum.get()
        last = mm([t_cst, t_misc, b.free], b.ap[0:8, 0:384], relb[0:32, :], C("onehot")[0:32, :], True, True, True)
        grow = srow[0:8, 0:384]
        t = V.op([last], ve.tensor_copy, grow, b.ap[0:8, 0:384])
        b.free = [t]
        part = grow.ap[0][0]
        tg = S.dma([t], s_in[4], 16, nc.sync.dma_start, gscr,
                   bass.AP(grow.tensor, grow.offset, [[part, 8], [0, 128], [1, 383]]))
        TB = take(2048).rearrange("p (h n) -> p h n", h=8)
        t_TB = S.dma([tg], s_rb, 16, nc.sync.dma_start, TB,
                     bass.AP(gscr.tensor, 127, [[382, 128], [128 * 383, 8], [1, 256]]))

        qkT = take(2048).rearrange("p (k n) -> p k n", k=8)
        aqk = take(2048).rearrange("p (k n) -> p k n", k=8)
        azT = take(1024).rearrange("p (k n) -> p k n", k=4)
        iqT = take(1024).rearrange("p (k n) -> p k n", k=4)
        ikT = take(256)
        d_b1 = {}
        gate = {}

        def conv(o, b, i, taps, wcol, tokens):
            t = V.op(tokens, ve.tensor_scalar, o, b, wcol(taps - 1), None, MUL)
            for j in range(taps - 2, -1, -1):
                s = taps - 1 - j
                t = V.op([t], ve.scalar_tensor_tensor, o[:, s:256], b[:, 0:256 - s], wcol(j), o[:, s:256], MUL, ADD)
            return t

        def ev_in(j, n, b, last):
            half = [b.ap[:, i * 256:(i + 1) * 256] for i in range(n)]
            if j < 8:
                fr = []
                for i in range(n):
                    s = wk.get()
                    cv = s.ap[:, 0:256]
                    k = j + i
                    t = conv(cv, half[i], 0, 4, lambda q: K("conv_w", q * 8 + k), [last, s.free, t_cols])
                    fr.append(t)
                    t = A.op([t], ac.activation, s.ap[:, 256:512], cv, ACT.Sigmoid)
                    t = V.op([t], ve.tensor_tensor, qkT[:, k, :], cv, s.ap[:, 256:512], MUL)
                    s.free = [t]
                    d_b1["qk", k] = t
                return fr
            if j < 12:
                t = A.op([last], ac.activation, aqk[:, j - 8:j - 6, :],
                         b.ap.rearrange("p (k n) -> p k n", k=2), ACT.Copy, scale=0.125)
                d_b1["aq", j - 8] = d_b1["aq", j - 7] = t
                return [t]
            if j < 16:
                t = A.op([last], ac.activation, aqk[:, j - 8:j - 6, :],
                         b.ap.rearrange("p (k n) -> p k n", k=2), ACT.Copy)
                d_b1["ak", j - 12] = d_b1["ak", j - 11] = t
                return [t]
            if j < 20:
                o = azT[:, j - 16:j - 14, :]
                p2 = b.ap.rearrange("p (k n) -> p k n", k=2)
                t = A.op([last], ac.activation, o, p2, ACT.Sigmoid)
                t = V.op([t], ve.tensor_tensor, o, o, p2, MUL)
                d_b1["az", j - 16] = d_b1["az", j - 15] = t
                return [t]
            if j < 24:
                t = A.op([last], ac.activation, iqT[:, j - 20:j - 18, :],
                         b.ap.rearrange("p (k n) -> p k n", k=2), ACT.Copy)
                d_b1["iq", j - 20] = d_b1["iq", j - 19] = t
                return [t]
            t = A.op([last], ac.activation, ikT, half[0], ACT.Copy)
            d_b1["ik"] = t
            return [t]

        def chunked_b(xT, deps, nk, src, blocks, evac, step):
            per = 2048 // (128 * nk)
            for u in range((blocks + per - 1) // per):
                nb = min(per, blocks - u * per)
                proj_b(xT, deps, nk, src[u:u + 1], nb, lambda j, n, b, l: evac(u * per + j, n, b, l))
                step(u)

        chunked_b(XT, tU, 8, D["w_in_b"], 25, ev_in, lambda u: mod0.step(1 + u % 2))

        w, tw = load(D["w_in_g"][0], 128)
        bi, bf, bw = psum.get(), psum.get(), psum.get()
        for k in range(8):
            l1 = mm([tw, tU[k], bi.free], bi.ap[0:4, 0:256], w.ap[:, k * 16:k * 16 + 4], XT[:, k, :],
                    k == 0, k == 7, k == 7)
        for k in range(8):
            l2 = mm([tw, bf.free], bf.ap[0:4, 0:256], w.ap[:, k * 16 + 4:k * 16 + 8], XT[:, k, :],
                    k == 0, k == 7, k == 7)
        for t in range(2):
            for k in range(8):
                l3 = mm([tw, bw.free], bw.ap[:, t * 8:t * 8 + 8], XT[:, k, t * 128:(t + 1) * 128],
                        w.ap[:, k * 16 + 8:k * 16 + 16], k == 0, k == 7, k == 7)
        w.free = [l3]
        iw = tiny(16)
        t_iw = V.op([l3], ve.tensor_scalar, iw, bw.ap[:, 0:16], 8.0 ** -0.5, None, MUL)
        bw.free = [t_iw]

        def sr(i):
            return srow[0:4, i * 256:(i + 1) * 256]

        LI, FS, AB, LF, BC, AR, MR = (sr(i) for i in range(2, 9))
        NM, BM = sr(0), sr(1)
        t_li = V.op([l1, t_cols], ve.tensor_scalar, LI, bi.ap[0:4, 0:256], K("b_gate", 0)[0:4, :], None, ADD)
        bi.free = [t_li]
        t_fs = V.op([l2], ve.tensor_scalar, FS, bf.ap[0:4, 0:256], K("b_gate", 1)[0:4, :], None, ADD)
        bf.free = [t_fs]
        t = A.op([t_fs], ac.activation, AB, FS, ACT.Abs)
        t = A.op([t], ac.activation, AB, AB, ACT.Exp, scale=-1.0)
        t = V.op([t], ve.tensor_scalar, AB, AB, 1.0, None, ADD)
        t = A.op([t], ac.activation, AB, AB, ACT.Ln)
        t2 = V.op([t_fs], ve.tensor_scalar, LF, FS, 0.0, None, MIN)
        t = V.op([t, t2], ve.tensor_tensor, LF, LF, AB, SUB)
        t_bc = V.op([t, t_cst], ve.tensor_tensor_scan, BC, ones[0:4, 0:256], LF, 0.0, MUL, ADD)
        t_ar = V.op([t_bc], ve.tensor_tensor, AR, LI, BC, SUB)
        t_mr = V.op([t_ar], ve.tensor_tensor_scan, MR, AR, AR, 0.0, MAX, MAX)
        t_nm = V.op([t_mr, tg], ve.tensor_scalar, NM, MR, -1.0, None, MUL)
        t_bm = V.op([t_mr, tg], ve.tensor_tensor, BM, MR, BC, ADD)
        em, acol = tiny(8), tiny(8)
        b = psum.get()
        for t in range(2):
            P.quiet([t_bm, b.free, t_cst], pe.transpose, b.ap[:, t * 4:t * 4 + 4],
                    BM[:, t * 128:(t + 1) * 128], ID[0:4, 0:4])
            last = P.op([t_ar], pe.transpose, b.ap[:, 8 + t * 4:12 + t * 4],
                        AR[:, t * 128:(t + 1) * 128], ID[0:4, 0:4])
        t_em = A.op([last], ac.activation, em, b.ap[:, 0:8], ACT.Exp, scale=-1.0)
        t_ac = V.op([t_em], ve.tensor_copy, acol, b.ap[:, 8:16])
        b.free = [t_ac]

        GT = take(2048).rearrange("p (t n) -> p t n", t=2)
        mv = take(2 * 4 * 258).rearrange("p (t h n) -> p t h n", t=2, h=4)
        av = take(1024).rearrange("p (t n) -> p t n", t=2)
        hm = take(2048).rearrange("p (t n) -> p t n", t=2)
        t_one = [G.op([], po.memset, mv[:, t, :, 256:257], 1.0) for t in range(2)]
        d_mv, d_av, d_g = {}, {}, {}
        mns = {}

        def ev_ina(t, cb, b, last):
            if cb < 2:
                t1 = A.op([last], ac.activation, GT[:, t, cb * 512:(cb + 1) * 512], b.ap, ACT.Sigmoid)
                d_g[t, cb] = t1
                return [t1]
            if cb < 4:
                c = cb - 2
                if t == 0:
                    mns[c] = rows(("m_norm", c * 512, 512))
                mn, tmn = mns[c]
                s = wk.get()
                g = GT[:, t, c * 512:(c + 1) * 512]
                t1 = A.op([last, s.free], ac.activation, s.ap, b.ap, ACT.Sigmoid)
                t2 = V.op([t1], ve.tensor_tensor, s.ap, s.ap, b.ap, MUL)
                t3 = V.op([t2, d_g[t, c]], ve.tensor_tensor, g, g, s.ap, MUL)
                s.free = [t3]
                t4 = G.op([t3, tmn], po.tensor_tensor, g, g, mn.ap[:, 0:512], MUL)
                mn.free = [t4]
                d_g[t, c] = t4
                return [t2]
            if cb < 6:
                h0 = (cb - 4) * 2
                t1 = copy(mv[:, t, h0:h0 + 2, 0:256], b.ap.rearrange("p (h n) -> p h n", h=2), [last])
                d_mv[t, h0] = d_mv[t, h0 + 1] = t1
                return [t1]
            t1 = copy(av[:, t, :], b.ap, [last])
            d_av[t] = t1
            return [t1]

        def chunked_a(xT, deps, nk, src, blocks, evac, step):
            nq = (nk + 3) // 4
            for cb in range(blocks):
                proj_a(xT, deps, nk, src[cb * nq:(cb + 1) * nq], 1, lambda t, c, b, l: evac(t, cb, b, l))
                step(cb)

        chunked_a(XT, tU, 8, D["w_in_a"], 7, ev_ina, lambda u: mod0.step(2))

        wsel = [None, None]
        t_sel = [None, None]
        for t in range(2):
            W = 128 * (t + 1)
            sc = [Y[:, 0, (2 * t + q) * 256:(2 * t + q + 1) * 256] for q in range(2)]
            prev = None
            for hs in ((0, 2), (1, 3), (4, 6), (5, 7)):
                b = psum.get()
                for e, h in enumerate(hs):
                    r = slice(64 * (h % 2), 64 * (h % 2) + 64)
                    last = mm([d_b1["iq", h // 2], d_b1["ik"], b.free], b.ap[:, e * W:(e + 1) * W],
                              iqT[r, h // 2, t * 128:(t + 1) * 128], ikT[r, 0:W], True, True, e == 1)
                s = wk.get()
                t1 = A.op([last, s.free], ac.activation, s.ap[:, 0:2 * W], b.ap[:, 0:2 * W], ACT.Relu, scale=0.125)
                b.free = [t1]
                for e, h in enumerate(hs):
                    src = s.ap[:, e * W:(e + 1) * W]
                    prev = V.op([t1, t_iw, prev, t_cst], ve.scalar_tensor_tensor, sc[0][:, 0:W], src,
                                iw[:, t * 8 + h:t * 8 + h + 1],
                                C("cm", 256 - W, 256) if h == 0 else sc[0][:, 0:W], MUL, ADD)
                s.free = [prev]
            m8 = tiny(16)
            for i in range(8):
                q = m8[:, (i % 2) * 8:(i % 2) * 8 + 8]
                t1 = V.op([prev], ve.max, q, sc[i % 2][:, 0:W])
                prev = V.op([t1], ve.match_replace, sc[(i + 1) % 2][:, 0:W], q, sc[i % 2][:, 0:W], -3e38)
            t1 = V.op([prev], ve.tensor_scalar, sc[1][:, 0:W], sc[0][:, 0:W], -2e38, -BIG, ALU.is_ge, MUL)
            t_sel[t] = V.op([t1, t_cst], ve.tensor_tensor, sc[1][:, 0:W], sc[1][:, 0:W], C("cm", 256 - W, 256), ADD)
            wsel[t] = sc[1]
            mod0.step(2)

        hss = tiny(8)
        rdn = tiny(8)
        d_h = {}
        for h in range(4):
            ST = []
            for j in range(2):
                W = 256 - 128 * j
                b = psum.get()
                mm([t_nm, t_cst, b.free], b.ap[:, 0:W], C("sel", h * 128, h * 128 + 128)[0:4, :],
                   NM[:, j * 128:256], True, True)
                last = mm([d_b1["qk", 4 + h], d_b1["qk", h]], b.ap[:, 256:256 + W],
                          qkT[:, 4 + h, j * 128:(j + 1) * 128], qkT[:, h, j * 128:256], True, True, True)
                s = wk.get()
                e = s.ap[:, 0:W]
                t1 = V.op([last, t_ac, s.free], ve.scalar_tensor_tensor, e, b.ap[:, 0:W],
                          acol[:, j * 4 + h:j * 4 + h + 1], C("cmT", 0, W), ADD, ADD)
                t1 = A.op([t1], ac.activation, e, e, ACT.Exp)
                t1 = V.op([t1], ve.scalar_tensor_tensor, e, b.ap[:, 256:256 + W], 128.0 ** -0.5, e, MUL, MUL)
                b.free = [t1]
                ST.append((s, t1))
            for t in range(2):
                b = psum.get()
                for j in range(t + 1):
                    c = (t - j) * 128
                    last = mm([ST[j][1], d_mv[j, h], t_one, b.free], b.ap[:, 0:257], ST[j][0].ap[:, c:c + 128],
                              mv[:, j, h, 0:257], j == 0, j == t, j == t)
                i = t * 4 + h
                t1 = V.op([last, t_em], ve.tensor_scalar, rdn[:, i:i + 1], b.ap[:, 256:257], -1.0, None, MUL)
                t1 = V.op([t1], ve.scalar_tensor_tensor, rdn[:, i:i + 1], b.ap[:, 256:257], em[:, i:i + 1],
                          rdn[:, i:i + 1], MAX, MAX)
                t1 = V.op([t1], ve.reciprocal, rdn[:, i:i + 1], rdn[:, i:i + 1])
                o = hm[:, t, h * 256:(h + 1) * 256]
                t1 = A.op([t1], ac.activation, o, b.ap[:, 0:256], ACT.Copy, scale=rdn[:, i:i + 1])
                b.free = [t1]
                s = wk.get()
                d_h[i] = A.op([t1, s.free], ac.activation, s.ap[:, 0:256], o, ACT.Square, accum_out=hss[:, i:i + 1])
                s.free = [d_h[i]]
            for s, _ in ST:
                s.free = [last]
            mod0.step(1)
        t1 = rsqrt(hss, hss, 1.0 / 256, 1e-6, [d_h[i] for i in range(8)])
        d_hm = [None, None]
        for t in range(2):
            for h in range(4):
                o = hm[:, t, h * 256:(h + 1) * 256]
                d_hm[t] = V.op([t1, d_g[t, h // 2]], ve.scalar_tensor_tensor, o, o, hss[:, t * 4 + h:t * 4 + h + 1],
                               GT[:, t, h * 256:(h + 1) * 256], MUL, MUL)

        def ev_copy(k, b, d, t):
            if k // 2 % 2:
                return A.op([t], ac.copy, d, b)
            return V.op([t], ve.tensor_copy, d, b)

        t_mix = [None] * 12
        t_mix[0:8] = transposed(lambda t, k: hm[:, t, k * 128:(k + 1) * 128], d_hm, mixT, 8, ev_copy)

        nmx, smx = tiny(16), tiny(16)

        def attention(score, add_bias, value, dh, finish, lag=2, beside=None):
            items = [(h, t) for h in range(8) for t in range(2)]
            Ps, PTs, outs = {}, {}, {}

            def first(i):
                h, t = items[i]
                W = 128 * (t + 1)
                b = psum.get()
                last = score(h, t, W, b)
                s = wk.get()
                p = s.ap[:, 0:W]
                t1 = add_bias(h, t, W, b, p, [last, s.free])
                b.free = [t1]
                t2 = V.op([t1], ve.tensor_reduce, nmx[:, i:i + 1], p, AX.X, MAX, negate=True)
                t3 = A.op([t2], ac.activation, p, p, ACT.Exp, bias=nmx[:, i:i + 1], accum_out=smx[:, i:i + 1])
                t4 = V.op([t3], ve.reciprocal, smx[:, i:i + 1], smx[:, i:i + 1])
                t5 = V.op([t4], ve.tensor_scalar, p, p, smx[:, i:i + 1], None, MUL)
                Ps[i] = s, t5

            def second(i):
                h, t = items[i]
                s, tk = Ps[i]
                b = psum.get()
                for j in range(t + 1):
                    last = P.op([tk, b.free], pe.transpose, b.ap[:, j * 128:(j + 1) * 128],
                                s.ap[:, j * 128:(j + 1) * 128], ID)
                s.free = [last]
                d = pt.get()
                t1 = A.op([last, d.free], ac.copy, d.ap[:, 0:128 * (t + 1)], b.ap[:, 0:128 * (t + 1)])
                b.free = [t1]
                PTs[i] = d, t1

            def third(i):
                h, t = items[i]
                d, tk = PTs[i]
                per = 128 // dh
                if t == 0 and h % per == 0:
                    outs["b"] = psum.get()
                b = outs["b"]
                r0 = (h % per) * dh
                for j in range(t + 1):
                    vt, l = value(j, h)
                    last = mm([tk, vt, b.free], b.ap[r0:r0 + dh, t * 128:(t + 1) * 128], l,
                              d.ap[:, j * 128:(j + 1) * 128], j == 0, j == t, j == t)
                d.free = [last]
                if t == 1 and h % per == per - 1:
                    b.free = finish(h // per, b, last)

            n = len(items)
            for i in range(n + 2 * lag):
                if i < n:
                    first(i)
                if 0 <= i - lag < n:
                    second(i - lag)
                if 0 <= i - 2 * lag < n:
                    third(i - 2 * lag)
                if beside is not None:
                    beside.step()

        def score1(h, t, W, b):
            r = slice(64 * (h % 2), 64 * (h % 2) + 64)
            return mm([d_b1["aq", h // 2], d_b1["ak", h // 2], b.free], b.ap[:, 0:W],
                      aqk[r, h // 2, t * 128:(t + 1) * 128], aqk[r, 4 + h // 2, 0:W], True, True, True)

        bmt = Turn([Y[:, 1, q * 256:(q + 1) * 256] for q in range(2)])

        def bias1(h, t, W, b, p, toks_):
            s = bmt.get()
            t1 = G.op([t_TB, t_sel[t], s.free], po.tensor_tensor, s.ap[:, 0:W], TB[:, h, 256 - W:256],
                      wsel[t][:, 0:W], ADD)
            t2 = V.op([t1, toks_], ve.tensor_tensor, p, b.ap[:, 0:W], s.ap[:, 0:W], ADD)
            s.free = [t2]
            return t2

        def fin1(k, b, last):
            t_mix[8 + k] = V.op([last, d_b1["az", k]], ve.tensor_tensor, mixT[:, 8 + k, :], b.ap[:, 0:256],
                                azT[:, k, :], MUL)
            return [t_mix[8 + k]]

        attention(score1, bias1, lambda j, h: (d_av[j], av[:, j, h * 64:(h + 1) * 64]), 64, fin1, beside=mod0)
        mod0.finish()

        d_r = [[None, None], [None, None]]

        def ev_wo(t, cb, b, last):
            o = X[:, t, cb * 512:(cb + 1) * 512]
            d_r[t][cb] = V.op([last, toks, dU], ve.tensor_tensor, o, o, b.ap, ADD)
            return [d_r[t][cb]]

        proj_a(mixT, t_mix, 12, D["w_out"], 2, ev_wo)
        tH = transposed(lambda t, k: X[:, t, k * 128:(k + 1) * 128], d_r, XT, 8, ev_copy)
        pl = {}

        def ev_ple(t, cb, b, last):
            pl[t, cb] = (b, last)
            return []

        proj_a2(pT, [t_misc, t_misc], D["w_ple"], ev_ple)
        d_x1 = [[None, None], [None, None]]

        def ev_gate(t, cb, b, last):
            s = wk.get()
            t1 = A.op([last, s.free], ac.activation, s.ap, b.ap, ACT.Sigmoid)
            pb_, pl_ = pl[t, cb]
            t2 = V.op([t1, pl_], ve.tensor_tensor, s.ap, s.ap, pb_.ap, MUL)
            pb_.free = [t2]
            o = X[:, t, cb * 512:(cb + 1) * 512]
            d_x1[t][cb] = V.op([t2, tH], ve.tensor_tensor, o, o, s.ap, ADD)
            s.free = [d_x1[t][cb]]
            return [t1]

        proj_a(XT, tH, 8, D["w_gate"], 2, ev_gate)
        nf, tnf = rows(("norm_final", 0, 1024))
        fs = tiny(2)
        d_x = []
        for t in range(2):
            t1 = A.op([d_x1[t], tU], ac.activation, Y[:, t, :], X[:, t, :], ACT.Square, accum_out=fs[:, t:t + 1])
            t1 = rsqrt(fs[:, t:t + 1], fs[:, t:t + 1], 1.0 / 1024, 1e-6, [t1])
            d_x.append(V.op([t1, tnf], ve.scalar_tensor_tensor, X[:, t, :], X[:, t, :], fs[:, t:t + 1],
                            nf.ap[:, 0:1024], MUL, MUL))
        nf.free = [d_x[1]]

        at[0] = 512
        cosT, sinT, posf, dist = take(256), take(256), take(258), take(512).rearrange("p (t n) -> p t n", t=2)
        base_at = at[0]
        ready = [d_x[1], tH, [d_r[t][c] for t in range(2) for c in range(2)]]
        t_pf = V.op([ready, t_misc], ve.tensor_copy, posf, posi[:, 0:258])
        a1, a2 = wk.get(), wk.get()
        ang, kk_ = a1.ap[:, 0:256], a1.ap[:, 256:512]
        TWO_PI = 6.283185307179586
        C1 = 6.28125
        C2 = float(np.float32(TWO_PI - C1))
        C2 = float(np.round(C2 * 2 ** 21) / 2 ** 21)
        C3 = TWO_PI - C1 - C2
        MAGIC = 12582912.0
        t_ang = V.op([t_pf, a1.free], ve.tensor_scalar, ang, posf[:, 0:256], K("inv_freq"), None, MUL)
        t_tab = []
        for tab, quarter in ((sinT, 0.0), (cosT, 0.25)):
            t1 = V.op([t_ang, t_tab[-1:] and t_tab[-1]], ve.tensor_scalar, kk_, ang, 1.0 / TWO_PI, quarter, MUL, ADD)
            t1 = V.op([t1], ve.tensor_scalar, kk_, kk_, MAGIC, None, ADD)
            t1 = V.op([t1], ve.tensor_scalar, kk_, kk_, -MAGIC, None, ADD)
            src = ang
            for cc in (C1, C2, C3):
                t1 = V.op([t1], ve.scalar_tensor_tensor, tab, kk_, -cc, src, MUL, ADD)
                src = tab
            if quarter:
                t1 = V.op([t1], ve.tensor_scalar, tab, tab, TWO_PI / 4, None, ADD)
            t1 = V.op([t1], ve.tensor_scalar, tab, tab, 3.1415925, -3.1415925, MIN, MAX)
            t1 = A.op([t1], ac.activation, tab, tab, ACT.Sin)
            if not quarter:
                t1 = V.op([t1, t_cols], ve.tensor_scalar, tab, tab, K("sign"), None, MUL)
            t_tab.append(t1)
        a1.free = a2.free = [t_tab[-1]]
        for t in range(2):
            t1 = V.op([t_pf], ve.tensor_scalar, dist[:, t, :], posf[:, 0:256], posf[:, 256 + t:257 + t], None, SUB)
            t1 = V.op([t1], ve.scalar_tensor_tensor, dist[:, t, :], dist[:, t, :], -1.0, dist[:, t, :], MUL, MAX)
            W = 128 * (t + 1)
            t_dist = V.op([t1], ve.tensor_tensor, dist[:, t, 0:W], dist[:, t, 0:W], C("cm", 256 - W, 256), SUB)

        ALPHA = 4.0 ** 0.25
        st = tiny(24)
        mv2 = tiny(8)

        def modulated(i, which, deps):
            a, s_ = (8, 0) if which == 0 else (24, 16)

            def e(k, b, d, t):
                m = MC2[i]
                if k // 2 % 2:
                    return A.op([t, t_mod[i]], ac.activation, d, b, ACT.Identity, bias=m[:, s_ + k:s_ + k + 1],
                                scale=m[:, a + k:a + k + 1])
                return V.op([t, t_mod[i]], ve.tensor_scalar, d, b, m[:, a + k:a + k + 1], m[:, s_ + k:s_ + k + 1],
                            MUL, ADD)
            return transposed(lambda t, k: X[:, t, k * 128:(k + 1) * 128], deps, XT, 8, e)

        d_z = [[None, None], [None, None]]

        def ev_resid(r, i, xdeps):
            def e(t, cb, b, last):
                cs = slice(cb * 512, (cb + 1) * 512)
                s = wk.get()
                t1 = V.op([last, t_mod[i], s.free], ve.tensor_tensor, s.ap, b.ap, R2[:, r, cs], MUL)
                t2 = V.op([t1, xdeps], ve.scalar_tensor_tensor, X[:, t, cs], X[:, t, cs], ALPHA, s.ap, MUL, ADD)
                s.free = [t2]
                d_z[t][cb] = t2
                return [t1]
            return e

        def layer_norm(n):
            g, tg_ = rows(("ln", n * 2048, 2048))
            out_t = []
            for t in range(2):
                sv = st[:, t * 12:(t + 1) * 12].rearrange("p (c s) -> p c s", c=2)
                for c in range(2):
                    t1 = V.op([d_z[t][c]], ve.bn_stats, sv[:, c, :], X[:, t, c * 512:(c + 1) * 512])
                m = mv2[:, t * 4:t * 4 + 4]
                t1 = V.op([t1], ve.bn_aggr, m[:, 0:2], sv)
                t1 = rsqrt(m[:, 1:2], m[:, 2:3], 1.0, 1e-5, [t1])
                t1 = V.op([t1], ve.tensor_scalar, X[:, t, :], X[:, t, :], m[:, 0:1], m[:, 2:3], SUB, MUL)
                t1 = V.op([t1, tg_], ve.tensor_tensor, X[:, t, :], X[:, t, :], g.ap[:, 0:1024], MUL)
                t1 = V.op([t1], ve.tensor_tensor, X[:, t, :], X[:, t, :], g.ap[:, 1024:2048], ADD)
                out_t.append(t1)
            g.free = [t1]
            return out_t

        def ffn(i, deps, beside):
            gT = Y_big
            tX = modulated(i, 1, deps)
            tg_ = [None] * 22
            for u in range(11):
                hold = {}

                def eva(j, n, b, last):
                    s = wk.get()
                    fr, t1s = [], []
                    for q in range(2):
                        k = 2 * u + q
                        t1s.append(A.op([last, s.free, t_cols], ac.activation, s.ap[:, q * 256:(q + 1) * 256],
                                        b.ap[:, q * 256:(q + 1) * 256], ACT.Identity, bias=K("fconv_b", i * 22 + k),
                                        scale=K("fconv_w", i * 66 + 44 + k)))
                    for q in range(2):
                        k = 2 * u + q
                        hb = b.ap[:, q * 256:(q + 1) * 256]
                        o = s.ap[:, q * 256:(q + 1) * 256]
                        lo = COL_AT["fconv_w"][0] + i * 66 + k
                        t1 = t1s
                        for j2 in (1, 0):
                            sh = 2 - j2
                            t1 = V.op([t1], ve.scalar_tensor_tensor, o[:, sh:256], hb[:, 0:256 - sh],
                                      cols[:, lo + 22 * j2:lo + 22 * j2 + 1], o[:, sh:256], MUL, ADD)
                        fr.append(t1)
                    t1 = A.op(fr, ac.activation, s.ap, s.ap, ACT.Gelu_apprx_tanh)
                    hold["a"] = s, t1
                    return fr

                def evb(j, n, b, last):
                    s, t1 = hold["a"]
                    t2 = V.op([last, t1], ve.tensor_tensor, gT[:, 2 * u:2 * u + 2, :],
                              s.ap.rearrange("p (k n) -> p k n", k=2), b.ap.rearrange("p (k n) -> p k n", k=2), MUL)
                    s.free = [t2]
                    tg_[2 * u] = tg_[2 * u + 1] = t2
                    return [t2]

                proj_b(XT, tX, 8, D[f"ffn_a{i}"][u:u + 1], 2, eva)
                proj_b(XT, tX, 8, D[f"ffn_b{i}"][u:u + 1], 2, evb)
                if beside is not None:
                    beside.step(2)
            if beside is not None:
                beside.finish()
            proj_a(gT, tg_, 22, D[f"ffn_o{i}"], 2, ev_resid(1, i, deps))
            return layer_norm(2 * i + 1)

        cq = take(1024).rearrange("p (t n) -> p t n", t=2)
        cT = take(1024).rearrange("p (k n) -> p k n", k=4)
        qT = take(2048).rearrange("p (k n) -> p k n", k=8)
        kT = take(2048).rearrange("p (k n) -> p k n", k=8)
        qr = take(1024).rearrange("p (k n) -> p k n", k=4)
        kr = take(256)
        vv = take(2048).rearrange("p (t n) -> p t n", t=2)
        oT = take(2048).rearrange("p (k n) -> p k n", k=8)
        at[0] = base_at
        Y_big = take(22 * 256).rearrange("p (k n) -> p k n", k=22)

        tX = modulated(0, 0, d_x)
        cs4 = tiny(4)
        d_cq = [None, None]

        def ev_cq(t, cb, b, last):
            t1 = None
            for c in range(2):
                s = wk.get()
                t1 = A.op([last, s.free], ac.activation, s.ap[:, 0:256], b.ap[:, c * 256:(c + 1) * 256], ACT.Square,
                          accum_out=cs4[:, 2 * t + c:2 * t + c + 1])
                s.free = [t1]
            t1 = rsqrt(cs4[:, 2 * t:2 * t + 2], cs4[:, 2 * t:2 * t + 2], 1.0 / 256, 1e-6, [t1])
            for c in range(2):
                t2 = V.op([t1], ve.tensor_scalar, cq[:, t, c * 256:(c + 1) * 256], b.ap[:, c * 256:(c + 1) * 256],
                          cs4[:, 2 * t + c:2 * t + c + 1], None, MUL)
            d_cq[t] = t2
            return [t2]

        proj_a(XT, tX, 8, D["mla_c"], 1, ev_cq)

        def rope(o, b, last):
            s = wk.get()
            t1 = V.op([last, t_tab, s.free], ve.tensor_tensor, s.ap[:, 0:256], b.ap[:, 0:256], cosT, MUL)
            t2 = V.op([last, t_tab], ve.tensor_tensor, s.ap[:, 256:512], b.ap[:, 256:512], sinT, MUL)
            t3 = G.op([t1, t2], po.tensor_tensor, o, s.ap[:, 0:256], s.ap[:, 256:512], ADD)
            s.free = [t3]
            return t2, t3

        d_kr = []

        def ev_kr(j, n, b, last):
            t2, t3 = rope(kr, b, last)
            d_kr.append(t3)
            return [t2]

        proj_b(XT, tX, 8, D["mla_kr"], 2, ev_kr)

        def ev_c(k, b, d, t):
            return V.op([t], ve.tensor_scalar, d, b, K("q_norm", k) if k < 2 else K("kv_norm", k - 2), None, MUL)

        tC = transposed(lambda t, k: cq[:, t, k * 128:(k + 1) * 128], d_cq, cT, 4, ev_c)
        d_q, d_k, d_qr, d_v = [None] * 8, [None] * 8, [None] * 4, {}

        def ev_q(j, n, b, last):
            if j < 8:
                t1 = copy(qT[:, j:j + 2, :], b.ap.rearrange("p (k n) -> p k n", k=2), [last])
                d_q[j] = d_q[j + 1] = t1
                return [t1]
            t2, t3 = rope(qr[:, (j - 8) // 2, :], b, last)
            d_qr[(j - 8) // 2] = t3
            return [t2]

        proj_b(cT[:, 0:2, :], tC[0:2], 2, D["mla_uq"], 16, ev_q)

        def ev_k(j, n, b, last):
            t1 = copy(kT[:, j:j + 2, :], b.ap.rearrange("p (k n) -> p k n", k=2), [last])
            d_k[j] = d_k[j + 1] = t1
            return [t1]

        proj_b(cT[:, 2:4, :], tC[2:4], 2, D["mla_uk"], 8, ev_k)

        def ev_v(t, cb, b, last):
            d_v[t, cb] = copy(vv[:, t, cb * 512:(cb + 1) * 512], b.ap, [last])
            return [d_v[t, cb]]

        proj_a2(cT[:, 2:4, :], tC[2:4], D["mla_uv"], ev_v)

        def score2(h, t, W, b):
            r = slice(64 * (h % 2), 64 * (h % 2) + 64)
            mm([d_q[h], d_k[h], b.free], b.ap[:, 0:W], qT[:, h, t * 128:(t + 1) * 128], kT[:, h, 0:W], True, False)
            return mm([d_qr[h // 2], d_kr], b.ap[:, 0:W], qr[r, h // 2, t * 128:(t + 1) * 128], kr[r, 0:W],
                      False, True, True)

        def bias2(h, t, W, b, p, toks_):
            return V.op(toks_, ve.scalar_tensor_tensor, p, b.ap[:, 0:W], 192.0 ** -0.5, C("cm", 256 - W, 256),
                        MUL, ADD)

        d_o = [None] * 8

        def fin2(k, b, last):
            d_o[k] = copy(oT[:, k, :], b.ap[:, 0:256], [last])
            return [d_o[k]]

        def val2(j, h):
            return d_v[j, h // 4], vv[:, j, h * 128:(h + 1) * 128]

        attention(score2, bias2, val2, 128, fin2)
        proj_a(oT, d_o, 8, D["mla_o"], 2, ev_resid(0, 0, tX))
        d1 = layer_norm(0)
        mod1 = Beside(modulation(1))

        class Late:
            def step(self, n=1):
                pass

            def finish(self):
                pass

        d2 = ffn(0, d1, Late())
        r2_free[0] = list(d_z[0]) + list(d_z[1])
        mod1.finish()

        tX = modulated(1, 0, d2)

        def ev_q3(j, n, b, last):
            t1 = A.op([last], ac.activation, qT[:, j:j + 2, :], b.ap.rearrange("p (k n) -> p k n", k=2), ACT.Copy,
                      scale=128.0 ** -0.5)
            d_q[j] = d_q[j + 1] = t1
            return [t1]

        proj_b(XT, tX, 8, D["moba_q"], 8, ev_q3)
        proj_b(XT, tX, 8, D["moba_k"], 8, ev_k)
        proj_a(XT, tX, 8, D["moba_v"], 2, ev_v)

        def score3(h, t, W, b):
            return mm([d_q[h], d_k[h], b.free], b.ap[:, 0:W], qT[:, h, t * 128:(t + 1) * 128], kT[:, h, 0:W],
                      True, True, True)

        def bias3(h, t, W, b, p, toks_):
            return V.op([toks_, t_dist], ve.scalar_tensor_tensor, p, dist[:, t, 0:W], -(2.0 ** -(h + 1)),
                        b.ap[:, 0:W], MUL, ADD)

        attention(score3, bias3, val2, 128, fin2)
        proj_a(oT, d_o, 8, D["moba_o"], 2, ev_resid(0, 1, tX))
        d1 = layer_norm(2)
        d2 = ffn(1, d1, None)
        s_out = sem("s_out")
        for t in range(2):
            S.dma([d2[t]], s_out, 16 * (t + 1), nc.sync.dma_start, out[t * 128:(t + 1) * 128, :], X[:, t, :])
        S.wait([(s_out, 32)])

        block = ctx.enter_context(nc.Block())

        @block.sync
        def _(eng):
            S.emit(eng)

        @block.gpsimd
        def _(eng):
            G.emit(eng)

        @block.scalar
        def _(eng):
            A.emit(eng)

        @block.vector
        def _(eng):
            V.emit(eng)

        @block.tensor
        def _(eng):
            P.emit(eng)


def constants():
    c = np.zeros((128, NCONST), np.float32)

    def put(name, a):
        c[:a.shape[0], CONST_AT[name][0]:CONST_AT[name][0] + a.shape[1]] = a

    put("ident", np.eye(128, dtype=np.float32))
    put("ones", np.ones((128, 256), np.float32))
    sel = np.zeros((4, 4, 128), np.float32)
    for h in range(4):
        sel[h, h] = 1.0
    put("sel", sel.reshape(4, 512))
    d = np.maximum(255 - np.arange(383), 0)
    large = 16 + (np.log(np.maximum(d, 1).astype(np.float32) / np.float32(16)) / np.log(8.0) * 16).astype(np.int32)
    bucket = np.where(d < 16, d, np.minimum(large, 31))
    oh = np.zeros((32, 384), np.float32)
    oh[bucket, np.arange(383)] = 1.0
    put("onehot", oh)
    i = np.arange(128)
    up = np.where(i[None, :] > i[:, None], -BIG, 0.0).astype(np.float32)
    z = np.zeros((128, 128), np.float32)
    put("cm", np.concatenate([z, up], 1))
    put("cmT", np.concatenate([up.T, z], 1))
    return c


def pack_b(w):
    nk, nb = w.shape[0] // 128, w.shape[1] // 128
    per = 16 // nk
    nu = -(-nb // per)
    out = np.zeros((nu, 128, per, nk, 128), w.dtype)
    for j in range(nb):
        out[j // per, :, j % per] = w[:, j * 128:(j + 1) * 128].reshape(nk, 128, 128).transpose(1, 0, 2)
    return out.reshape(nu, 128, 2048)


def pack_a(w):
    nk, ncb = w.shape[0] // 128, w.shape[1] // 512
    nq = -(-nk // 4)
    out = np.zeros((ncb, nq, 128, 4, 512), w.dtype)
    for cb in range(ncb):
        for k in range(nk):
            out[cb, k // 4, :, k % 4] = w[k * 128:(k + 1) * 128, cb * 512:(cb + 1) * 512]
    return out.reshape(ncb * nq, 128, 2048)


def pack_a2(w):
    return np.ascontiguousarray(w.reshape(2, 128, 2, 512).transpose(1, 2, 0, 3).reshape(1, 128, 2048))


def layout(I):
    f = np.float32
    a = {k: np.asarray(v) for k, v in I.items()}
    o = {}
    o["x"] = a["x"][0]
    o["pT"] = np.ascontiguousarray(a["p"][0, 0].T)
    o["rel_bias"] = a["rel_bias"]
    o["pos_r"] = a["positions_2"].reshape(1, 256)
    o["pos_c"] = np.ascontiguousarray(a["positions_2"].reshape(2, 128).T)
    o["consts"] = constants()
    c = np.zeros((128, NCOL), f)

    def put(name, m):
        c[:m.shape[0], COL_AT[name][0]:COL_AT[name][0] + m.shape[1]] = m

    def col(v):
        return v.reshape(-1, 128).T

    put("norm_in", col(a["norm_in"][0]))
    put("conv_w", col(a["conv_w"][0].reshape(-1)))
    put("fconv_w", col(a["ffn_conv_w_2"].reshape(-1)))
    put("fconv_b", col(a["ffn_conv_b_2"].reshape(-1)))
    put("q_norm", col(a["mla_q_norm_2"][0]))
    put("kv_norm", col(a["mla_kv_norm_2"][0]))
    put("mod_b", col(a["mod_b_2"].reshape(-1)))
    put("c", col(a["c_2"][0]))
    put("b_gate", a["b_gate"][0].reshape(2, 4).T)
    inv = (10000.0 ** (-np.arange(32, dtype=f) / f(32))).astype(f)
    put("inv_freq", np.tile(inv, 4)[:, None])
    put("sign", np.tile(np.repeat(np.array([-1.0, 1.0], f), 32), 2)[:, None])
    o["cols"] = c
    w = a["w_in"][0]
    cut = np.cumsum([0, 512, 512, 1024, 1024, 1024, 8, 512, 512, 512, 512, 512, 64, 8])
    mq, mk, m_v, mo, mz, mif, aq, ak, a_v, az, iq, ik, iw = (w[:, cut[i]:cut[i + 1]] for i in range(13))
    o["w_in_b"] = pack_b(np.concatenate([mq, mk, aq, ak, az, iq, ik, ik], 1))
    g = np.concatenate([mif, iw], 1).reshape(8, 128, 16).transpose(1, 0, 2).reshape(1, 128, 128)
    o["w_in_g"] = np.ascontiguousarray(g)
    o["w_in_a"] = pack_a(np.concatenate([mo, mz, m_v, a_v], 1))
    o["w_out"] = pack_a(a["w_out"][0])
    o["w_ple"] = pack_a2(a["w_ple"][0])
    o["w_gate"] = pack_a(a["w_ple_gate"][0])
    o["m_norm"], o["norm_final"] = a["m_norm"], a["norm_final"].reshape(1, -1)
    o["mod_b"] = a["mod_b_2"]
    o["mod_w"] = np.ascontiguousarray(a["mod_w_2"].reshape(2, 8, 128, 3, 2048).transpose(0, 3, 1, 2, 4)).reshape(
        48, 128, 2048)
    o["ln"] = np.ascontiguousarray(np.stack([a["ln_g_2"], a["ln_b_2"]], 2).reshape(4, 2048))
    for i in range(2):
        o[f"ffn_a{i}"] = pack_b(a["ffn_w_in_2"][i][:, 0:2816])
        o[f"ffn_b{i}"] = pack_b(a["ffn_w_in_2"][i][:, 2816:])
        o[f"ffn_o{i}"] = pack_a(a["ffn_w_out_2"][i])
    w = a["mla_w_in_2"][0]
    o["mla_c"] = pack_a(w[:, 0:512])
    r, s = w[:, 512:576], np.concatenate([w[:, 544:576], w[:, 512:544]], 1)
    o["mla_kr"] = pack_b(np.concatenate([r, r, s, s], 1))
    w = a["mla_w_uq_2"][0].reshape(256, 8, 192)
    parts = [w[:, :, 0:128].reshape(256, 1024)]
    for j in range(4):
        r = w[:, 2 * j:2 * j + 2, 128:192]
        parts += [r.reshape(256, 128), np.concatenate([r[:, :, 32:], r[:, :, :32]], 2).reshape(256, 128)]
    o["mla_uq"] = pack_b(np.concatenate(parts, 1))
    w = a["mla_w_ukv_2"][0].reshape(256, 8, 256)
    o["mla_uk"] = pack_b(w[:, :, 0:128].reshape(256, 1024))
    o["mla_uv"] = pack_a2(w[:, :, 128:256].reshape(256, 1024))
    o["mla_o"] = pack_a(a["mla_w_o_2"][0])
    w = a["moba_w_in_2"][0]
    o["moba_q"], o["moba_k"] = pack_b(w[:, 0:1024]), pack_b(w[:, 1024:2048])
    o["moba_v"] = pack_a(w[:, 2048:3072])
    o["moba_o"] = pack_a(a["moba_w_o_2"][0])
    return {k: np.ascontiguousarray(v) for k, v in o.items()}


def kernel(**inputs):
    import concourse.bacc as bacc
    from concourse.bass_utils import run_bass_kernel_spmd

    nc = bacc.Bacc("TRN2", target_bir_lowering=False, num_devices=1)
    arrays = {f"in_{k}": v for k, v in layout(inputs).items()}
    D = {k[3:]: nc.dram_tensor(k, v.shape, mybir.dt.from_np(v.dtype), kind="ExternalInput").ap()
         for k, v in arrays.items()}
    out = nc.dram_tensor("out_0", (256, 1024), mybir.dt.float32, kind="ExternalOutput").ap()
    build(nc, D, out)
    r = run_bass_kernel_spmd(nc, [arrays], core_ids=[0])
    return r.results[0]["out_0"].reshape(1, 256, 1024)
```

```python
import numpy as np
import concourse.bass as bass
from concourse import mybir
from contextlib import ExitStack

BIG = 1e30
COLS = [("norm_in", 8), ("conv_w", 32), ("fconv_w", 132), ("fconv_b", 44), ("q_norm", 2), ("kv_norm", 2),
        ("mod_b", 96), ("c", 8), ("b_gate", 2), ("inv_freq", 1), ("sign", 1), ("nf", 8), ("ln", 64)]
CONSTS = [("ident", 128), ("ones", 256), ("cm", 256), ("cmT", 256)]


def spans(table):
    out, at = {}, 0
    for name, n in table:
        out[name] = (at, at + n)
        at += n
    return out, at


COL_AT, NCOL = spans(COLS)
CONST_AT, NCONST = spans(CONSTS)


LAG = 1
P0, P1, P2, P3, P4, P5 = 0, .5, .25, 0, 0, .0
SHARE = 0.5
RATE = 0.85


class Queue:

    def __init__(self, sem):
        self.sem, self.count, self.items, self.seen = sem, 0, [], {}

    def wait(self, tokens):
        for t in tokens:
            if t is None:
                continue
            if isinstance(t, list):
                self.wait(t)
                continue
            sem, value = t
            if self.seen.get(sem.name, 0) < value:
                self.seen[sem.name] = value
                self.items.append((None, (sem, value), None, None, 0))

    def op(self, tokens, fn, *args, **kw):
        self.wait(tokens)
        self.count += 1
        self.items.append((fn, args, kw, self.sem, 1))
        return self.sem, self.count

    def quiet(self, tokens, fn, *args, **kw):
        self.wait(tokens)
        self.items.append((fn, args, kw, None, 0))

    def dma(self, tokens, sem, value, fn, *args, **kw):
        self.wait(tokens)
        self.items.append((fn, args, kw, sem, 16))
        return sem, value

    def emit(self, eng):
        for fn, args, kw, sem, by in self.items:
            if fn is None:
                eng.wait_ge(*args)
            elif sem is None:
                fn(*args, **kw)
            else:
                fn(*args, **kw).then_inc(sem, by)


class Spot:

    def __init__(self, ap):
        self.ap, self.free = ap, []


class Turn:

    def __init__(self, aps):
        self.spots = [Spot(a) for a in aps]

    def add(self, ap, tokens):
        s = Spot(ap)
        s.free = tokens
        self.spots.insert(0, s)
        return s

    def get(self):
        s = next(x for x in self.spots if x.free is not None)
        self.spots.remove(s)
        self.spots.append(s)
        s.last, s.free = s.free, None
        return s


def build(nc, D, out):
    f32, f32r, i32 = mybir.dt.float32, mybir.dt.float32r, mybir.dt.int32
    ALU, ACT, AX = mybir.AluOpType, mybir.ActivationFunctionType, mybir.AxisListType
    MUL, ADD, SUB, MAX, MIN = ALU.mult, ALU.add, ALU.subtract, ALU.max, ALU.min
    ctx = ExitStack()
    with ctx:
        def sb(name, cols, dt=f32):
            return ctx.enter_context(nc.sbuf_tensor(name, [128, cols], dt))

        def sem(name):
            return ctx.enter_context(nc.semaphore(name))

        P, V, A, G, S = (Queue(sem(n)) for n in ("s_pe", "s_dve", "s_act", "s_pool", "s_sp"))
        ve, ac, po, pe = nc.vector, nc.scalar, nc.gpsimd, nc.tensor

        NR, NW = 5, 4
        ring_t = sb("ring", NR * 1024)
        raw = Turn([ring_t[:, i * 1024:(i + 1) * 1024] for i in range(NR)])
        for i, r_ in enumerate(raw.spots):
            r_.sem, r_.count = sem(f"s_w{i}"), 0

        def more_raw(ap, tokens):
            r_ = raw.add(ap, tokens)
            r_.sem, r_.count = sem(f"s_w{len(raw.spots) - 1}"), 0

        wsp = sb("wsp", NW * 2048, f32r)
        parts_ = Turn([wsp[:, i * 2048:(i + 1) * 2048] for i in range(NW)])

        def load(src, n=1024):
            s = raw.get()
            s.count += 16
            return s, S.dma(s.last, s.sem, s.count, nc.sync.dma_start, s.ap[:, 0:n], src)

        def rows(name, off, n):
            return load(bass.AP(D[name].tensor, off, [[0, 128], [1, n]]), n)

        class Stream:

            def __init__(self, plan):
                self.pool, self.turn = P0, 0.0
                self.plan, self.at, self.lows, self.ready, self.tasks, self.loads = plan, 0, 0, [], [], []

            def fetch(self):
                name, u, n = self.plan[len(self.ready) + len(self.loads)]
                self.loads.append(load(D[name][u][:, 0:n], n))

            def prepare(self):
                name, u, n = self.plan[len(self.ready)]
                if not self.loads:
                    self.fetch()
                r, tr = self.loads.pop(0)
                w = parts_.get()
                hi, lo = w.ap[:, 0:n], w.ap[:, 1024:1024 + n]
                th = A.op([tr, w.last], ac.copy, hi, r.ap[:, 0:n])
                self.ready.append([name, u, w, hi, lo, [th, tr], r, n])

            def low(self):
                name, u, w, hi, lo, toks, r, n = self.ready[self.lows]
                self.turn += self.pool
                if self.turn >= 1:
                    self.turn -= 1
                    tl = G.op(toks, po.tensor_tensor, lo, r.ap[:, 0:n], hi.bitcast(f32), SUB)
                else:
                    tl = V.op(toks, ve.tensor_tensor, lo, r.ap[:, 0:n], hi.bitcast(f32), SUB)
                r.free = [tl]
                toks[1] = tl
                self.lows += 1

            def next(self, name, u):
                while len(self.ready) < min(self.at + len(parts_.spots), len(self.plan)) and \
                        any(x.free is not None for x in parts_.spots):
                    self.prepare()
                    while len(self.ready) - self.lows > LAG:
                        self.low()
                while self.lows <= self.at:
                    self.low()
                got = self.ready[self.at]
                assert got[0:2] == [name, u], (got[0:2], name, u)
                self.at += 1
                return got[2:6]

            def done(self, w, last):
                w.free = [last]
                self.step(1.0)

            def step(self, share):
                for t in list(self.tasks):
                    t[2] += t[1] * share
                    while t[2] >= 1 and t in self.tasks:
                        t[2] -= 1
                        if next(t[0], 1) == 1:
                            self.tasks.remove(t)

            def beside(self, gen, rate):
                t = [gen, rate, 0.0]
                self.tasks.append(t)
                return t

            def finish(self, t):
                if t in self.tasks:
                    self.tasks.remove(t)
                for _ in t[0]:
                    self.step(SHARE)

        psum = Turn([ctx.enter_context(nc.psum_tensor(f"ps{i}", [128, 512], f32))[:, :] for i in range(8)])

        cst = sb("cst", NCONST)
        cols = sb("cols", NCOL)
        X = sb("X", 2048)[:, :].rearrange("p (t n) -> p t n", t=2)
        XTr = sb("XT", 4096, f32r)
        R2 = sb("R2", 2048)[:, :].rearrange("p (m n) -> p m n", m=2)
        acc = [sb(f"acc{i}", 1024)[:, :] for i in range(2)]
        small = sb("small", 512)
        AR_N, RA_N = 14864, 8192
        arena = sb("arena", AR_N)
        ra = sb("ra", RA_N, f32r)
        wk = Turn([sb(f"wk{i}", 512)[:, :] for i in range(3)])
        pb = Turn([sb(f"pb{i}", 256)[:, :] for i in range(4)])
        pt = Turn([sb(f"pt{i}", 256)[:, :] for i in range(3)])
        posi = sb("posi", 258, i32)
        gscr = nc.dram_tensor("gscr", [8, 128, 383], f32, kind="Internal").ap()

        def C(name, a=0, b=None):
            lo, hi = CONST_AT[name]
            return cst[:, lo + a:(hi if b is None else lo + b)]

        def K(name, i=0, n=1):
            lo = COL_AT[name][0]
            return cols[:, lo + i:lo + i + n]

        at = [0]

        def take(n):
            at[0] += n
            assert at[0] <= AR_N, at[0]
            return arena[:, at[0] - n:at[0]]

        sm_at = [0]

        def tiny(n):
            sm_at[0] += n
            assert sm_at[0] <= 512
            return small[:, sm_at[0] - n:sm_at[0]]

        def grid(ap, k):
            return ap.rearrange("p (k n) -> p k n", k=k)

        class Parts:

            def __init__(self, t, off, n):
                self.hi = [t[:, off + k * 256:off + (k + 1) * 256] for k in range(n)]
                self.lo = [t[:, off + (n + k) * 256:off + (n + k + 1) * 256] for k in range(n)]
                self.hi2 = [t[:, off + k * 256:off + (k + 2) * 256] for k in range(0, n, 2)]
                self.lo2 = [t[:, off + (n + k) * 256:off + (n + k + 2) * 256] for k in range(0, n, 2)]
                self.dep = [None] * n

            def part(self, a, b):
                p = Parts.__new__(Parts)
                p.hi, p.lo, p.dep = self.hi[a:b], self.lo[a:b], self.dep[a:b]
                return p

        s_in = [sem(f"s_in{i}") for i in range(7)]
        s_rb = sem("s_rb")
        xsrc = D["x"].rearrange("(t p) n -> t p n", t=2)
        t_x = [S.dma([], s_in[2], 16, nc.sync.dma_start, X[:, 0, :], xsrc[0])]
        t_cst = S.dma([], s_in[0], 16, nc.sync.dma_start, cst[:, 0:384], D["consts"][:, 0:384])
        t_x.append(S.dma([], s_in[5], 16, nc.sync.dma_start, X[:, 1, :], xsrc[1]))
        t_cols = S.dma([], s_in[1], 16, nc.sync.dma_start, cols[:, :], D["cols"])
        relb = tiny(8)
        pT = grid(take(512), 2)
        ID = C("ident")
        ones = C("ones")

        units = []

        def plan(name, n, cols_=1024):
            units.extend((name, u, cols_) for u in range(n))

        plan("w_iq", 5)
        plan("w_g", 1, 128)
        plan("w_mqk", 8)
        plan("w_mv", 8)
        plan("w_aqk", 8)
        plan("w_av", 4)
        plan("w_az", 4)
        plan("w_moz", 16)
        plan("w_out", 6)
        plan("w_ple", 2)
        units.extend(("w_out", u, 1024) for u in range(6, 12))
        plan("w_gate", 8)
        plan("mla_c", 4)
        plan("mla_kr", 2)
        plan("mla_uv", 2)
        for g in range(2):
            units.extend([("mla_uk", g, 1024), ("mla_uq", 2 * g, 1024), ("mla_uq", 2 * g + 1, 1024)])
        plan("mla_o", 8)
        for i in range(2):
            if i == 1:
                plan("moba_v", 8)
                for h in range(0, 8, 2):
                    for n_ in ("q", "k"):
                        units.extend((f"moba_{n_}", h + e, 1024) for e in range(2))
                plan("moba_o", 8)
            for u in range(11):
                for n_ in ("a", "b"):
                    units.extend((f"ffn_{n_}{i}", 2 * u + e, 1024) for e in range(2))
                if u:
                    units.extend((f"ffn_o{i}", 2 * u - 2 + e, 1024) for e in range(2))
            units.extend((f"ffn_o{i}", 20 + e, 1024) for e in range(2))
        W = Stream(units)
        for _ in range(3):
            W.fetch()
        t_cst2 = S.dma([], s_in[6], 16, nc.sync.dma_start, cst[:, 384:NCONST], D["consts"][:, 384:NCONST])

        def mm(tokens, o, l, r, start, stop, mark=False, group=True):
            if mark:
                return P.op(tokens, pe.matmul, o, l, r, start=start, stop=stop)
            P.quiet(tokens, pe.matmul, o, l, r, start=start, stop=stop)

        def mm3(tokens, o, l, r, start, stop, mark=False):
            (lh, ll), (rh, rl) = l, r
            mm(tokens, o, lh, rh, start, False)
            mm([], o, lh, rl, False, False)
            return mm([], o, ll, rh, False, stop, mark)

        def proj_b(x, nk, name, first, blocks, evac, outer=False):
            per = 8 // nk
            if outer:
                got = [W.next(name, first + j) for j in range(2)]
                b = psum.get()
                for k in range(nk):
                    c = slice(k * 128, (k + 1) * 128)
                    for m in range(2):
                        w, hi, lo, tw = got[m]
                        last = mm3([tw, x.dep[k], b.last], b.ap[:, m * 256:(m + 1) * 256], (hi[:, c], lo[:, c]),
                                   (x.hi[k], x.lo[k]), k == 0 and m == 0, k == nk - 1 and m == 1, k == nk - 1)
                b.free = evac(0, 2, b, last)
                for m in range(2):
                    W.done(got[m][0], last)
            w = None
            for j in range(2 if outer else 0, blocks):
                if j % per == 0:
                    w, hi, lo, tw = W.next(name, first + j // per)
                if j % 2 == 0:
                    b = psum.get()
                m = j % 2
                for k in range(nk):
                    c = slice(((j % per) * nk + k) * 128, ((j % per) * nk + k + 1) * 128)
                    last = mm3([tw, x.dep[k], b.last], b.ap[:, m * 256:(m + 1) * 256], (hi[:, c], lo[:, c]),
                               (x.hi[k], x.lo[k]), k == 0, k == nk - 1, k == nk - 1)
                if m == 1 or j == blocks - 1:
                    b.free = evac(j - m, m + 1, b, last)
                if j % per == per - 1 or j == blocks - 1:
                    W.done(w, last)

        def proj_a(x, nk, name, first, blocks, evac, tail=False, before=None):
            nq = nk // 2
            for cb in range(blocks):
                bs = [psum.get(), psum.get()]
                q = 0
                while q < nq:
                    m = 2 if tail and cb == blocks - 1 and q == nq - 2 else 1
                    if before:
                        before(cb, q)
                    got = [W.next(name, first + cb * nq + q + e) for e in range(m)]
                    for t in range(2):
                        tc = slice(t * 128, (t + 1) * 128)
                        for e in range(m):
                            w, hi, lo, tw = got[e]
                            for k in range(2):
                                kg = 2 * (q + e) + k
                                c = slice(k * 512, (k + 1) * 512)
                                last = mm3([tw, x.dep[kg], bs[t].last], bs[t].ap, (x.hi[kg][:, tc], x.lo[kg][:, tc]),
                                           (hi[:, c], lo[:, c]), kg == 0, kg == nk - 1, k == 1)
                        if q + m == nq:
                            bs[t].free = evac(t, cb, bs[t], last)
                    q += m
                    for e in range(m):
                        W.done(got[e][0], last)

        def split(f, hi, lo, tokens, pool=False):
            t1 = A.op(tokens, ac.copy, hi, f)
            if pool:
                t2 = G.op([t1], po.tensor_tensor, lo, f, hi.bitcast(f32), SUB)
            else:
                t2 = V.op([t1], ve.tensor_tensor, lo, f, hi.bitcast(f32), SUB)
            return [t1, t2]

        def transposed(src, deps, dst, nk, scale=None, shift=None, need=None):
            def dep(t, k):
                return deps[t][k // 4] if isinstance(deps[t], dict) else deps[t]

            pending = []

            def low_part():
                k, s, t1 = pending.pop(0)
                if k == 4:
                    t2 = G.op([t1], po.tensor_tensor, dst.lo2[k // 2], s.ap, dst.hi2[k // 2].bitcast(f32), SUB)
                else:
                    t2 = V.op([t1], ve.tensor_tensor, dst.lo2[k // 2], s.ap, dst.hi2[k // 2].bitcast(f32), SUB)
                s.free = [t2]
                dst.dep[k] = dst.dep[k + 1] = [t1, t2]

            for k in range(0, nk, 2):
                b = psum.get()
                for i in range(2):
                    for t in range(2):
                        o = b.ap[:, i * 256 + t * 128:i * 256 + (t + 1) * 128]
                        if i == 1 and t == 1:
                            last = P.op([dep(t, k), b.last, t_cst], pe.transpose, o, src(t, k + i), ID)
                        else:
                            P.quiet([dep(t, k), b.last, t_cst], pe.transpose, o, src(t, k + i), ID)
                if scale is None:
                    d = split(b.ap, dst.hi2[k // 2], dst.lo2[k // 2], [last])
                    b.free = d
                    dst.dep[k] = dst.dep[k + 1] = d
                elif shift is None:
                    t1 = [A.op([last, need], ac.activation, dst.hi[k + i], b.ap[:, i * 256:(i + 1) * 256],
                               ACT.Copy, scale=scale(k + i)) for i in range(2)]
                    for i in range(2):
                        t2 = V.op([t1, need], ve.scalar_tensor_tensor, dst.lo[k + i], b.ap[:, i * 256:(i + 1) * 256],
                                  scale(k + i), dst.hi[k + i].bitcast(f32), MUL, SUB)
                        dst.dep[k + i] = [t1, t2]
                    b.free = [t2]
                else:
                    s = wk.get()
                    for i in range(2):
                        o, f = s.ap[:, i * 256:(i + 1) * 256], b.ap[:, i * 256:(i + 1) * 256]
                        if k == 6:
                            t1 = A.op([last, s.last, need], ac.activation, o, f, ACT.Identity, bias=shift(k + i),
                                      scale=scale(k + i))
                        else:
                            t1 = V.op([last, s.last, need], ve.tensor_scalar, o, f, scale(k + i), shift(k + i),
                                      MUL, ADD)
                    b.free = [t1]
                    t1 = A.op([t1], ac.copy, dst.hi2[k // 2], s.ap)
                    pending.append((k, s, t1))
                    if len(pending) > 1:
                        low_part()
            while pending:
                low_part()

        half_neg = tiny(8)
        t_hn = V.op([], ve.memset, half_neg, -0.5)

        def rsqrt(src, o, n, scale, eps, tokens):
            t = V.op(tokens, ve.tensor_scalar, o, src, scale, eps, MUL, ADD)
            return G.op([t, t_hn], po.tensor_tensor, o, o, half_neg[:, 0:n], ALU.pow)

        turn = [0]

        def copy(o, i, tokens):
            turn[0] += 1
            if turn[0] % 2:
                return V.op(tokens, ve.tensor_copy, o, i)
            return A.op(tokens, ac.copy, o, i)

        XT = Parts(XTr, 0, 8)

        qkT = grid(take(2048), 8)
        GTf = take(2048)
        GT = grid(GTf, 2)
        aqk = grid(take(2048), 8)
        azT = grid(take(1024), 4)
        iqT = grid(take(1024), 4)
        ikT = take(256)
        mv = take(2 * 4 * 258).rearrange("p (t h n) -> p t h n", t=2, h=4)
        avf = take(1024)
        av = grid(avf, 2)
        scr = take(2816)
        MX = Parts(ra, 0, 12)
        TB = grid(ra[:, 6144:8192], 8)

        sel, onehot = azT[0:4, 0:2, :].rearrange("p k n -> p (k n)"), av[0:32, 0, 0:384]

        ss = tiny(2)
        Y = GT
        dU = []
        for t in range(2):
            t1 = V.op([t_x[t]], ve.tensor_tensor, Y[:, t, :], X[:, t, :], X[:, t, :], MUL)
            t1 = V.op([t1], ve.tensor_reduce, ss[:, t:t + 1], Y[:, t, :], AX.X, ADD) if t == 1 else \
                A.op([t1], ac.activation, Y[:, t, :], Y[:, t, :], ACT.Copy, accum_out=ss[:, t:t + 1])
            t1 = rsqrt(ss[:, t:t + 1], ss[:, t:t + 1], 1, 1.0 / 1024, 1e-6, [t1])
            dU.append(V.op([t1], ve.tensor_scalar, Y[:, t, :], X[:, t, :], ss[:, t:t + 1], None, MUL))

        transposed(lambda t, k: Y[:, t, k * 128:(k + 1) * 128], dU, XT, 8, lambda k: K("norm_in", k), need=[t_cols])

        S.dma([], s_in[3], 16, nc.sync.dma_start, relb[0:32, :], D["rel_bias"])
        S.dma([], s_in[3], 32, nc.sync.dma_start, posi[:, 0:256],
              bass.AP(D["pos_r"].tensor, 0, [[0, 128], [1, 256]]))
        S.dma([], s_in[3], 48, nc.sync.dma_start, posi[:, 256:258], D["pos_c"])
        S.dma([], s_in[3], 64, nc.sync.dma_start, onehot, D["onehot"])
        S.dma([], s_in[3], 80, nc.sync.dma_start, sel, D["sel"])
        t_misc = S.dma([], s_in[3], 96, nc.sync.dma_start, pT, D["pT"].rearrange("(k p) n -> p k n", k=2))

        b = psum.get()
        last = mm([t_cst, t_cst2, t_misc, b.last], b.ap[0:8, 0:384], relb[0:32, :], onehot, True, True, True)
        grow = scr[0:8, 0:384]
        t = V.op([last], ve.tensor_copy, grow, b.ap[0:8, 0:384])
        b.free = [t]
        part = grow.ap[0][0]
        tg = G.dma([t], s_in[4], 16, nc.gpsimd.dma_start, gscr,
                   bass.AP(grow.tensor, grow.offset, [[part, 8], [0, 128], [1, 383]]))
        t_TB = G.dma([tg], s_rb, 16, nc.gpsimd.dma_start, TB.bitcast(f32),
                     bass.AP(gscr.tensor, 127, [[382, 128], [128 * 383, 8], [1, 256]]))

        cact = tiny(8)
        cc_ = K("c", 0, 8)
        ct = A.op([t_cols], ac.activation, cact, cc_, ACT.Tanh, scale=0.5)
        ct = V.op([ct], ve.scalar_tensor_tensor, cact, cact, 1.0, cc_, ADD, MUL)
        ct = V.op([ct], ve.tensor_scalar, cact, cact, 0.5, None, MUL)
        t_mod = {}
        MCi = [[tiny(32), tiny(16)], [tiny(32), tiny(16)]]

        r2_used = {}
        ones_r = sb("ones_r", 128, f32r)
        mr = sb("mr", 1024, f32r)
        t_or = A.op([t_cst], ac.copy, ones_r[:, :], ones[:, 0:128])

        def modulation():
            done, mr_free = [], []
            for i in range(2):
                mc, ab = MCi[i]
                for m in range(6):
                    pa = pp_ = None
                    for k in range(8):
                        w, tw = load(D["mod_w"][(i * 6 + m) * 8 + k])
                        if k % 2 == 0:
                            if k == 0:
                                pa = V.op([tw, ct, done], ve.tensor_scalar, acc[0], w.ap, cact[:, k:k + 1], None, MUL)
                            else:
                                pa = V.op([tw, pa], ve.scalar_tensor_tensor, acc[0], w.ap, cact[:, k:k + 1], acc[0],
                                          MUL, ADD)
                            w.free = [pa]
                        elif k == 1:
                            pp_ = A.op([tw, ct, done], ac.activation, acc[1], w.ap, ACT.Copy, scale=cact[:, k:k + 1])
                            w.free = [pp_]
                        else:
                            t1 = A.op([tw, ct], ac.activation, w.ap, w.ap, ACT.Copy, scale=cact[:, k:k + 1])
                            pp_ = G.op([t1, pp_], po.tensor_tensor, acc[1], acc[1], w.ap, ADD)
                            w.free = [pp_]
                        yield
                    t0 = G.op([pa, pp_], po.tensor_tensor, acc[0], acc[0], acc[1], ADD)
                    yield
                    row = m in (2, 5)
                    r = 0 if m == 2 else 1
                    while i and row and r not in r2_used:
                        yield
                    x = {0: 0, 1: 8, 3: 16, 4: 24}.get(m)
                    if row:
                        br, tb = rows("mod_b", i * 6144 + m * 1024, 1024)
                    for cb in range(2):
                        cs = slice(cb * 512, (cb + 1) * 512)
                        t1 = A.op([t0, mr_free], ac.copy, mr[:, 0:512], acc[0][:, cs])
                        yield
                        t2 = V.op([t1], ve.tensor_tensor, mr[:, 512:1024], acc[0][:, cs], mr[:, 0:512].bitcast(f32),
                                  SUB)
                        done = [t2]
                        yield
                        b = psum.get()
                        if row:
                            mm([t2, t_or, b.last], b.ap, ones_r[:, :], mr[:, 0:512], True, False)
                            last = mm([], b.ap, ones_r[:, :], mr[:, 512:1024], False, True, True)
                            t = V.op([last, tb, r2_used.get(r) if i else None], ve.tensor_tensor, R2[:, r, cs],
                                     b.ap, br.ap[:, cs], ADD)
                        else:
                            for k in range(4):
                                o = b.ap[:, 2 * k:2 * k + 2]
                                mm([t2, t_or, b.last], o, mr[:, k * 128:(k + 1) * 128], ones_r[:, 0:2], True, False)
                                last = mm([], o, mr[:, 512 + k * 128:640 + k * 128], ones_r[:, 0:2], False, True,
                                          k == 3)
                            y = x + cb * 4
                            t = V.op([last, t_cols], ve.tensor_tensor, mc[:, y:y + 4],
                                     b.ap[:, 0:8].rearrange("p (k n) -> p k n", n=2)[:, :, 0],
                                     K("mod_b", i * 48 + m * 8 + cb * 4, 4), ADD)
                        b.free = [t]
                        mr_free = [last]
                    if row:
                        br.free = [t]
                        t_mod[i, m] = [t]
                    elif m in (1, 4):
                        n = 2 * i - 1 + (m == 4)
                        a_, s_ = mc[:, x:x + 8], mc[:, x - 8:x]
                        t = V.op([t], ve.tensor_scalar, a_, a_, 1.0, None, ADD)
                        if n >= 0:
                            g_, b_ = K("ln", n * 16, 8), K("ln", n * 16 + 8, 8)
                            o_ = ab[:, 0:8] if m == 1 else ab[:, 8:16]
                            t = V.op([t], ve.tensor_tensor, o_, a_, b_, MUL)
                            t = V.op([t], ve.tensor_tensor, s_, s_, o_, ADD)
                        else:
                            g_ = K("nf", 0, 8)
                        t = V.op([t], ve.tensor_tensor, a_, a_, g_, MUL)
                        t_mod[i, m] = [t]
                    yield

        mod = W.beside(modulation(), RATE)

        def until(key):
            while key not in t_mod:
                next(mod[0])
            return t_mod[key]

        d_b1 = {}

        def ev_iq(j, n, b, last):
            if j < 4:
                t = A.op([last], ac.activation, iqT[:, j:j + 2, :], grid(b.ap, 2), ACT.Copy)
                d_b1["iq", j] = d_b1["iq", j + 1] = t
            else:
                t = A.op([last], ac.activation, ikT, b.ap[:, 0:256], ACT.Copy)
                d_b1["ik"] = t
            return [t]

        proj_b(XT, 8, "w_iq", 0, 5, ev_iq, True)

        w, hi, lo, tw = W.next("w_g", 0)
        bw = psum.get()
        for t in range(2):
            tc = slice(t * 128, (t + 1) * 128)
            for k in range(8):
                c = slice(k * 16, (k + 1) * 16)
                last = mm3([tw, XT.dep[k], bw.last], bw.ap[:, t * 16:(t + 1) * 16], (XT.hi[k][:, tc], XT.lo[k][:, tc]),
                           (hi[:, c], lo[:, c]), k == 0, k == 7, k == 7)
        W.done(w, last)
        iw, gw = tiny(32), tiny(32)
        t_iw = V.op([last], ve.tensor_scalar, iw, bw.ap[:, 0:32], 8.0 ** -0.5, None, MUL)
        t_gw = V.op([last], ve.tensor_copy, gw, bw.ap[:, 0:32])
        bw.free = [t_gw]

        srow = scr[0:4, 1536:2816]
        ARr, FS, BC, MR, NM = (srow[:, i * 256:(i + 1) * 256] for i in range(5))
        bi = psum.get()
        bf = psum.get()
        for t in range(2):
            tc = slice(t * 128, (t + 1) * 128)
            l1 = mm([t_gw, bi.last, t_cst], bi.ap[0:4, tc], gw[:, t * 16:t * 16 + 4], ID, True, True, t == 1)
        for t in range(2):
            tc = slice(t * 128, (t + 1) * 128)
            l2 = mm([bf.last], bf.ap[0:4, tc], gw[:, t * 16 + 4:t * 16 + 8], ID, True, True, t == 1)
        t_li = V.op([l1, t_cols], ve.tensor_scalar, ARr, bi.ap[0:4, 0:256], K("b_gate", 0)[0:4, :], None, ADD)
        bi.free = [t_li]
        t_fs = V.op([l2], ve.tensor_scalar, FS, bf.ap[0:4, 0:256], K("b_gate", 1)[0:4, :], None, ADD)
        bf.free = [t_fs]
        t = V.op([t_fs], ve.scalar_tensor_tensor, BC, FS, -1.0, FS, MUL, MAX)
        t = A.op([t], ac.activation, BC, BC, ACT.Exp, scale=-1.0)
        t = V.op([t], ve.tensor_scalar, BC, BC, 1.0, None, ADD)
        t = A.op([t], ac.activation, BC, BC, ACT.Ln)
        t2 = V.op([t_fs], ve.tensor_scalar, FS, FS, 0.0, None, MIN)
        t = V.op([t, t2], ve.tensor_tensor, FS, FS, BC, SUB)
        t_bc = V.op([t, t_cst], ve.tensor_tensor_scan, BC, ones[0:4, 0:256], FS, 0.0, MUL, ADD)
        t_ar = V.op([t_bc], ve.tensor_tensor, ARr, ARr, BC, SUB)
        t_mr = V.op([t_ar], ve.tensor_tensor_scan, MR, ARr, ARr, 0.0, MAX, MAX)
        t_nm = V.op([t_mr], ve.tensor_scalar, NM, MR, -1.0, None, MUL)
        t_bm = V.op([t_nm], ve.tensor_tensor, MR, MR, BC, ADD)
        em, acol = tiny(8), tiny(8)

        def gate_columns():
            b = psum.get()
            for t in range(2):
                P.quiet([t_bm, b.last, t_cst], pe.transpose, b.ap[:, t * 4:t * 4 + 4],
                        MR[:, t * 128:(t + 1) * 128], ID[0:4, 0:4])
                last = P.op([t_ar], pe.transpose, b.ap[:, 8 + t * 4:12 + t * 4],
                            ARr[:, t * 128:(t + 1) * 128], ID[0:4, 0:4])
            t_em = A.op([last], ac.activation, em, b.ap[:, 0:8], ACT.Exp, scale=-1.0)
            t_ac = V.op([t_em], ve.tensor_copy, acol, b.ap[:, 8:16])
            b.free = [t_ac]
            return t_em, t_ac

        wsel = [None, None]
        t_sel = [None, None]

        def indexer():
            for t in range(2):
                n = 128 * (t + 1)
                sc = [scr[:, (2 * t + q) * 256:(2 * t + q) * 256 + 256] for q in range(2)]
                prev = None
                for hs in ((0, 2), (1, 3), (4, 6), (5, 7)):
                    b = psum.get()
                    for e, h in enumerate(hs):
                        r = slice(64 * (h % 2), 64 * (h % 2) + 64)
                        last = mm([d_b1["iq", h // 2], d_b1["ik"], b.last], b.ap[:, e * n:(e + 1) * n],
                                  iqT[r, h // 2, t * 128:(t + 1) * 128], ikT[r, 0:n], True, True, e == 1)
                    s = wk.get()
                    t1 = A.op([last, s.last], ac.activation, s.ap[:, 0:2 * n], b.ap[:, 0:2 * n], ACT.Relu,
                              scale=0.125)
                    b.free = [t1]
                    for e, h in enumerate(hs):
                        prev = V.op([t1, t_iw, prev, t_cst2, tg], ve.scalar_tensor_tensor, sc[0][:, 0:n],
                                    s.ap[:, e * n:(e + 1) * n], iw[:, t * 16 + 8 + h:t * 16 + 9 + h],
                                    C("cm", 256 - n, 256) if h == 0 else sc[0][:, 0:n], MUL, ADD)
                    s.free = [prev]
                    yield
                m8 = tiny(16)
                for i in range(8):
                    q = m8[:, (i % 2) * 8:(i % 2) * 8 + 8]
                    t1 = V.op([prev], ve.max, q, sc[i % 2][:, 0:n])
                    prev = V.op([t1], ve.match_replace, sc[(i + 1) % 2][:, 0:n], q, sc[i % 2][:, 0:n], -3e38)
                    if i % 2:
                        yield
                t1 = V.op([prev], ve.tensor_scalar, sc[1][:, 0:n], sc[0][:, 0:n], -2e38, -BIG, ALU.is_ge, MUL)
                t_sel[t] = V.op([t1, t_cst2], ve.tensor_tensor, sc[1][:, 0:n], sc[1][:, 0:n],
                                C("cm", 256 - n, 256), ADD)
                wsel[t] = sc[1]
                yield

        idx = W.beside(indexer(), 1.0)

        def conv(o, b, k, tokens):
            t = tokens
            for j in (2, 1, 0):
                s = 3 - j
                t = V.op([t], ve.scalar_tensor_tensor, o[:, s:256], b[:, 0:256 - s], K("conv_w", j * 8 + k),
                         o[:, s:256], MUL, ADD)
            return t

        def ev_mqk(j, n, b, last):
            fr = []
            s, th = wk.get(), wk.get()
            t0 = [A.op([last, s.last, t_cols], ac.activation, s.ap[:, i * 256:(i + 1) * 256],
                       b.ap[:, i * 256:(i + 1) * 256], ACT.Copy, scale=K("conv_w", 24 + j + i)) for i in range(n)]
            for i in range(n):
                fr.append(conv(s.ap[:, i * 256:(i + 1) * 256], b.ap[:, i * 256:(i + 1) * 256], j + i,
                               t0))
            t = A.op([fr, th.last], ac.activation, th.ap, s.ap, ACT.Tanh, scale=0.5)
            t = V.op([t, fr, dXT], ve.scalar_tensor_tensor, qkT[:, j:j + 2, :], grid(th.ap, 2), 1.0, grid(s.ap, 2),
                     ADD, MUL)
            s.free = th.free = [t]
            d_b1["qk", j] = d_b1["qk", j + 1] = t
            return fr

        dXT = [XT.dep[k] for k in range(8)]
        W.pool = P1
        proj_b(XT, 8, "w_mqk", 0, 8, ev_mqk)
        W.pool = P2
        d_mv, d_av, d_g = {}, {}, {}
        t_one = [G.op([], po.memset, mv[:, t, :, 256:257], 1.0) for t in range(2)]

        def ev_mv(t, cb, b, last):
            t1 = copy(mv[:, t, 2 * cb:2 * cb + 2, 0:256], b.ap.rearrange("p (h n) -> p h n", h=2), [last])
            d_mv[t, 2 * cb] = d_mv[t, 2 * cb + 1] = t1
            return [t1]

        proj_a(XT, 8, "w_mv", 0, 2, ev_mv)
        W.finish(idx)

        hss = tiny(8)
        rdn = tiny(8)
        d_h = {}
        hm = qkT

        def mlstm():
            t_em, t_ac = gate_columns()
            yield
            for h in range(4):
                ST = []
                for j in range(2):
                    n = 256 - 128 * j
                    b = psum.get()
                    mm([t_nm, t_misc, b.last], b.ap[:, 0:n], sel[:, h * 128:h * 128 + 128],
                       NM[:, j * 128:256], True, True)
                    last = mm([d_b1["qk", 4 + h], d_b1["qk", h]], b.ap[:, 256:256 + n],
                              qkT[:, 4 + h, j * 128:(j + 1) * 128], qkT[:, h, j * 128:256], True, True, True)
                    s = pb.get()
                    e = s.ap[:, 0:n]
                    t1 = V.op([last, t_ac, s.last], ve.scalar_tensor_tensor, e, b.ap[:, 0:n],
                              acol[:, j * 4 + h:j * 4 + h + 1], C("cmT", 0, n), ADD, ADD)
                    t1 = A.op([t1], ac.activation, e, e, ACT.Exp)
                    t1 = V.op([t1], ve.scalar_tensor_tensor, e, b.ap[:, 256:256 + n], 0.25 * 128.0 ** -0.5, e,
                              MUL, MUL)
                    b.free = [t1]
                    ST.append((s, t1))
                    yield
                for t in range(2):
                    b = psum.get()
                    for j in range(t + 1):
                        c = (t - j) * 128
                        last = mm([ST[j][1], d_mv[j, h], t_one, b.last], b.ap[:, 0:257], ST[j][0].ap[:, c:c + 128],
                                  mv[:, j, h, 0:257], j == 0, j == t, j == t)
                    i = t * 4 + h
                    t1 = V.op([last, t_em], ve.tensor_scalar, rdn[:, i:i + 1], b.ap[:, 256:257], -1.0, None, MUL)
                    t1 = V.op([t1], ve.scalar_tensor_tensor, rdn[:, i:i + 1], b.ap[:, 256:257], em[:, i:i + 1],
                              rdn[:, i:i + 1], MAX, MAX)
                    t1 = V.op([t1], ve.reciprocal, rdn[:, i:i + 1], rdn[:, i:i + 1])
                    o = hm[:, t * 4 + h, :]
                    t1 = A.op([t1], ac.activation, o, b.ap[:, 0:256], ACT.Copy, scale=rdn[:, i:i + 1])
                    b.free = [t1]
                    s = pt.get()
                    d_h[i] = A.op([t1, s.last], ac.activation, s.ap, o, ACT.Square, accum_out=hss[:, i:i + 1])
                    s.free = [d_h[i]]
                for s, _ in ST:
                    s.free = [last]
                lstm_end[:] = [last]
                yield

        lstm_end = []
        lstm = W.beside(mlstm(), 1.05)

        def ev_aqk(j, n, b, last):
            t = A.op([last], ac.activation, aqk[:, j:j + 2, :], grid(b.ap, 2), ACT.Copy,
                     scale=0.125 if j < 4 else 1.0)
            d_b1["aqk", j] = d_b1["aqk", j + 1] = t
            return [t]

        proj_b(XT, 8, "w_aqk", 0, 8, ev_aqk)

        def ev_av(t, cb, b, last):
            d_av[t] = copy(av[:, t, :], b.ap, [last])
            return [d_av[t]]

        proj_a(XT, 8, "w_av", 0, 1, ev_av)
        W.finish(lstm)
        mvf = mv.rearrange("p t h n -> p (t h n)")
        for i in range(2):
            more_raw(mvf[:, i * 1024:(i + 1) * 1024], [lstm_end])

        def ev_az(j, n, b, last):
            o = azT[:, j:j + 2, :]
            t = A.op([last], ac.activation, o, grid(b.ap, 2), ACT.Tanh, scale=0.5)
            t = V.op([t], ve.scalar_tensor_tensor, o, o, 1.0, grid(b.ap, 2), ADD, MUL)
            d_b1["az", j] = d_b1["az", j + 1] = t
            return [t]

        nmx, smx = tiny(16), tiny(16)

        def attention(score, add_bias, value, dh, finish, may=lambda h: True, lag=3):
            items = [(h, t) for h in range(8) for t in range(2)]
            Ps, PTs, outs = {}, {}, {}

            def first(i):
                h, t = items[i]
                n = 128 * (t + 1)
                b = psum.get()
                last = score(h, t, n, b)
                s = pb.get()
                p = s.ap[:, 0:n]
                t1 = add_bias(h, t, n, b, p, [last, s.last])
                b.free = [t1]
                t2 = V.op([t1], ve.tensor_reduce, nmx[:, i:i + 1], p, AX.X, MAX, negate=True)
                t3 = A.op([t2], ac.activation, p, p, ACT.Exp, bias=nmx[:, i:i + 1], accum_out=smx[:, i:i + 1])
                Ps[i] = s, t3

            def norm(i):
                s, t3 = Ps[i]
                p = s.ap[:, 0:128 * (items[i][1] + 1)]
                t4 = V.op([t3], ve.reciprocal, smx[:, i:i + 1], smx[:, i:i + 1])
                t5 = V.op([t4], ve.tensor_scalar, p, p, smx[:, i:i + 1], None, MUL)
                Ps[i] = s, t5

            def second(i):
                h, t = items[i]
                s, tk = Ps[i]
                b = psum.get()
                for j in range(t + 1):
                    last = P.op([tk, b.last], pe.transpose, b.ap[:, j * 128:(j + 1) * 128],
                                s.ap[:, j * 128:(j + 1) * 128], ID)
                s.free = [last]
                d = pt.get()
                t1 = A.op([last, d.last], ac.copy, d.ap[:, 0:128 * (t + 1)], b.ap[:, 0:128 * (t + 1)])
                b.free = [t1]
                PTs[i] = d, t1

            def third(i):
                h, t = items[i]
                d, tk = PTs[i]
                per = 128 // dh
                if t == 0 and h % per == 0:
                    outs["b"] = psum.get()
                b = outs["b"]
                r0 = (h % per) * dh
                for j in range(t + 1):
                    vt, l = value(j, h)
                    last = mm([tk, vt, b.last], b.ap[r0:r0 + dh, t * 128:(t + 1) * 128], l,
                              d.ap[:, j * 128:(j + 1) * 128], j == 0, j == t, j == t)
                d.free = [last]
                if t == 1 and h % per == per - 1:
                    b.free = finish(h // per, b, last)

            n = len(items)
            for i in range(n + lag + 2):
                if i < n:
                    while not may(items[i][0]):
                        yield
                    first(i)
                if 0 <= i - 1 < n:
                    norm(i - 1)
                if 0 <= i - lag < n:
                    second(i - lag)
                if 0 <= i - lag - 2 < n:
                    third(i - lag - 2)
                yield

        def score1(h, t, n, b):
            r = slice(64 * (h % 2), 64 * (h % 2) + 64)
            return mm([d_b1["aqk", h // 2], d_b1["aqk", 4 + h // 2], b.last], b.ap[:, 0:n],
                      aqk[r, h // 2, t * 128:(t + 1) * 128], aqk[r, 4 + h // 2, 0:n], True, True, True)

        bmt = Turn([scr[:, 1024 + q * 256:1280 + q * 256] for q in range(2)])

        def bias1(h, t, n, b, p, toks_):
            s = bmt.get()
            t1 = G.op([t_TB, t_sel[t], s.last], po.tensor_tensor, s.ap[:, 0:n], TB[:, h, 256 - n:256].bitcast(f32),
                      wsel[t][:, 0:n], ADD)
            t2 = V.op([t1, toks_], ve.tensor_tensor, p, b.ap[:, 0:n], s.ap[:, 0:n], ADD)
            s.free = [t2]
            return t2

        def fin1(k, b, last):
            s = wk.get()
            f = s.ap[:, 0:256]
            t1 = V.op([last, d_b1["az", k], s.last], ve.scalar_tensor_tensor, f, b.ap[:, 0:256], 0.5, azT[:, k, :],
                      MUL, MUL)
            MX.dep[8 + k] = split(f, MX.hi[8 + k], MX.lo[8 + k], [t1])
            s.free = [MX.dep[8 + k][1]]
            return [t1]

        proj_b(XT, 8, "w_az", 0, 4, ev_az)
        dsa = W.beside(attention(score1, bias1, lambda j, h: (d_av[j], av[:, j, h * 64:(h + 1) * 64]), 64, fin1), 1.4)

        def ev_moz(t, cb, b, last):
            c, z = cb // 2, cb % 2
            g = GT[:, t, c * 512:(c + 1) * 512]
            if not z:
                d_g[t, c] = A.op([last, dXT], ac.activation, g, b.ap, ACT.Tanh, scale=0.5)
                return [d_g[t, c]]
            if t == 0:
                mns[c] = rows("m_norm", c * 512, 512)
            mn, tmn = mns[c]
            s = wk.get()
            t1 = A.op([last, s.last], ac.activation, s.ap, b.ap, ACT.Tanh, scale=0.5)
            t2 = V.op([t1], ve.scalar_tensor_tensor, s.ap, s.ap, 1.0, b.ap, ADD, MUL)
            t3 = V.op([t2, d_g[t, c]], ve.scalar_tensor_tensor, g, g, 1.0, s.ap, ADD, MUL)
            s.free = [t3]
            t4 = V.op([t3, tmn], ve.tensor_tensor, g, g, mn.ap[:, 0:512], MUL)
            if t == 1:
                mn.free = [t4]
            d_g[t, c] = t4
            return [t2]

        mns = {}
        t_r = rsqrt(hss, hss, 8, 16.0 / 256, 16e-6, [d_h[i] for i in range(8)])
        proj_a(XT, 8, "w_moz", 0, 2, ev_moz)

        def gated(c):
            for t in range(2):
                for h in (2 * c, 2 * c + 1):
                    o = hm[:, t * 4 + h, :]
                    d = V.op([t_r, d_g[t, c]], ve.scalar_tensor_tensor, o, o, hss[:, t * 4 + h:t * 4 + h + 1],
                             GT[:, t, h * 256:(h + 1) * 256], MUL, MUL)
                d_hm[t] = d
            m = MX.part(4 * c, 4 * c + 4)
            m.hi2, m.lo2 = MX.hi2[2 * c:2 * c + 2], MX.lo2[2 * c:2 * c + 2]
            transposed(lambda t, k: hm[:, t * 4 + 2 * c + k // 2, (k % 2) * 128:(k % 2) * 128 + 128], d_hm, m, 4)
            MX.dep[4 * c:4 * c + 4] = m.dep

        d_hm = [None, None]
        gated(0)
        proj_a(XT, 8, "w_moz", 8, 2, lambda t, cb, b, l: ev_moz(t, 2 + cb, b, l))
        d_r = [{}, {}]

        def ev_wo(t, cb, b, last):
            o = X[:, t, cb * 512:(cb + 1) * 512]
            d_r[t][cb] = V.op([last, dU], ve.tensor_tensor, o, o, b.ap, ADD)
            return [d_r[t][cb]]

        def before_out(cb, q):
            if q == 2:
                gated(1)
                W.finish(dsa)

        proj_a(MX, 12, "w_out", 0, 1, ev_wo, False, before_out)
        PT2 = Parts(ra, 6144, 2)
        d = split(pT.rearrange("p k n -> p (k n)"), PT2.hi2[0], PT2.lo2[0], [t_misc, MX.dep[8:12]])
        PT2.dep = [d, d]
        pl = {}
        PL = aqk.rearrange("p k n -> p (k n)").rearrange("p (t n) -> p t n", t=2)

        ple_end = []

        def ev_ple(t, cb, b, last):
            o = PL[:, t, cb * 512:(cb + 1) * 512]
            t1 = A.op([last, MX.dep[8:12]], ac.copy, o, b.ap)
            pl[t, cb] = t1
            ple_end[:] = [last]
            return [t1]

        proj_a(PT2, 2, "w_ple", 0, 2, ev_ple)
        cosT, sinT, posf = scr[:, 0:256], scr[:, 256:512], scr[:, 512:770]
        dist = grid(scr[:, 770:1282], 2)
        t_pf = V.op([t_misc, MX.dep[8:12]], ve.tensor_copy, posf, posi[:, 0:258])
        a1 = wk.get()
        ang, kk_ = a1.ap[:, 0:256], a1.ap[:, 256:512]
        TWO_PI = 6.283185307179586
        C1 = 6.28125
        C2 = round((TWO_PI - C1) * 2 ** 21) / 2 ** 21
        C3 = TWO_PI - C1 - C2
        MAGIC = 12582912.0
        t_ang = V.op([t_pf, a1.last], ve.tensor_scalar, ang, posf[:, 0:256], K("inv_freq"), None, MUL)
        t_tab = []
        for tab, quarter in ((sinT, 0.0), (cosT, 0.25)):
            t1 = V.op([t_ang, t_tab[-1:]], ve.tensor_scalar, kk_, ang, 1.0 / TWO_PI, quarter, MUL, ADD)
            t1 = V.op([t1], ve.tensor_scalar, kk_, kk_, MAGIC, None, ADD)
            t1 = V.op([t1], ve.tensor_scalar, kk_, kk_, -MAGIC, None, ADD)
            src = ang
            for cc in (C1, C2, C3):
                t1 = V.op([t1], ve.scalar_tensor_tensor, tab, kk_, -cc, src, MUL, ADD)
                src = tab
            t3 = t1
            if quarter:
                t1 = V.op([t1], ve.tensor_scalar, tab, tab, TWO_PI / 4, None, ADD)
            t1 = V.op([t1], ve.tensor_scalar, tab, tab, 3.1415925, -3.1415925, MIN, MAX)
            t1 = A.op([t1], ac.activation, tab, tab, ACT.Sin)
            if not quarter:
                t1 = V.op([t1, t_cols], ve.tensor_scalar, tab, tab, K("sign"), None, MUL)
            t_tab.append(t1)
        a1.free = [t3]
        for t in range(2):
            t1 = V.op([t_pf], ve.tensor_scalar, dist[:, t, :], posf[:, 0:256], posf[:, 256 + t:257 + t], None, SUB)
            t1 = V.op([t1], ve.scalar_tensor_tensor, dist[:, t, :], dist[:, t, :], -1.0, dist[:, t, :], MUL, MAX)
            n = 128 * (t + 1)
            t_dist = V.op([t1], ve.tensor_tensor, dist[:, t, 0:n], dist[:, t, 0:n], C("cm", 256 - n, 256), SUB)

        proj_a(MX, 12, "w_out", 6, 1, lambda t, cb, b, l: ev_wo(t, 1, b, l), True)
        transposed(lambda t, k: X[:, t, k * 128:(k + 1) * 128], d_r, XT, 8)
        d_x1 = [[None, None], [None, None]]

        def ev_gate(t, cb, b, last):
            s = wk.get()
            t1 = A.op([last, s.last], ac.activation, s.ap, b.ap, ACT.Tanh, scale=0.5)
            t2 = V.op([t1, pl[t, cb]], ve.scalar_tensor_tensor, s.ap, s.ap, 1.0, PL[:, t, cb * 512:(cb + 1) * 512],
                      ADD, MUL)
            o = X[:, t, cb * 512:(cb + 1) * 512]
            t3 = V.op([t2, XT.dep], ve.scalar_tensor_tensor, o, s.ap, 0.5, o, MUL, ADD)
            s.free = [t3]
            fq = wk.get()
            d_x1[t][cb] = A.op([t3, fq.last], ac.activation, fq.ap, o, ACT.Square,
                               accum_out=fs[:, 2 * t + cb:2 * t + cb + 1])
            fq.free = [d_x1[t][cb]]
            return [t1]

        fs = tiny(4)
        proj_a(XT, 8, "w_gate", 0, 2, ev_gate, True)
        d_x = []
        for t in range(2):
            t1 = V.op([d_x1[t]], ve.tensor_tensor, fs[:, 2 * t:2 * t + 1], fs[:, 2 * t:2 * t + 1],
                      fs[:, 2 * t + 1:2 * t + 2], ADD)
            t1 = rsqrt(fs[:, 2 * t:2 * t + 1], fs[:, 2 * t:2 * t + 1], 1, 1.0 / 1024, 1e-6, [t1])
            d_x.append(V.op([t1], ve.tensor_scalar, X[:, t, :], X[:, t, :], fs[:, 2 * t:2 * t + 1], None, MUL))

        more_raw(avf[:, 0:1024], [MX.dep[8:12]])
        parts_.add(ra[:, 6144:8192], [ple_end])
        W.pool = P3
        ALPHA = 4.0 ** 0.25
        st = tiny(24)
        mv2 = tiny(8)

        def modulated(i, which, deps):
            m = MCi[i][0]
            a, s_ = (8, 0) if which == 0 else (24, 16)
            transposed(lambda t, k: X[:, t, k * 128:(k + 1) * 128], deps, XT, 8,
                       lambda k: m[:, a + k:a + k + 1], lambda k: m[:, s_ + k:s_ + k + 1], [until((i, 1 if which == 0 else 4))])

        d_g2 = [None, None]

        def gain(name, off, bias):
            dep = XT.dep
            for n in range(1 + bias):
                g, tg_ = rows(name, off + n * 1024, 1024)
                d_g2[0] = V.op([dep, d_g2[0], tg_], ve.tensor_tensor, X[:, 0, :], X[:, 0, :], g.ap, ADD if n else MUL)
                d_g2[1] = G.op([dep, d_g2[1], tg_], po.tensor_tensor, X[:, 1, :], X[:, 1, :], g.ap, ADD if n else MUL)
                g.free = [d_g2[0], d_g2[1]]
                yield
                yield

        d_z = [[None, None], [None, None]]

        def resid(r, i, t, cb, b, last):
            W.finish(gn)
            cs = slice(cb * 512, (cb + 1) * 512)
            s = wk.get()
            t1 = V.op([last, until((i, 5 if r else 2)), s.last], ve.tensor_tensor, s.ap, b.ap, R2[:, r, cs], MUL)
            if i == 0 and t == 1 and cb == 1:
                r2_used[r] = [t1]
            t2 = V.op([t1, d_g2[t]], ve.scalar_tensor_tensor, X[:, t, cs], X[:, t, cs], ALPHA, s.ap, MUL, ADD)
            s.free = [t2]
            d_z[t][cb] = V.op([t2], ve.bn_stats, st[:, (2 * t + cb) * 6:(2 * t + cb) * 6 + 6], X[:, t, cs])
            return [t1]

        def layer_norm():
            out_t = []
            for t in range(2):
                m = mv2[:, t * 4:t * 4 + 4]
                t1 = V.op([d_z[t]], ve.bn_aggr, m[:, 0:2],
                          st[:, t * 12:(t + 1) * 12].rearrange("p (c s) -> p c s", c=2))
                t1 = rsqrt(m[:, 1:2], m[:, 2:3], 1, 1.0, 1e-5, [t1])
                t2 = V.op([t1], ve.tensor_scalar, m[:, 3:4], m[:, 0:1], m[:, 2:3], -1.0, MUL, MUL)
                t3 = V.op([t2], ve.tensor_scalar, X[:, t, 0:512], X[:, t, 0:512], m[:, 2:3], m[:, 3:4], MUL, ADD)
                t4 = A.op([t2], ac.activation, X[:, t, 512:1024], X[:, t, 512:1024], ACT.Identity, bias=m[:, 3:4],
                          scale=m[:, 2:3])
                out_t.append({0: t3, 1: t4})
            return out_t

        gp = Turn([ra[:, q * 1024:(q + 1) * 1024] for q in range(3)])

        def ffn(i):
            outs = [[psum.get() for _ in range(2)] for _ in range(2)]
            held = []

            def second(u, last_one):
                g, dg = held.pop(0)
                if last_one:
                    got = [W.next(f"ffn_o{i}", 2 * u + e) for e in range(2)]
                for t, e in ((0, 0), (0, 1), (1, 0), (1, 1)) if last_one else ((0, 0), (1, 0), (0, 1), (1, 1)):
                    if last_one:
                        w, hi, lo, tw = got[e]
                    elif t == 0:
                        w, hi, lo, tw = W.next(f"ffn_o{i}", 2 * u + e)
                    k0 = u == 0 and e == 0
                    k1 = last_one and e == 1
                    if True:
                        c = slice(e * 256 + t * 128, e * 256 + (t + 1) * 128)
                        cl = slice(512 + e * 256 + t * 128, 512 + e * 256 + (t + 1) * 128)
                        for cb in range(2):
                            cs = slice(cb * 512, (cb + 1) * 512)
                            last = mm3([tw, dg, outs[t][cb].last], outs[t][cb].ap, (g.ap[:, c], g.ap[:, cl]),
                                       (hi[:, cs], lo[:, cs]), k0, k1, k1 or (t == 1 and cb == 1))
                            if k1:
                                outs[t][cb].free = resid(1, i, t, cb, outs[t][cb], last)
                    if t == 1 and not last_one:
                        W.done(w, last)
                if last_one:
                    W.done(got[0][0], last)
                    W.done(got[1][0], last)
                g.free = [last]

            for u in range(11):
                hold = {}

                def eva(j, n, b, last):
                    s = wk.get()
                    t1s = [A.op([last, s.last, t_cols], ac.activation, s.ap[:, q * 256:(q + 1) * 256],
                                b.ap[:, q * 256:(q + 1) * 256], ACT.Identity, bias=K("fconv_b", i * 22 + 2 * u + q),
                                scale=K("fconv_w", i * 66 + 44 + 2 * u + q)) for q in range(2)]
                    fr = []
                    for q in range(2):
                        hb = b.ap[:, q * 256:(q + 1) * 256]
                        o = s.ap[:, q * 256:(q + 1) * 256]
                        t1 = t1s
                        for j2 in (1, 0):
                            sh = 2 - j2
                            t1 = V.op([t1], ve.scalar_tensor_tensor, o[:, sh:256], hb[:, 0:256 - sh],
                                      K("fconv_w", i * 66 + 22 * j2 + 2 * u + q), o[:, sh:256], MUL, ADD)
                        fr.append(t1)
                    hold["a"] = s, A.op(fr, ac.activation, s.ap, s.ap, ACT.Gelu_apprx_tanh)
                    return fr

                def evb(j, n, b, last):
                    s, t1 = hold["a"]
                    g = gp.get()
                    t2 = V.op([last, t1], ve.tensor_tensor, s.ap, s.ap, b.ap, MUL)
                    d = split(s.ap, g.ap[:, 0:512], g.ap[:, 512:1024], [t2, g.last], pool=True)
                    s.free = [d[1]]
                    held.append((g, d))
                    return [t2]

                proj_b(XT, 8, f"ffn_a{i}", 2 * u, 2, eva, u == 0)
                proj_b(XT, 8, f"ffn_b{i}", 2 * u, 2, evb)
                if u:
                    second(u - 1, False)
            second(10, True)

        modulated(0, 0, d_x)
        gn = W.beside(gain("norm_final", 0, False), 0.7)
        at[0] = 0
        cqf = take(1024)
        cq = grid(cqf, 2)
        qT, kT = grid(take(2048), 8), grid(take(2048), 8)
        qrf = take(1024)
        qr, kr, vv = grid(qrf, 4), take(256), grid(take(2048), 2)
        CT, OT = Parts(ra, 0, 4), Parts(ra, 2048, 8)

        cs4 = tiny(4)
        d_cq = [None, None]

        def ev_cq(t, cb, b, last):
            t1 = None
            s = wk.get()
            for c in range(2):
                t1 = A.op([last, s.last], ac.activation, s.ap[:, c * 256:(c + 1) * 256],
                          b.ap[:, c * 256:(c + 1) * 256], ACT.Square,
                          accum_out=cs4[:, 2 * t + c:2 * t + c + 1])
            s.free = [t1]
            t1 = rsqrt(cs4[:, 2 * t:2 * t + 2], cs4[:, 2 * t:2 * t + 2], 2, 1.0 / 256, 1e-6, [t1])
            for c in range(2):
                t2 = V.op([t1], ve.tensor_scalar, cq[:, t, c * 256:(c + 1) * 256], b.ap[:, c * 256:(c + 1) * 256],
                          cs4[:, 2 * t + c:2 * t + c + 1], None, MUL)
            d_cq[t] = t2
            return [t2]

        proj_a(XT, 8, "mla_c", 0, 1, ev_cq)

        def rope(o, b, last):
            s = wk.get()
            t1 = V.op([last, t_tab, s.last], ve.tensor_tensor, s.ap[:, 0:256], b.ap[:, 0:256], cosT, MUL)
            t2 = V.op([last, t_tab], ve.tensor_tensor, s.ap[:, 256:512], b.ap[:, 256:512], sinT, MUL)
            t3 = G.op([t1, t2], po.tensor_tensor, o, s.ap[:, 0:256], s.ap[:, 256:512], ADD)
            s.free = [t3]
            return t2, t3

        d_kr = []

        def ev_kr(j, n, b, last):
            t2, t3 = rope(kr, b, last)
            d_kr.append(t3)
            return [t2]

        proj_b(XT, 8, "mla_kr", 0, 2, ev_kr)
        transposed(lambda t, k: cq[:, t, k * 128:(k + 1) * 128], d_cq, CT, 4,
                   lambda k: K("q_norm", k) if k < 2 else K("kv_norm", k - 2))
        d_q, d_k, d_qr, d_v = [None] * 8, [None] * 8, [None] * 4, {}

        def ev_k(j, n, b, last):
            t1 = copy(kT[:, j:j + 2, :], grid(b.ap, 2), [last])
            d_k[j] = d_k[j + 1] = t1
            return [t1]

        def ev_v(t, cb, b, last):
            d_v[t, cb] = copy(vv[:, t, cb * 512:(cb + 1) * 512], b.ap, [last])
            return [d_v[t, cb]]

        proj_a(CT.part(2, 4), 2, "mla_uv", 0, 2, ev_v)

        def ev_q(j, n, b, last):
            g, r = j // 8, j % 8
            if r < 4:
                h = 4 * g + r
                t1 = copy(qT[:, h:h + 2, :], grid(b.ap, 2), [last])
                d_q[h] = d_q[h + 1] = t1
                return [t1]
            p = 2 * g + (r - 4) // 2
            t2, t3 = rope(qr[:, p, :], b, last)
            d_qr[p] = t3
            return [t2]

        def score2(h, t, n, b):
            r = slice(64 * (h % 2), 64 * (h % 2) + 64)
            mm([d_q[h], d_k[h], b.last], b.ap[:, 0:n], qT[:, h, t * 128:(t + 1) * 128], kT[:, h, 0:n], True, False)
            return mm([d_qr[h // 2], d_kr], b.ap[:, 0:n], qr[r, h // 2, t * 128:(t + 1) * 128], kr[r, 0:n],
                      False, True, True)

        def bias2(h, t, n, b, p, toks_):
            return V.op(toks_, ve.scalar_tensor_tensor, p, b.ap[:, 0:n], 192.0 ** -0.5, C("cm", 256 - n, 256),
                        MUL, ADD)

        def fin2(k, b, last):
            OT.dep[k] = split(b.ap[:, 0:256], OT.hi[k], OT.lo[k], [last, extra_end])
            return OT.dep[k]

        def val2(j, h):
            return d_v[j, h // 4], vv[:, j, h * 128:(h + 1) * 128]

        extra_end = []
        mla = attention(score2, bias2, val2, 128, fin2, lambda h: d_qr[h // 2] is not None)
        for g in range(2):
            proj_b(CT.part(2, 4), 2, "mla_uk", g, 4, lambda j, n, b, l: ev_k(4 * g + j, n, b, l))
            proj_b(CT.part(0, 2), 2, "mla_uq", 2 * g, 8, lambda j, n, b, l: ev_q(8 * g + j, n, b, l))
            if g == 0:
                mt = W.beside(mla, 2.0)

        def with_heads(task):

            def before(cb, q):
                while cb == 0 and (OT.dep[2 * q] is None or OT.dep[2 * q + 1] is None):
                    next(task[0])
                    W.step(SHARE)
            return before

        proj_a(OT, 8, "mla_o", 0, 2, lambda t, cb, b, l: resid(0, 0, t, cb, b, l), True,
               with_heads(mt))
        mla_end = (P.sem, P.count)
        d1 = layer_norm()
        modulated(0, 1, d1)
        W.pool = P4
        gn = W.beside(gain("ln", 0, True), 0.7)
        more_raw(cqf, [mla_end])
        more_raw(qrf, [mla_end])
        extra = parts_.add(ra[:, 4096:6144], [mla_end])
        ffn(0)
        parts_.spots.remove(extra)
        d2 = layer_norm()

        modulated(1, 0, d2)
        W.pool = P5
        gn = W.beside(gain("ln", 2048, True), 0.7)

        def ev_q3(j, n, b, last):
            t1 = A.op([last], ac.activation, qT[:, j:j + 2, :], grid(b.ap, 2), ACT.Copy, scale=128.0 ** -0.5)
            d_q[j] = d_q[j + 1] = t1
            return [t1]

        def score3(h, t, n, b):
            return mm([d_q[h], d_k[h], b.last], b.ap[:, 0:n], qT[:, h, t * 128:(t + 1) * 128], kT[:, h, 0:n],
                      True, True, True)

        def bias3(h, t, n, b, p, toks_):
            return V.op([toks_, t_dist], ve.scalar_tensor_tensor, p, dist[:, t, 0:n], -(2.0 ** -(h + 1)),
                        b.ap[:, 0:n], MUL, ADD)

        proj_a(XT, 8, "moba_v", 0, 2, ev_v)
        extra_end.append(extra.free)
        moba = W.beside(attention(score3, bias3, val2, 128, fin2, lambda h: d_k[h] is not None), 1.1)
        d_k[0:8] = [None] * 8
        OT.dep[0:8] = [None] * 8
        for h in range(0, 8, 2):
            proj_b(XT, 8, "moba_q", h, 2, lambda j, n, b, l: ev_q3(h + j, n, b, l))
            proj_b(XT, 8, "moba_k", h, 2, lambda j, n, b, l: ev_k(h + j, n, b, l))
        proj_a(OT, 8, "moba_o", 0, 2, lambda t, cb, b, l: resid(0, 1, t, cb, b, l), True,
               with_heads(moba))
        d1 = layer_norm()
        modulated(1, 1, d1)
        gn = W.beside(gain("ln", 4096, True), 0.7)
        parts_.add(ra[:, 4096:6144], [(P.sem, P.count)])
        ffn(1)
        d2 = layer_norm()
        g, tg_ = rows("ln", 6144, 1024)
        bb, tb_ = rows("ln", 7168, 1024)
        s_out = sem("s_out")
        for t in range(2):
            t1 = V.op([*d2[t].values(), tg_], ve.tensor_tensor, X[:, t, :], X[:, t, :], g.ap, MUL)
            t1 = V.op([t1, tb_], ve.tensor_tensor, X[:, t, :], X[:, t, :], bb.ap, ADD)
            S.dma([t1], s_out, 16 * (t + 1), nc.sync.dma_start, out[t * 128:(t + 1) * 128, :], X[:, t, :])
        S.wait([(s_out, 32)])

        block = ctx.enter_context(nc.Block())

        @block.sync
        def _(eng):
            S.emit(eng)

        @block.gpsimd
        def _(eng):
            G.emit(eng)

        @block.scalar
        def _(eng):
            A.emit(eng)

        @block.vector
        def _(eng):
            V.emit(eng)

        @block.tensor
        def _(eng):
            P.emit(eng)


def constants():
    c = np.zeros((128, NCONST), np.float32)

    def put(name, a):
        c[:a.shape[0], CONST_AT[name][0]:CONST_AT[name][0] + a.shape[1]] = a

    put("ident", np.eye(128, dtype=np.float32))
    put("ones", np.ones((128, 256), np.float32))
    sel = np.zeros((4, 4, 128), np.float32)
    for h in range(4):
        sel[h, h] = 1.0
    d = np.maximum(255 - np.arange(383), 0)
    large = 16 + (np.log(np.maximum(d, 1).astype(np.float32) / np.float32(16)) / np.log(8.0) * 16).astype(np.int32)
    bucket = np.where(d < 16, d, np.minimum(large, 31))
    oh = np.zeros((32, 384), np.float32)
    oh[bucket, np.arange(383)] = 1.0
    i = np.arange(128)
    up = np.where(i[None, :] > i[:, None], -BIG, 0.0).astype(np.float32)
    z = np.zeros((128, 128), np.float32)
    put("cm", np.concatenate([z, up], 1))
    put("cmT", np.concatenate([up.T, z], 1))
    return c, sel.reshape(4, 512), oh


def pack_b(w):
    nk, nb = w.shape[0] // 128, w.shape[1] // 128
    per = 8 // nk
    nu = -(-nb // per)
    out = np.zeros((nu, 128, per, nk, 128), w.dtype)
    for j in range(nb):
        out[j // per, :, j % per] = w[:, j * 128:(j + 1) * 128].reshape(nk, 128, 128).transpose(1, 0, 2)
    return out.reshape(nu, 128, 1024)


def pack_a(w):
    nk, ncb = w.shape[0] // 128, w.shape[1] // 512
    return w.reshape(nk // 2, 2, 128, ncb, 512).transpose(3, 0, 2, 1, 4).reshape(ncb * nk // 2, 128, 1024)


def layout(I):
    f = np.float32
    a = {k: np.asarray(v) for k, v in I.items()}
    o = {}
    o["x"] = a["x"][0]
    o["pT"] = np.ascontiguousarray(a["p"][0, 0].T)
    o["rel_bias"] = a["rel_bias"]
    o["pos_r"] = a["positions_2"].reshape(1, 256)
    o["pos_c"] = np.ascontiguousarray(a["positions_2"].reshape(2, 128).T)
    o["consts"], o["sel"], o["onehot"] = constants()
    c = np.zeros((128, NCOL), f)

    def put(name, m):
        c[:m.shape[0], COL_AT[name][0]:COL_AT[name][0] + m.shape[1]] = m

    def col(v):
        return v.reshape(-1, 128).T

    put("norm_in", col(a["norm_in"][0]))
    put("conv_w", col(a["conv_w"][0].reshape(-1)))
    put("fconv_w", col(a["ffn_conv_w_2"].reshape(-1)))
    put("fconv_b", col(a["ffn_conv_b_2"].reshape(-1)))
    put("q_norm", col(a["mla_q_norm_2"][0]))
    put("kv_norm", col(a["mla_kv_norm_2"][0]))
    put("mod_b", col(a["mod_b_2"].reshape(-1)))
    put("c", col(a["c_2"][0]))
    put("b_gate", a["b_gate"][0].reshape(2, 4).T)
    inv = (10000.0 ** (-np.arange(32, dtype=f) / f(32))).astype(f)
    put("inv_freq", np.tile(inv, 4)[:, None])
    put("nf", col(a["norm_final"]))
    put("ln", col(np.stack([a["ln_g_2"], a["ln_b_2"]], 2).reshape(-1)))
    put("sign", np.tile(np.repeat(np.array([-1.0, 1.0], f), 32), 2)[:, None])
    o["cols"] = c
    w = a["w_in"][0]
    cut = np.cumsum([0, 512, 512, 1024, 1024, 1024, 8, 512, 512, 512, 512, 512, 64, 8])
    mq, mk, m_v, mo, mz, mif, aq, ak, a_v, az, iq, ik, iw = (w[:, cut[i]:cut[i + 1]] for i in range(13))
    o["w_iq"] = pack_b(np.concatenate([iq, ik, ik], 1))
    o["w_mqk"] = pack_b(np.concatenate([mq, mk], 1))
    o["w_mv"], o["w_av"] = pack_a(m_v), pack_a(a_v)
    o["w_aqk"], o["w_az"] = pack_b(np.concatenate([aq, ak], 1)), pack_b(az)
    o["w_g"] = np.concatenate([mif, iw], 1).reshape(8, 128, 16).transpose(1, 0, 2).reshape(1, 128, 128)
    o["w_moz"] = pack_a(np.concatenate([mo[:, :512], mz[:, :512], mo[:, 512:], mz[:, 512:]], 1))
    o["w_out"] = pack_a(a["w_out"][0])
    o["w_ple"] = pack_a(a["w_ple"][0])
    o["w_gate"] = pack_a(a["w_ple_gate"][0])
    o["m_norm"], o["norm_final"] = a["m_norm"], a["norm_final"].reshape(1, -1)
    o["mod_b"] = a["mod_b_2"]
    o["mod_w"] = np.ascontiguousarray(a["mod_w_2"].reshape(2, 8, 128, 6, 1024).transpose(0, 3, 1, 2, 4)).reshape(
        96, 128, 1024)
    o["ln"] = np.ascontiguousarray(np.stack([a["ln_g_2"], a["ln_b_2"]], 2).reshape(4, 2048))
    for i in range(2):
        o[f"ffn_a{i}"] = pack_b(a["ffn_w_in_2"][i][:, 0:2816])
        o[f"ffn_b{i}"] = pack_b(a["ffn_w_in_2"][i][:, 2816:])
        o[f"ffn_o{i}"] = a["ffn_w_out_2"][i].reshape(22, 128, 1024)
    w = a["mla_w_in_2"][0]
    o["mla_c"] = pack_a(w[:, 0:512])
    r, s = w[:, 512:576], np.concatenate([w[:, 544:576], w[:, 512:544]], 1)
    o["mla_kr"] = pack_b(np.concatenate([r, r, s, s], 1))
    w = a["mla_w_uq_2"][0].reshape(256, 8, 192)
    parts = []
    for g in range(2):
        parts.append(w[:, 4 * g:4 * g + 4, 0:128].reshape(256, 512))
        for j in (2 * g, 2 * g + 1):
            r = w[:, 2 * j:2 * j + 2, 128:192]
            parts += [r.reshape(256, 128), np.concatenate([r[:, :, 32:], r[:, :, :32]], 2).reshape(256, 128)]
    o["mla_uq"] = pack_b(np.concatenate(parts, 1))
    w = a["mla_w_ukv_2"][0].reshape(256, 8, 256)
    o["mla_uk"] = pack_b(w[:, :, 0:128].reshape(256, 1024))
    o["mla_uv"] = pack_a(w[:, :, 128:256].reshape(256, 1024))
    o["mla_o"] = pack_a(a["mla_w_o_2"][0])
    w = a["moba_w_in_2"][0]
    o["moba_q"], o["moba_k"] = pack_b(w[:, 0:1024]), pack_b(w[:, 1024:2048])
    o["moba_v"] = pack_a(w[:, 2048:3072])
    o["moba_o"] = pack_a(a["moba_w_o_2"][0])
    return {k: np.ascontiguousarray(v) for k, v in o.items()}


def kernel(**inputs):
    import concourse.bacc as bacc
    from concourse.bass_utils import run_bass_kernel_spmd

    nc = bacc.Bacc("TRN2", target_bir_lowering=False, num_devices=1)
    arrays = {f"in_{k}": v for k, v in layout(inputs).items()}
    D = {k[3:]: nc.dram_tensor(k, v.shape, mybir.dt.from_np(v.dtype), kind="ExternalInput").ap()
         for k, v in arrays.items()}
    out = nc.dram_tensor("out_0", (256, 1024), mybir.dt.float32, kind="ExternalOutput").ap()
    build(nc, D, out)
    r = run_bass_kernel_spmd(nc, [arrays], core_ids=[0])
    return r.results[0]["out_0"].reshape(1, 256, 1024)
```

```python
import numpy as np
import concourse.bass as bass
from concourse import mybir
from contextlib import ExitStack

BIG = 1e30
COLS = [("norm_in", 8), ("conv_w", 32), ("fconv_w", 132), ("fconv_b", 44), ("q_norm", 2), ("kv_norm", 2),
        ("mod_b", 96), ("c", 8), ("b_gate", 2), ("inv_freq", 1), ("sign", 1), ("nf", 8), ("ln", 64)]
CONSTS = [("ident", 128), ("ones", 256), ("cm", 256), ("cmT", 256)]


def spans(table):
    out, at = {}, 0
    for name, n in table:
        out[name] = (at, at + n)
        at += n
    return out, at


COL_AT, NCOL = spans(COLS)
CONST_AT, NCONST = spans(CONSTS)


MOD_PACE = [0.7, 0.9, 0.8, 1.25, 1.0, 0.8, 0.65]
LSTM_PACE, DSA_PACE, MLA_PACE, MOBA_PACE, GATES_PACE, INDEXER_PACE = 1.22, 1.53, 1.6, 0.87, 0.6, 0.8
SHARE = 0.65
POOL_PART = [0.1, 0.5, 0.15, 0.2, 0, 0.3]
LAG, DELAY = 1, 2


class Queue:

    def __init__(self, sem):
        self.sem, self.count, self.items, self.seen = sem, 0, [], {}

    def wait(self, tokens):
        for t in tokens:
            if t is None:
                continue
            if isinstance(t, list):
                self.wait(t)
                continue
            sem, value = t
            if self.seen.get(sem.name, 0) < value:
                self.seen[sem.name] = value
                self.items.append((None, (sem, value), None, None, 0))

    def op(self, tokens, fn, *args, **kw):
        self.wait(tokens)
        self.count += 1
        self.items.append((fn, args, kw, self.sem, 1))
        return self.sem, self.count

    def quiet(self, tokens, fn, *args, **kw):
        self.wait(tokens)
        self.items.append((fn, args, kw, None, 0))

    def dma(self, tokens, sem, value, fn, *args, **kw):
        self.wait(tokens)
        self.items.append((fn, args, kw, sem, 16))
        return sem, value

    def emit(self, eng):
        for fn, args, kw, sem, by in self.items:
            if fn is None:
                eng.wait_ge(*args)
            elif sem is None:
                fn(*args, **kw)
            else:
                fn(*args, **kw).then_inc(sem, by)


class Spot:

    clock = 0

    def __init__(self, ap):
        self.ap, self.free = ap, []

    @property
    def free(self):
        return self.tokens

    @free.setter
    def free(self, tokens):
        self.tokens = tokens
        Spot.clock += 1
        self.since = Spot.clock


class Turn:

    def __init__(self, aps):
        self.spots = [Spot(a) for a in aps]

    def add(self, ap, tokens):
        s = Spot(ap)
        s.free = tokens
        self.spots.insert(0, s)
        return s

    def get(self):
        s = min((x for x in self.spots if x.free is not None), key=lambda x: x.since)
        s.last, s.free = s.free, None
        return s


def build(nc, D, out):
    f32, f32r, i32 = mybir.dt.float32, mybir.dt.float32r, mybir.dt.int32
    ALU, ACT, AX = mybir.AluOpType, mybir.ActivationFunctionType, mybir.AxisListType
    MUL, ADD, SUB, MAX, MIN = ALU.mult, ALU.add, ALU.subtract, ALU.max, ALU.min
    ctx = ExitStack()
    with ctx:
        def sb(name, cols, dt=f32):
            return ctx.enter_context(nc.sbuf_tensor(name, [128, cols], dt))

        def sem(name):
            return ctx.enter_context(nc.semaphore(name))

        P, V, A, G, S = (Queue(sem(n)) for n in ("s_pe", "s_dve", "s_act", "s_pool", "s_sp"))
        ve, ac, po, pe = nc.vector, nc.scalar, nc.gpsimd, nc.tensor

        NR, NW = 5, 4
        ring_t = sb("ring", NR * 1024)
        raw = Turn([ring_t[:, i * 1024:(i + 1) * 1024] for i in range(NR)])
        for i, r_ in enumerate(raw.spots):
            r_.sem, r_.count = sem(f"s_w{i}"), 0

        raw_n = [NR]

        def more_raw(ap, tokens):
            r_ = raw.add(ap, tokens)
            raw_n[0] += 1
            r_.sem, r_.count = sem(f"s_w{raw_n[0]}"), 0
            return r_

        wsp = sb("wsp", NW * 2048, f32r)
        parts_ = Turn([wsp[:, i * 2048:(i + 1) * 2048] for i in range(NW)])

        def load(src, n=1024):
            s = raw.get()
            s.count += 16
            return s, S.dma(s.last, s.sem, s.count, nc.sync.dma_start, s.ap[:, 0:n], src)

        def rows(name, off, n):
            return load(bass.AP(D[name].tensor, off, [[0, 128], [1, n]]), n)

        class Stream:

            def __init__(self, plan):
                self.soon = []
                self.pool, self.turn, self.still = POOL_PART[0], 0.0, False
                self.plan, self.at, self.lows, self.ready, self.tasks, self.loads = plan, 0, 0, [], [], []

            def fetch(self):
                name, u, n = self.plan[len(self.ready) + len(self.loads)]
                self.loads.append(load(D[name][u][:, 0:n], n))

            def prepare(self):
                name, u, n = self.plan[len(self.ready)]
                if not self.loads:
                    self.fetch()
                r, tr = self.loads.pop(0)
                w = parts_.get()
                hi, lo = w.ap[:, 0:n], w.ap[:, 1024:1024 + n]
                th = A.op([tr, w.last], ac.copy, hi, r.ap[:, 0:n])
                self.ready.append([name, u, w, hi, lo, [th, tr], r, n])

            def low(self):
                name, u, w, hi, lo, toks, r, n = self.ready[self.lows]
                self.turn += self.pool
                if self.turn >= 1:
                    self.turn -= 1
                    tl = G.op(toks, po.tensor_tensor, lo, r.ap[:, 0:n], hi.bitcast(f32), SUB)
                else:
                    tl = V.op(toks, ve.tensor_tensor, lo, r.ap[:, 0:n], hi.bitcast(f32), SUB)
                r.free = [tl]
                toks[1] = tl
                self.lows += 1

            def next(self, name, u):
                while len(self.ready) < min(self.at + len(parts_.spots), len(self.plan)) and \
                        any(x.free is not None for x in parts_.spots):
                    self.prepare()
                    while len(self.ready) - self.lows > LAG:
                        self.low()
                while self.lows <= self.at:
                    self.low()
                while self.soon:
                    self.soon.pop(0)()
                got = self.ready[self.at]
                assert got[0:2] == [name, u], (got[0:2], name, u)
                self.at += 1
                return got[2:6]

            def done(self, w, last):
                w.free = [last]
                self.step(1.0)

            def step(self, share):
                for t in list(self.tasks):
                    t[2] += t[1] * share
                    if self.still:
                        continue
                    while t[2] >= 1 and t in self.tasks:
                        t[2] -= 1
                        if next(t[0], 1) == 1:
                            self.tasks.remove(t)

            def beside(self, gen, rate):
                t = [gen, rate, 0.0]
                self.tasks.append(t)
                return t

            def finish(self, t):
                if t in self.tasks:
                    self.tasks.remove(t)
                for _ in t[0]:
                    self.step(SHARE)

        psum = Turn([ctx.enter_context(nc.psum_tensor(f"ps{i}", [128, 512], f32))[:, :] for i in range(8)])

        cst = sb("cst", NCONST)
        cols = sb("cols", NCOL)
        X = sb("X", 2048)[:, :].rearrange("p (t n) -> p t n", t=2)
        XTr = sb("XT", 4096, f32r)
        R2 = sb("R2", 2048)[:, :].rearrange("p (m n) -> p m n", m=2)
        acc = [sb(f"acc{i}", 1024)[:, :] for i in range(2)]
        small = sb("small", 512)
        AR_N, RA_N = 14864, 8192
        arena = sb("arena", AR_N)
        ra = sb("ra", RA_N, f32r)
        wk = Turn([sb(f"wk{i}", 512)[:, :] for i in range(3)])
        pb = Turn([sb(f"pb{i}", 256)[:, :] for i in range(4)])
        pt = Turn([sb(f"pt{i}", 256)[:, :] for i in range(3)])
        posi = sb("posi", 258, i32)
        gscr = nc.dram_tensor("gscr", [8, 128, 383], f32, kind="Internal").ap()

        def C(name, a=0, b=None):
            lo, hi = CONST_AT[name]
            return cst[:, lo + a:(hi if b is None else lo + b)]

        def K(name, i=0, n=1):
            lo = COL_AT[name][0]
            return cols[:, lo + i:lo + i + n]

        at = [0]

        def take(n):
            at[0] += n
            assert at[0] <= AR_N, at[0]
            return arena[:, at[0] - n:at[0]]

        sm_at = [0]

        def tiny(n):
            sm_at[0] += n
            assert sm_at[0] <= 512
            return small[:, sm_at[0] - n:sm_at[0]]

        def grid(ap, k):
            return ap.rearrange("p (k n) -> p k n", k=k)

        class Parts:

            def __init__(self, t, off, n):
                self.hi = [t[:, off + k * 256:off + (k + 1) * 256] for k in range(n)]
                self.lo = [t[:, off + (n + k) * 256:off + (n + k + 1) * 256] for k in range(n)]
                self.hi2 = [t[:, off + k * 256:off + (k + 2) * 256] for k in range(0, n, 2)]
                self.lo2 = [t[:, off + (n + k) * 256:off + (n + k + 2) * 256] for k in range(0, n, 2)]
                self.dep = [None] * n

            def part(self, a, b):
                p = Parts.__new__(Parts)
                p.hi, p.lo, p.dep = self.hi[a:b], self.lo[a:b], self.dep[a:b]
                return p

        s_in = [sem(f"s_in{i}") for i in range(7)]
        s_rb = sem("s_rb")
        xsrc = D["x"].rearrange("(t p) n -> t p n", t=2)
        t_x = [S.dma([], s_in[2], 16, nc.sync.dma_start, X[:, 0, :], xsrc[0])]
        t_cst = S.dma([], s_in[0], 16, nc.sync.dma_start, cst[:, 0:384], D["consts"][:, 0:384])
        t_x.append(S.dma([], s_in[5], 16, nc.sync.dma_start, X[:, 1, :], xsrc[1]))
        t_cols = S.dma([], s_in[1], 16, nc.sync.dma_start, cols[:, :], D["cols"])
        relb = tiny(8)
        pT = grid(take(512), 2)
        ID = C("ident")
        ones = C("ones")

        units = []

        def plan(name, n, cols_=1024):
            units.extend((name, u, cols_) for u in range(n))

        plan("w_iq", 5)
        plan("w_g", 1, 768)
        plan("w_mqk", 8)
        plan("w_mv", 8)
        plan("w_aqk", 8)
        plan("w_av", 4)
        plan("w_az", 4)
        plan("w_moz", 16)
        plan("w_out", 6)
        plan("w_ple", 2)
        units.extend(("w_out", u, 1024) for u in range(6, 12))
        plan("w_gate", 8)
        plan("mla_c", 4)
        plan("mla_kr", 2)
        plan("mla_uv", 2)
        for g in range(2):
            units.extend([("mla_uk", g, 1024), ("mla_uq", 2 * g, 1024), ("mla_uq", 2 * g + 1, 1024)])
        plan("mla_o", 8)
        for i in range(2):
            if i == 1:
                plan("moba_v", 8)
                for h in range(0, 8, 2):
                    for n_ in ("q", "k"):
                        units.extend((f"moba_{n_}", h + e, 1024) for e in range(2))
                plan("moba_o", 8)
            for u in range(11):
                for n_ in ("a", "b"):
                    units.extend((f"ffn_{n_}{i}", 2 * u + e, 1024) for e in range(2))
                if u:
                    units.extend((f"ffn_o{i}", 2 * u - 2 + e, 1024) for e in range(2))
            units.extend((f"ffn_o{i}", 20 + e, 1024) for e in range(2))
        W = Stream(units)
        for _ in range(3):
            W.fetch()
        t_cst2 = S.dma([], s_in[6], 16, nc.sync.dma_start, cst[:, 384:NCONST], D["consts"][:, 384:NCONST])

        def mm(tokens, o, l, r, start, stop, mark=False, group=True):
            if mark:
                return P.op(tokens, pe.matmul, o, l, r, start=start, stop=stop)
            P.quiet(tokens, pe.matmul, o, l, r, start=start, stop=stop)

        def mm3(tokens, o, l, r, start, stop, mark=False):
            (lh, ll), (rh, rl) = l, r
            mm(tokens, o, lh, rh, start, False)
            mm([], o, lh, rl, False, False)
            return mm([], o, ll, rh, False, stop, mark)

        def proj_b(x, nk, name, first, blocks, evac, outer=False):
            per = 8 // nk
            if outer:
                got = [W.next(name, first + j) for j in range(2)]
                b = psum.get()
                for k in range(nk):
                    c = slice(k * 128, (k + 1) * 128)
                    for m in range(2):
                        w, hi, lo, tw = got[m]
                        last = mm3([tw, x.dep[k], b.last], b.ap[:, m * 256:(m + 1) * 256], (hi[:, c], lo[:, c]),
                                   (x.hi[k], x.lo[k]), k == 0 and m == 0, k == nk - 1 and m == 1, k == nk - 1)
                b.free = evac(0, 2, b, last)
                for m in range(2):
                    W.done(got[m][0], last)
            w = None
            for j in range(2 if outer else 0, blocks):
                if j % per == 0:
                    w, hi, lo, tw = W.next(name, first + j // per)
                if j % 2 == 0:
                    b = psum.get()
                m = j % 2
                for k in range(nk):
                    c = slice(((j % per) * nk + k) * 128, ((j % per) * nk + k + 1) * 128)
                    last = mm3([tw, x.dep[k], b.last], b.ap[:, m * 256:(m + 1) * 256], (hi[:, c], lo[:, c]),
                               (x.hi[k], x.lo[k]), k == 0, k == nk - 1, k == nk - 1)
                if m == 1 or j == blocks - 1:
                    b.free = evac(j - m, m + 1, b, last)
                if j % per == per - 1 or j == blocks - 1:
                    W.done(w, last)

        def proj_a(x, nk, name, first, blocks, evac, tail=False, before=None):
            nq = nk // 2
            for cb in range(blocks):
                bs = [psum.get(), psum.get()]
                q = 0
                while q < nq:
                    m = 2 if tail and cb == blocks - 1 and q == nq - 2 else 1
                    if before:
                        before(cb, q)
                    if m == 2:
                        W.still = True
                    got = [W.next(name, first + cb * nq + q + e) for e in range(m)]
                    for t in range(2):
                        tc = slice(t * 128, (t + 1) * 128)
                        for e in range(m):
                            w, hi, lo, tw = got[e]
                            for k in range(2):
                                kg = 2 * (q + e) + k
                                c = slice(k * 512, (k + 1) * 512)
                                last = mm3([tw, x.dep[kg], bs[t].last], bs[t].ap, (x.hi[kg][:, tc], x.lo[kg][:, tc]),
                                           (hi[:, c], lo[:, c]), kg == 0, kg == nk - 1, k == 1)
                        if q + m == nq:
                            bs[t].free = evac(t, cb, bs[t], last)
                    q += m
                    for e in range(m):
                        W.done(got[e][0], last)

        def split(f, hi, lo, tokens, pool=False):
            t1 = A.op(tokens, ac.copy, hi, f)
            if pool:
                t2 = G.op([t1], po.tensor_tensor, lo, f, hi.bitcast(f32), SUB)
            else:
                t2 = V.op([t1], ve.tensor_tensor, lo, f, hi.bitcast(f32), SUB)
            return [t1, t2]

        def transposed(src, deps, dst, nk, scale=None, shift=None, need=None, order=None, apart=False):
            def dep(t, k):
                return deps[t][k // 4] if isinstance(deps[t], dict) else deps[t]

            pending = []

            def low_part():
                k, s, t1 = pending.pop(0)
                if k == 4:
                    t2 = G.op([t1], po.tensor_tensor, dst.lo2[k // 2], s.ap, dst.hi2[k // 2].bitcast(f32), SUB)
                else:
                    t2 = V.op([t1], ve.tensor_tensor, dst.lo2[k // 2], s.ap, dst.hi2[k // 2].bitcast(f32), SUB)
                s.free = [t2]
                dst.dep[k] = dst.dep[k + 1] = [t1, t2]

            banks = {}
            if apart:
                for k in range(0, nk, 2):
                    banks[k] = psum.get()
                    for i in range(2):
                        P.quiet([dep(0, k), banks[k].last, t_cst], pe.transpose,
                                banks[k].ap[:, i * 256:i * 256 + 128], src(0, k + i), ID)
            for k in order or range(0, nk, 2):
                b = banks[k] if apart else psum.get()
                for i in range(2):
                    for t in range(1 if apart else 0, 2):
                        o = b.ap[:, i * 256 + t * 128:i * 256 + (t + 1) * 128]
                        if i == 1 and t == 1:
                            last = P.op([dep(t, k), b.last, t_cst], pe.transpose, o, src(t, k + i), ID)
                        else:
                            P.quiet([dep(t, k), b.last, t_cst], pe.transpose, o, src(t, k + i), ID)
                if scale is None:
                    d = split(b.ap, dst.hi2[k // 2], dst.lo2[k // 2], [last])
                    b.free = d
                    dst.dep[k] = dst.dep[k + 1] = d
                elif shift is None:
                    t1 = [A.op([last, need], ac.activation, dst.hi[k + i], b.ap[:, i * 256:(i + 1) * 256],
                               ACT.Copy, scale=scale(k + i)) for i in range(2)]
                    for i in range(2):
                        t2 = V.op([t1, need], ve.scalar_tensor_tensor, dst.lo[k + i], b.ap[:, i * 256:(i + 1) * 256],
                                  scale(k + i), dst.hi[k + i].bitcast(f32), MUL, SUB)
                        dst.dep[k + i] = [t1, t2]
                    b.free = [t2]
                else:
                    s = wk.get()
                    for i in range(2):
                        o, f = s.ap[:, i * 256:(i + 1) * 256], b.ap[:, i * 256:(i + 1) * 256]
                        if k == 6:
                            t1 = A.op([last, s.last, need], ac.activation, o, f, ACT.Identity, bias=shift(k + i),
                                      scale=scale(k + i))
                        else:
                            t1 = V.op([last, s.last, need], ve.tensor_scalar, o, f, scale(k + i), shift(k + i),
                                      MUL, ADD)
                    b.free = [t1]
                    t1 = A.op([t1], ac.copy, dst.hi2[k // 2], s.ap)
                    pending.append((k, s, t1))
                    if len(pending) > 1:
                        low_part()
            while pending:
                low_part()
            if apart:
                W.still = False

        half_neg = tiny(8)
        t_hn = V.op([], ve.memset, half_neg, -0.5)

        def rsqrt(src, o, n, scale, eps, tokens):
            t = V.op(tokens, ve.tensor_scalar, o, src, scale, eps, MUL, ADD)
            return G.op([t, t_hn], po.tensor_tensor, o, o, half_neg[:, 0:n], ALU.pow)

        turn = [0]

        def copy(o, i, tokens):
            turn[0] += 1
            if turn[0] % 2:
                return V.op(tokens, ve.tensor_copy, o, i)
            return A.op(tokens, ac.copy, o, i)

        XT = Parts(XTr, 0, 8)

        qkT = grid(take(2048), 8)
        GTf = take(2048)
        GT = grid(GTf, 2)
        aqk = grid(take(2048), 8)
        azT = grid(take(1024), 4)
        iqT = grid(take(1024), 4)
        ikT = take(256)
        mv = take(2 * 4 * 258).rearrange("p (t h n) -> p t h n", t=2, h=4)
        avf = take(1024)
        av = grid(avf, 2)
        scr = take(2816)
        MX = Parts(ra, 0, 12)
        TB = grid(ra[:, 6144:8192], 8)

        sel, onehot = azT[0:4, 0:2, :].rearrange("p k n -> p (k n)"), av[0:32, 0, 0:384]

        ss = tiny(2)
        Y = GT
        dU = []
        for t in range(2):
            t1 = A.op([t_x[t]], ac.activation, Y[:, t, :], X[:, t, :], ACT.Square, accum_out=ss[:, t:t + 1])
            t1 = rsqrt(ss[:, t:t + 1], ss[:, t:t + 1], 1, 1.0 / 1024, 1e-6, [t1])
            t2 = V.op([t1], ve.tensor_scalar, Y[:, t, 0:512], X[:, t, 0:512], ss[:, t:t + 1], None, MUL)
            t3 = A.op([t1], ac.activation, Y[:, t, 512:1024], X[:, t, 512:1024], ACT.Copy, scale=ss[:, t:t + 1])
            dU.append({0: t2, 1: t3})

        W.prepare()
        W.low()
        transposed(lambda t, k: Y[:, t, k * 128:(k + 1) * 128], dU, XT, 8, lambda k: K("norm_in", k), need=[t_cols],
                   apart=True)

        lent = [more_raw(GTf[:, i * 1024:(i + 1) * 1024], [(P.sem, P.count)]) for i in range(2)]
        S.dma([], s_in[3], 16, nc.sync.dma_start, relb[0:32, :], D["rel_bias"])
        S.dma([], s_in[3], 32, nc.sync.dma_start, posi[:, 0:256],
              bass.AP(D["pos_r"].tensor, 0, [[0, 128], [1, 256]]))
        S.dma([], s_in[3], 48, nc.sync.dma_start, posi[:, 256:258], D["pos_c"])
        S.dma([], s_in[3], 64, nc.sync.dma_start, onehot, D["onehot"])
        S.dma([], s_in[3], 80, nc.sync.dma_start, sel, D["sel"])
        t_misc = S.dma([], s_in[3], 96, nc.sync.dma_start, pT, D["pT"].rearrange("(k p) n -> p k n", k=2))

        cact = tiny(8)
        cc_ = K("c", 0, 8)
        ct = A.op([t_cols], ac.activation, cact, cc_, ACT.Tanh, scale=0.5)
        ct = V.op([ct], ve.scalar_tensor_tensor, cact, cact, 1.0, cc_, ADD, MUL)
        ct = V.op([ct], ve.tensor_scalar, cact, cact, 0.5, None, MUL)
        t_mod = {}
        MCi = [[tiny(32), tiny(16)], [tiny(32), tiny(16)]]

        r2_used = {}
        ones_r = sb("ones_r", 128, f32r)
        mr = sb("mr", 1024, f32r)
        t_or = A.op([t_cst], ac.copy, ones_r[:, :], ones[:, 0:128])

        def modulation():
            done, mr_free = [], []
            for i in range(2):
                mc, ab = MCi[i]
                for m in range(6):
                    pa = pp_ = None
                    for k in range(8):
                        w, tw = load(D["mod_w"][(i * 6 + m) * 8 + k])
                        if k % 2 == 0:
                            if k == 0:
                                pa = V.op([tw, ct, done], ve.tensor_scalar, acc[0], w.ap, cact[:, k:k + 1], None, MUL)
                            else:
                                pa = V.op([tw, pa], ve.scalar_tensor_tensor, acc[0], w.ap, cact[:, k:k + 1], acc[0],
                                          MUL, ADD)
                            w.free = [pa]
                        elif k == 1:
                            pp_ = A.op([tw, ct, done], ac.activation, acc[1], w.ap, ACT.Copy, scale=cact[:, k:k + 1])
                            w.free = [pp_]
                        else:
                            t1 = A.op([tw, ct], ac.activation, w.ap, w.ap, ACT.Copy, scale=cact[:, k:k + 1])
                            pp_ = G.op([t1, pp_], po.tensor_tensor, acc[1], acc[1], w.ap, ADD)
                            w.free = [pp_]
                        yield
                    t0 = G.op([pa, pp_], po.tensor_tensor, acc[0], acc[0], acc[1], ADD)
                    yield
                    row = m in (2, 5)
                    r = 0 if m == 2 else 1
                    while i and row and r not in r2_used:
                        yield
                    x = {0: 0, 1: 8, 3: 16, 4: 24}.get(m)
                    if row:
                        br, tb = rows("mod_b", i * 6144 + m * 1024, 1024)
                    for cb in range(2):
                        cs = slice(cb * 512, (cb + 1) * 512)
                        t1 = A.op([t0, mr_free], ac.copy, mr[:, 0:512], acc[0][:, cs])
                        yield
                        t2 = V.op([t1], ve.tensor_tensor, mr[:, 512:1024], acc[0][:, cs], mr[:, 0:512].bitcast(f32),
                                  SUB)
                        done = [t2]
                        for _ in range(DELAY):
                            yield
                        b = psum.get()
                        if row:
                            mm([t2, t_or, b.last], b.ap, ones_r[:, :], mr[:, 0:512], True, False)
                            last = mm([], b.ap, ones_r[:, :], mr[:, 512:1024], False, True, True)
                            t = V.op([last, tb, r2_used.get(r) if i else None], ve.tensor_tensor, R2[:, r, cs],
                                     b.ap, br.ap[:, cs], ADD)
                        else:
                            for k in range(4):
                                o = b.ap[:, 2 * k:2 * k + 2]
                                mm([t2, t_or, b.last], o, mr[:, k * 128:(k + 1) * 128], ones_r[:, 0:2], True, False)
                                last = mm([], o, mr[:, 512 + k * 128:640 + k * 128], ones_r[:, 0:2], False, True,
                                          k == 3)
                            y = x + cb * 4
                            t = V.op([last, t_cols], ve.tensor_tensor, mc[:, y:y + 4],
                                     b.ap[:, 0:8].rearrange("p (k n) -> p k n", n=2)[:, :, 0],
                                     K("mod_b", i * 48 + m * 8 + cb * 4, 4), ADD)
                        b.free = [t]
                        mr_free = [last]
                    if row:
                        br.free = [t]
                        t_mod[i, m] = [t]
                    elif m in (1, 4):
                        n = 2 * i - 1 + (m == 4)
                        a_, s_ = mc[:, x:x + 8], mc[:, x - 8:x]
                        t = V.op([t], ve.tensor_scalar, a_, a_, 1.0, None, ADD)
                        if n >= 0:
                            g_, b_ = K("ln", n * 16, 8), K("ln", n * 16 + 8, 8)
                            o_ = ab[:, 0:8] if m == 1 else ab[:, 8:16]
                            t = V.op([t], ve.tensor_tensor, o_, a_, b_, MUL)
                            t = V.op([t], ve.tensor_tensor, s_, s_, o_, ADD)
                        else:
                            g_ = K("nf", 0, 8)
                        t = V.op([t], ve.tensor_tensor, a_, a_, g_, MUL)
                        t_mod[i, m] = [t]
                    yield

        mod = W.beside(modulation(), MOD_PACE[0])

        def until(key):
            while key not in t_mod:
                next(mod[0])
            return t_mod[key]

        d_b1 = {}

        def ev_iq(j, n, b, last):
            if j < 4:
                t = A.op([last], ac.activation, iqT[:, j:j + 2, :], grid(b.ap, 2), ACT.Copy)
                d_b1["iq", j] = d_b1["iq", j + 1] = t
            else:
                t = A.op([last], ac.activation, ikT, b.ap[:, 0:256], ACT.Copy)
                d_b1["ik"] = t
            return [t]

        proj_b(XT, 8, "w_iq", 0, 5, ev_iq, True)

        b = psum.get()
        last = mm([t_cst, t_cst2, t_misc, b.last], b.ap[0:8, 0:384], relb[0:32, :], onehot, True, True, True)
        grow = scr[0:8, 0:384]
        t = V.op([last], ve.tensor_copy, grow, b.ap[0:8, 0:384])
        b.free = [t]
        part = grow.ap[0][0]
        tg = G.dma([t], s_in[4], 16, nc.gpsimd.dma_start, gscr,
                   bass.AP(grow.tensor, grow.offset, [[part, 8], [0, 128], [1, 383]]))

        w, hi, lo, tw = W.next("w_g", 0)
        bw = psum.get()
        for k in range(8):
            c = slice(k * 96, (k + 1) * 96)
            last = mm3([tw, XT.dep[k], bw.last], bw.ap[0:96, 0:256], (hi[:, c], lo[:, c]), (XT.hi[k], XT.lo[k]),
                       k == 0, k == 7, k == 7)
        W.done(w, last)
        srow = scr[0:4, 1536:2816]
        ARr, FS, BC, MR, NM = (srow[:, i * 256:(i + 1) * 256] for i in range(5))
        iwT = wk.get()
        iw = tiny(16)
        t_fs = V.op([last, t_cols], ve.tensor_scalar, FS, bw.ap[32:36, 0:256], K("b_gate", 1)[0:4, :], None, ADD)
        t_iT = A.op([t_fs, iwT.last], ac.activation, iwT.ap[64:72, 0:256], bw.ap[64:72, 0:256], ACT.Copy,
                    scale=8.0 ** -0.5)
        t_li = V.op([t_iT], ve.tensor_scalar, ARr, bw.ap[0:4, 0:256], K("b_gate", 0)[0:4, :], None, ADD)
        bw.free = [t_li]
        t_nm, t_ar, t_bm = [], [], []

        def gates():
            t = V.op([t_fs], ve.scalar_tensor_tensor, BC, FS, -1.0, FS, MUL, MAX)
            yield
            t = A.op([t], ac.activation, BC, BC, ACT.Exp, scale=-1.0)
            yield
            t = V.op([t], ve.tensor_scalar, BC, BC, 1.0, None, ADD)
            t2 = V.op([t_fs], ve.tensor_scalar, FS, FS, 0.0, None, MIN)
            yield
            t = A.op([t], ac.activation, BC, BC, ACT.Ln)
            yield
            t = V.op([t, t2], ve.tensor_tensor, FS, FS, BC, SUB)
            t = V.op([t, t_cst], ve.tensor_tensor_scan, BC, ones[0:4, 0:256], FS, 0.0, MUL, ADD)
            yield
            t = V.op([t, t_li], ve.tensor_tensor, ARr, ARr, BC, SUB)
            t_ar.append(t)
            t = V.op([t], ve.tensor_tensor_scan, MR, ARr, ARr, 0.0, MAX, MAX)
            yield
            t_nm.append(V.op([t], ve.tensor_scalar, NM, MR, -1.0, None, MUL))
            t_bm.append(V.op(t_nm, ve.tensor_tensor, MR, MR, BC, ADD))

        gts = W.beside(gates(), GATES_PACE)
        em, acol = tiny(8), tiny(8)

        def gate_columns():
            b = psum.get()
            for t in range(2):
                P.quiet([t_bm, b.last, t_cst], pe.transpose, b.ap[:, t * 4:t * 4 + 4],
                        MR[:, t * 128:(t + 1) * 128], ID[0:4, 0:4])
                last = P.op([t_ar], pe.transpose, b.ap[:, 8 + t * 4:12 + t * 4],
                            ARr[:, t * 128:(t + 1) * 128], ID[0:4, 0:4])
            t_em = A.op([last], ac.activation, em, b.ap[:, 0:8], ACT.Exp, scale=-1.0)
            t_ac = V.op([t_em], ve.tensor_copy, acol, b.ap[:, 8:16])
            b.free = [t_ac]
            return t_em, t_ac

        wsel = [None, None]
        t_sel = [None, None]

        t_iw = []

        def iw_columns():
            yield
            b = psum.get()
            for t in range(2):
                last = P.op([t_iT, b.last, t_cst], pe.transpose, b.ap[:, t * 8:t * 8 + 8],
                            iwT.ap[64:72, t * 128:(t + 1) * 128], ID[64:72, 64:72])
            iwT.free = [last]
            t_iw.append(A.op([last], ac.copy, iw, b.ap[:, 0:16]))
            b.free = t_iw

        def indexer():
            for t in range(2):
                n = 128 * (t + 1)
                sc = [scr[:, (2 * t + q) * 256:(2 * t + q) * 256 + 256] for q in range(2)]
                prev = None
                for hs in ((0, 2), (1, 3), (4, 6), (5, 7)):
                    b = psum.get()
                    for e, h in enumerate(hs):
                        r = slice(64 * (h % 2), 64 * (h % 2) + 64)
                        last = mm([d_b1["iq", h // 2], d_b1["ik"], b.last], b.ap[:, e * n:(e + 1) * n],
                                  iqT[r, h // 2, t * 128:(t + 1) * 128], ikT[r, 0:n], True, True, e == 1)
                    s = wk.get()
                    t1 = A.op([last, s.last], ac.activation, s.ap[:, 0:2 * n], b.ap[:, 0:2 * n], ACT.Relu,
                              scale=0.125)
                    b.free = [t1]
                    for e, h in enumerate(hs):
                        prev = V.op([t1, t_iw, prev, t_cst2, tg], ve.scalar_tensor_tensor, sc[0][:, 0:n],
                                    s.ap[:, e * n:(e + 1) * n], iw[:, t * 8 + h:t * 8 + 1 + h],
                                    C("cm", 256 - n, 256) if h == 0 else sc[0][:, 0:n], MUL, ADD)
                    s.free = [prev]
                    yield
                m8 = tiny(16)
                for i in range(8):
                    q = m8[:, (i % 2) * 8:(i % 2) * 8 + 8]
                    t1 = V.op([prev], ve.max, q, sc[i % 2][:, 0:n])
                    prev = V.op([t1], ve.match_replace, sc[(i + 1) % 2][:, 0:n], q, sc[i % 2][:, 0:n], -3e38)
                    if i % 2:
                        yield
                t1 = V.op([prev], ve.tensor_scalar, sc[1][:, 0:n], sc[0][:, 0:n], -2e38, -BIG, ALU.is_ge, MUL)
                t_sel[t] = V.op([t1, t_cst2], ve.tensor_tensor, sc[1][:, 0:n], sc[1][:, 0:n],
                                C("cm", 256 - n, 256), ADD)
                wsel[t] = sc[1]
                yield

        W.beside(iw_columns(), 1.0)

        def ev_mqk(j, n, b, last):
            s, th = wq.get(), wq.get()
            fr = [A.op([last, s.last, t_cols], ac.activation, s.ap[:, i * 256:(i + 1) * 256],
                       b.ap[:, i * 256:(i + 1) * 256], ACT.Copy, scale=K("conv_w", 24 + j + i)) for i in range(n)]
            fr = [fr] * n
            for tap in (2, 1, 0):
                for i in range(n):
                    sh = 3 - tap
                    o = s.ap[:, i * 256:(i + 1) * 256]
                    fr[i] = V.op([fr[i]], ve.scalar_tensor_tensor, o[:, sh:256], b.ap[:, i * 256:(i + 1) * 256 - sh],
                                 K("conv_w", tap * 8 + j + i), o[:, sh:256], MUL, ADD)
            t = []
            W.soon.append(lambda: t.append(A.op([fr, th.last], ac.activation, th.ap, s.ap, ACT.Tanh, scale=0.5)))
            silus.append((j, s, th, t))
            if len(silus) > 1:
                silu()
            if j == 6:
                W.soon.append(silu)
            return fr

        silus = []
        mvf = mv.rearrange("p t h n -> p (t h n)")
        wq = Turn([mvf[:, i * 512:(i + 1) * 512] for i in range(4)])

        def silu():
            j, s, th, t = silus.pop(0)
            t = V.op([t, dXT], ve.scalar_tensor_tensor, qkT[:, j:j + 2, :], grid(th.ap, 2), 1.0, grid(s.ap, 2),
                     ADD, MUL)
            s.free = th.free = [t]
            d_b1["qk", j] = d_b1["qk", j + 1] = t

        dXT = [XT.dep[k] for k in range(8)]
        W.pool = POOL_PART[1]
        proj_b(XT, 8, "w_mqk", 0, 8, ev_mqk)
        W.pool = POOL_PART[2]
        d_mv, d_av, d_g = {}, {}, {}
        idx = W.beside(indexer(), INDEXER_PACE)
        t_TB = G.dma([tg], s_rb, 16, nc.gpsimd.dma_start, TB.bitcast(f32),
                     bass.AP(gscr.tensor, 127, [[382, 128], [128 * 383, 8], [1, 256]]))

        t_one = []

        def ev_mv(t, cb, b, last):
            if not t_one:
                t_one.extend(G.op([d_b1["qk", 6]], po.memset, mv[:, t_, :, 256:257], 1.0) for t_ in range(2))
            t1 = copy(mv[:, t, 2 * cb:2 * cb + 2, 0:256], b.ap.rearrange("p (h n) -> p h n", h=2), [last, d_b1["qk", 6]])
            d_mv[t, 2 * cb] = d_mv[t, 2 * cb + 1] = t1
            return [t1]

        mod[1] = MOD_PACE[1]
        proj_a(XT, 8, "w_mv", 0, 2, ev_mv)

        hss = tiny(8)
        rdn = tiny(8)
        d_h = {}
        hm = qkT

        def mlstm():
            t_em, t_ac = gate_columns()
            yield
            for h in range(4):
                ST = []
                for j in range(2):
                    n = 256 - 128 * j
                    b = psum.get()
                    mm([t_nm, t_misc, b.last], b.ap[:, 0:n], sel[:, h * 128:h * 128 + 128],
                       NM[:, j * 128:256], True, True)
                    last = mm([d_b1["qk", 4 + h], d_b1["qk", h]], b.ap[:, 256:256 + n],
                              qkT[:, 4 + h, j * 128:(j + 1) * 128], qkT[:, h, j * 128:256], True, True, True)
                    s = pb.get()
                    e = s.ap[:, 0:n]
                    t1 = V.op([last, t_ac, s.last], ve.scalar_tensor_tensor, e, b.ap[:, 0:n],
                              acol[:, j * 4 + h:j * 4 + h + 1], C("cmT", 0, n), ADD, ADD)
                    t1 = A.op([t1], ac.activation, e, e, ACT.Exp)
                    t1 = V.op([t1], ve.scalar_tensor_tensor, e, b.ap[:, 256:256 + n], 0.25 * 128.0 ** -0.5, e,
                              MUL, MUL)
                    b.free = [t1]
                    ST.append((s, t1))
                    yield
                for t in range(2):
                    b = psum.get()
                    for j in range(t + 1):
                        c = (t - j) * 128
                        last = mm([ST[j][1], d_mv[j, h], t_one, b.last], b.ap[:, 0:257], ST[j][0].ap[:, c:c + 128],
                                  mv[:, j, h, 0:257], j == 0, j == t, j == t)
                    i = t * 4 + h
                    t1 = V.op([last, t_em], ve.tensor_scalar, rdn[:, i:i + 1], b.ap[:, 256:257], -1.0, None, MUL)
                    t1 = V.op([t1], ve.scalar_tensor_tensor, rdn[:, i:i + 1], b.ap[:, 256:257], em[:, i:i + 1],
                              rdn[:, i:i + 1], MAX, MAX)
                    t1 = V.op([t1], ve.reciprocal, rdn[:, i:i + 1], rdn[:, i:i + 1])
                    o = hm[:, t * 4 + h, :]
                    t1 = A.op([t1], ac.activation, o, b.ap[:, 0:256], ACT.Copy, scale=rdn[:, i:i + 1])
                    b.free = [t1]
                    s = pt.get()
                    d_h[i] = A.op([t1, s.last], ac.activation, s.ap, o, ACT.Square, accum_out=hss[:, i:i + 1])
                    s.free = [d_h[i]]
                for s, _ in ST:
                    s.free = [last]
                lstm_end[:] = [last]
                yield

        lstm_end = []
        W.finish(gts)
        lstm = W.beside(mlstm(), LSTM_PACE)

        def ev_aqk(j, n, b, last):
            t = A.op([last], ac.activation, aqk[:, j:j + 2, :], grid(b.ap, 2), ACT.Copy,
                     scale=0.125 if j < 4 else 1.0)
            d_b1["aqk", j] = d_b1["aqk", j + 1] = t
            return [t]

        proj_b(XT, 8, "w_aqk", 0, 8, ev_aqk)

        def ev_av(t, cb, b, last):
            d_av[t] = copy(av[:, t, :], b.ap, [last])
            return [d_av[t]]

        proj_a(XT, 8, "w_av", 0, 1, ev_av)
        W.finish(lstm)
        for i in range(2):
            more_raw(mvf[:, i * 1024:(i + 1) * 1024], [lstm_end])

        def ev_az(j, n, b, last):
            o = azT[:, j:j + 2, :]
            t = A.op([last], ac.activation, o, grid(b.ap, 2), ACT.Tanh, scale=0.5)
            t = V.op([t], ve.scalar_tensor_tensor, o, o, 1.0, grid(b.ap, 2), ADD, MUL)
            d_b1["az", j] = d_b1["az", j + 1] = t
            return [t]

        nmx, smx = tiny(16), tiny(16)

        def attention(score, add_bias, value, dh, finish, may=lambda h: True, lag=3, ahead=None):
            items = [(h, t) for h in range(8) for t in range(2)]
            Ps, PTs, outs = {}, {}, {}

            def first(i):
                h, t = items[i]
                n = 128 * (t + 1)
                b = psum.get()
                last = score(h, t, n, b)
                s = pb.get()
                p = s.ap[:, 0:n]
                t1 = add_bias(h, t, n, b, p, [last, s.last])
                b.free = [t1]
                t2 = V.op([t1], ve.tensor_reduce, nmx[:, i:i + 1], p, AX.X, MAX, negate=True)
                t3 = A.op([t2], ac.activation, p, p, ACT.Exp, bias=nmx[:, i:i + 1], accum_out=smx[:, i:i + 1])
                Ps[i] = s, t3

            def norm(i):
                s, t3 = Ps[i]
                p = s.ap[:, 0:128 * (items[i][1] + 1)]
                t4 = V.op([t3], ve.reciprocal, smx[:, i:i + 1], smx[:, i:i + 1])
                t5 = V.op([t4], ve.tensor_scalar, p, p, smx[:, i:i + 1], None, MUL)
                Ps[i] = s, t5

            def second(i):
                h, t = items[i]
                s, tk = Ps[i]
                b = psum.get()
                for j in range(t + 1):
                    last = P.op([tk, b.last], pe.transpose, b.ap[:, j * 128:(j + 1) * 128],
                                s.ap[:, j * 128:(j + 1) * 128], ID)
                s.free = [last]
                d = pt.get()
                t1 = A.op([last, d.last], ac.copy, d.ap[:, 0:128 * (t + 1)], b.ap[:, 0:128 * (t + 1)])
                b.free = [t1]
                PTs[i] = d, t1

            def third(i):
                h, t = items[i]
                d, tk = PTs[i]
                per = 128 // dh
                if t == 0 and h % per == 0:
                    outs["b"] = psum.get()
                b = outs["b"]
                r0 = (h % per) * dh
                for j in range(t + 1):
                    vt, l = value(j, h)
                    last = mm([tk, vt, b.last], b.ap[r0:r0 + dh, t * 128:(t + 1) * 128], l,
                              d.ap[:, j * 128:(j + 1) * 128], j == 0, j == t, j == t)
                d.free = [last]
                if t == 1 and h % per == per - 1:
                    b.free = finish(h // per, b, last)

            n = len(items)
            for i in range(n + lag + 2):
                if ahead and i == 0:
                    for q in range(3):
                        ahead(*items[q])
                if ahead and i + 3 < n:
                    ahead(*items[i + 3])
                if i < n:
                    while not may(items[i][0]):
                        yield
                    first(i)
                if 0 <= i - 1 < n:
                    norm(i - 1)
                if 0 <= i - lag < n:
                    second(i - lag)
                if 0 <= i - lag - 2 < n:
                    third(i - lag - 2)
                yield

        def score1(h, t, n, b):
            r = slice(64 * (h % 2), 64 * (h % 2) + 64)
            return mm([d_b1["aqk", h // 2], d_b1["aqk", 4 + h // 2], b.last], b.ap[:, 0:n],
                      aqk[r, h // 2, t * 128:(t + 1) * 128], aqk[r, 4 + h // 2, 0:n], True, True, True)

        bmt = Turn([scr[:, 1024 + q * 256:1280 + q * 256] for q in range(5)])
        for q in range(2, 5):
            bmt.spots[q].free = [lstm_end]
        biases = []

        def ahead1(h, t):
            n = 128 * (t + 1)
            s = bmt.get()
            biases.append((s, G.op([t_TB, t_sel[t], s.last], po.tensor_tensor, s.ap[:, 0:n],
                                   TB[:, h, 256 - n:256].bitcast(f32), wsel[t][:, 0:n], ADD)))

        def bias1(h, t, n, b, p, toks_):
            s, t1 = biases.pop(0)
            t2 = V.op([t1, toks_], ve.tensor_tensor, p, b.ap[:, 0:n], s.ap[:, 0:n], ADD)
            s.free = [t2]
            return t2

        def fin1(k, b, last):
            s = wk.get()
            f = s.ap[:, 0:256]
            t1 = V.op([last, d_b1["az", k], s.last], ve.scalar_tensor_tensor, f, b.ap[:, 0:256], 0.5, azT[:, k, :],
                      MUL, MUL)
            MX.dep[8 + k] = split(f, MX.hi[8 + k], MX.lo[8 + k], [t1])
            s.free = [MX.dep[8 + k][1]]
            return [t1]

        mod[1] = MOD_PACE[2]
        proj_b(XT, 8, "w_az", 0, 4, ev_az)
        for r_ in lent:
            raw.spots.remove(r_)
        W.finish(idx)
        dsa = W.beside(attention(score1, bias1, lambda j, h: (d_av[j], av[:, j, h * 64:(h + 1) * 64]), 64, fin1,
                                 ahead=ahead1), DSA_PACE)

        def ev_moz(t, cb, b, last):
            c, z = cb // 2, cb % 2
            g = GT[:, t, c * 512:(c + 1) * 512]
            if not z:
                d_g[t, c] = A.op([last, dXT, [r_.free for r_ in lent]], ac.activation, g, b.ap, ACT.Tanh, scale=0.5)
                return [d_g[t, c]]
            if t == 0:
                mns[c] = rows("m_norm", c * 512, 512)
            mn, tmn = mns[c]
            s = wk.get()
            t1 = A.op([last, s.last], ac.activation, s.ap, b.ap, ACT.Tanh, scale=0.5)
            t2 = V.op([t1], ve.scalar_tensor_tensor, s.ap, s.ap, 1.0, b.ap, ADD, MUL)
            t3 = V.op([t2, d_g[t, c]], ve.scalar_tensor_tensor, g, g, 1.0, s.ap, ADD, MUL)
            s.free = [t3]
            t4 = V.op([t3, tmn], ve.tensor_tensor, g, g, mn.ap[:, 0:512], MUL)
            if t == 1:
                mn.free = [t4]
            d_g[t, c] = t4
            return [t2]

        mns = {}
        t_r = rsqrt(hss, hss, 8, 16.0 / 256, 16e-6, [d_h[i] for i in range(8)])
        proj_a(XT, 8, "w_moz", 0, 2, ev_moz)

        def gated(c):
            for t in range(2):
                for h in (2 * c, 2 * c + 1):
                    o = hm[:, t * 4 + h, :]
                    d = V.op([t_r, d_g[t, c]], ve.scalar_tensor_tensor, o, o, hss[:, t * 4 + h:t * 4 + h + 1],
                             GT[:, t, h * 256:(h + 1) * 256], MUL, MUL)
                d_hm[t] = d

        def gated_out(c):
            m = MX.part(4 * c, 4 * c + 4)
            m.hi2, m.lo2 = MX.hi2[2 * c:2 * c + 2], MX.lo2[2 * c:2 * c + 2]
            transposed(lambda t, k: hm[:, t * 4 + 2 * c + k // 2, (k % 2) * 128:(k % 2) * 128 + 128], d_hm, m, 4)
            MX.dep[4 * c:4 * c + 4] = m.dep

        d_hm = [None, None]
        gated(0)
        proj_a(XT, 8, "w_moz", 8, 2, lambda t, cb, b, l: ev_moz(t, 2 + cb, b, l),
               before=lambda cb, q: gated_out(0) if (cb, q) == (0, 1) else None)
        gated(1)
        d_r = [{}, {}]

        def ev_wo(t, cb, b, last):
            o = X[:, t, cb * 512:(cb + 1) * 512]
            d_r[t][cb] = V.op([last], ve.tensor_tensor, o, o, b.ap, ADD)
            return [d_r[t][cb]]

        def before_out(cb, q):
            if q == 2:
                gated_out(1)
                W.finish(dsa)
            if q == 4:
                d = split(pT.rearrange("p k n -> p (k n)"), PT2.hi2[0], PT2.lo2[0], [t_misc, MX.dep[8:12]])
                PT2.dep = [d, d]

        PT2 = Parts(ra, 6144, 2)
        proj_a(MX, 12, "w_out", 0, 1, ev_wo, False, before_out)
        pl = {}
        PL = aqk.rearrange("p k n -> p (k n)").rearrange("p (t n) -> p t n", t=2)

        ple_end = []

        def ev_ple(t, cb, b, last):
            o = PL[:, t, cb * 512:(cb + 1) * 512]
            t1 = A.op([last, MX.dep[8:12]], ac.copy, o, b.ap)
            pl[t, cb] = t1
            ple_end[:] = [last]
            return [t1]

        proj_a(PT2, 2, "w_ple", 0, 2, ev_ple)
        cosT, sinT, posf = scr[:, 0:256], scr[:, 256:512], scr[:, 512:770]
        dist = grid(scr[:, 770:1282], 2)
        t_tab, t_dist = [], []

        def tables():
            t_pf = V.op([t_misc, MX.dep[8:12]], ve.tensor_copy, posf, posi[:, 0:258])
            a1 = wk.get()
            ang, kk_ = a1.ap[:, 0:256], a1.ap[:, 256:512]
            TWO_PI = 6.283185307179586
            C1 = 6.28125
            C2 = round((TWO_PI - C1) * 2 ** 21) / 2 ** 21
            C3 = TWO_PI - C1 - C2
            MAGIC = 12582912.0
            t_ang = V.op([t_pf, a1.last], ve.tensor_scalar, ang, posf[:, 0:256], K("inv_freq"), None, MUL)
            for tab, quarter in ((sinT, 0.0), (cosT, 0.25)):
                t1 = V.op([t_ang, t_tab[-1:]], ve.tensor_scalar, kk_, ang, 1.0 / TWO_PI, quarter, MUL, ADD)
                t1 = V.op([t1], ve.tensor_scalar, kk_, kk_, MAGIC, None, ADD)
                t1 = V.op([t1], ve.tensor_scalar, kk_, kk_, -MAGIC, None, ADD)
                yield
                src = ang
                for cc in (C1, C2, C3):
                    t1 = V.op([t1], ve.scalar_tensor_tensor, tab, kk_, -cc, src, MUL, ADD)
                    src = tab
                if quarter:
                    a1.free = [t1]
                    t1 = V.op([t1], ve.tensor_scalar, tab, tab, TWO_PI / 4, None, ADD)
                t1 = V.op([t1], ve.tensor_scalar, tab, tab, 3.1415925, -3.1415925, MIN, MAX)
                t1 = A.op([t1], ac.activation, tab, tab, ACT.Sin)
                yield
                if not quarter:
                    t1 = V.op([t1, t_cols], ve.tensor_scalar, tab, tab, K("sign"), None, MUL)
                t_tab.append(t1)
            for t in range(2):
                t1 = V.op([t_pf], ve.tensor_scalar, dist[:, t, :], posf[:, 0:256], posf[:, 256 + t:257 + t], None,
                          SUB)
                t1 = V.op([t1], ve.scalar_tensor_tensor, dist[:, t, :], dist[:, t, :], -1.0, dist[:, t, :], MUL, MAX)
                n = 128 * (t + 1)
                t1 = V.op([t1], ve.tensor_tensor, dist[:, t, 0:n], dist[:, t, 0:n], C("cm", 256 - n, 256), SUB)
                yield
            t_dist.append(t1)

        tbl = W.beside(tables(), 1.0)
        proj_a(MX, 12, "w_out", 6, 1, lambda t, cb, b, l: ev_wo(t, 1, b, l), True)
        transposed(lambda t, k: X[:, t, k * 128:(k + 1) * 128], d_r, XT, 8, apart=True)
        d_x1 = [[None, None], [None, None]]

        d_x = [None, None]

        def rms_start(t):
            t1 = V.op([d_x1[t]], ve.tensor_tensor, fs[:, 2 * t:2 * t + 1], fs[:, 2 * t:2 * t + 1],
                      fs[:, 2 * t + 1:2 * t + 2], ADD)
            d_x[t] = rsqrt(fs[:, 2 * t:2 * t + 1], fs[:, 2 * t:2 * t + 1], 1, 1.0 / 1024, 1e-6, [t1])

        def rms_finish(t):
            t2 = V.op([d_x[t]], ve.tensor_scalar, X[:, t, 0:512], X[:, t, 0:512], fs[:, 2 * t:2 * t + 1], None, MUL)
            t3 = A.op([d_x[t]], ac.activation, X[:, t, 512:1024], X[:, t, 512:1024], ACT.Copy,
                      scale=fs[:, 2 * t:2 * t + 1])
            d_x[t] = {0: t2, 1: t3}

        def ev_gate(t, cb, b, last):
            s = wk.get()
            t1 = A.op([last, s.last], ac.activation, s.ap, b.ap, ACT.Tanh, scale=0.5)
            t2 = V.op([t1, pl[t, cb]], ve.scalar_tensor_tensor, s.ap, s.ap, 1.0, PL[:, t, cb * 512:(cb + 1) * 512],
                      ADD, MUL)
            o = X[:, t, cb * 512:(cb + 1) * 512]
            t3 = V.op([t2, XT.dep], ve.scalar_tensor_tensor, o, s.ap, 0.5, o, MUL, ADD)
            s.free = [t3]
            if t == 1 and cb == 1:
                rms_finish(0)
            fq = wk.get()
            d_x1[t][cb] = A.op([t3, fq.last], ac.activation, fq.ap, o, ACT.Square,
                               accum_out=fs[:, 2 * t + cb:2 * t + cb + 1])
            fq.free = [d_x1[t][cb]]
            if cb == 1:
                rms_start(t)
            return [t1]

        fs = tiny(4)
        proj_a(XT, 8, "w_gate", 0, 2, ev_gate, True)
        rms_finish(1)
        W.finish(tbl)

        more_raw(avf[:, 0:1024], [MX.dep[8:12]])
        parts_.add(ra[:, 6144:8192], [ple_end])
        W.pool = POOL_PART[3]
        ALPHA = 4.0 ** 0.25
        st = tiny(24)
        mv2 = tiny(8)

        def modulated(i, which, deps):
            m = MCi[i][0]
            a, s_ = (8, 0) if which == 0 else (24, 16)
            transposed(lambda t, k: X[:, t, k * 128:(k + 1) * 128], deps, XT, 8,
                       lambda k: m[:, a + k:a + k + 1], lambda k: m[:, s_ + k:s_ + k + 1], [until((i, 1 if which == 0 else 4))], apart=True)

        d_g2 = [None, None]

        def gain(name, off, bias):
            dep = XT.dep
            for n in range(1 + bias):
                g, tg_ = rows(name, off + n * 1024, 1024)
                tg_ = A.op([tg_], ac.activation, g.ap, g.ap, ACT.Copy, scale=ALPHA)
                d_g2[0] = V.op([dep, d_g2[0], tg_], ve.tensor_tensor, X[:, 0, :], X[:, 0, :], g.ap, ADD if n else MUL)
                d_g2[1] = G.op([dep, d_g2[1], tg_], po.tensor_tensor, X[:, 1, :], X[:, 1, :], g.ap, ADD if n else MUL)
                g.free = [d_g2[0], d_g2[1]]
                yield
                yield

        d_z = [None, None]
        later = []

        def resid(r, i, t, cb, b, last):
            W.finish(gn)
            cs = slice(cb * 512, (cb + 1) * 512)
            s = wk.get()
            t1 = V.op([last, until((i, 5 if r else 2)), s.last], ve.tensor_tensor, s.ap, b.ap, R2[:, r, cs], MUL)
            if t == 1 and cb == 1:
                ln_finish(0)
                if final:
                    final_gain(G, po, 0, 512, 1024)
            if i == 0 and t == 1 and cb == 1:
                r2_used[r] = [t1]
            x = X[:, t, cs]
            if cb == 0 and r == 0:
                t2 = V.op([t1, d_g2[t]], ve.tensor_tensor, x, x, s.ap, ADD)
                s.free = [t2]
                V.op([t2], ve.bn_stats, st[:, 2 * t * 6:2 * t * 6 + 6], x)
            elif cb == 0:
                t2 = G.op([t1, d_g2[t]], po.tensor_tensor, x, x, s.ap, ADD)
                later.append((s, t2))
            else:
                t2 = V.op([t1, d_g2[t]], ve.tensor_tensor, x, x, s.ap, ADD)
                s.free = [t2]
                t3 = V.op([t2], ve.bn_stats, st[:, (2 * t + 1) * 6:(2 * t + 1) * 6 + 6], x)
                t2 = t3
                if r:
                    s, t2 = later.pop(0)
                    s.free = [t2]
                    t2 = V.op([t2, t3], ve.bn_stats, st[:, 2 * t * 6:2 * t * 6 + 6], X[:, t, 0:512])
                m = mv2[:, t * 4:t * 4 + 4]
                t1_ = V.op([t2], ve.bn_aggr, m[:, 0:2], st[:, t * 12:(t + 1) * 12].rearrange("p (c s) -> p c s", c=2))
                d_z[t] = rsqrt(m[:, 1:2], m[:, 2:3], 1, 1.0, 1e-5, [t1_])
                if t and final:
                    final_gain(V, ve, 0, 0, 512)
            return [t1]

        normed = {}
        final = []
        s_out = sem("s_out")
        sent = []

        def final_gain(q, eng, t, c0, c1):
            (g, tg_), (bb, tb_) = final
            x = X[:, t, c0:c1]
            t1 = q.op([normed[t][0], normed[t][1], tg_], eng.tensor_tensor, x, x, g.ap[:, c0:c1], MUL)
            t1 = q.op([t1, tb_], eng.tensor_tensor, x, x, bb.ap[:, c0:c1], ADD)
            sent.append(S.dma([t1], s_out, 16 * len(sent) + 16, nc.sync.dma_start,
                              out[t * 128:(t + 1) * 128, c0:c1], x))

        def ln_finish(t, cut=512):
            m = mv2[:, t * 4:t * 4 + 4]
            t2 = V.op([d_z[t]], ve.tensor_scalar, m[:, 3:4], m[:, 0:1], m[:, 2:3], -1.0, MUL, MUL)
            t3 = V.op([t2], ve.tensor_scalar, X[:, t, 0:cut], X[:, t, 0:cut], m[:, 2:3], m[:, 3:4], MUL, ADD)
            t4 = A.op([t2], ac.activation, X[:, t, cut:1024], X[:, t, cut:1024], ACT.Identity, bias=m[:, 3:4],
                      scale=m[:, 2:3])
            normed[t] = {0: t3, 1: t4}

        def layer_norm():
            ln_finish(1)
            return [normed[0], normed[1]]

        gp = Turn([ra[:, q * 1024:(q + 1) * 1024] for q in range(3)])

        def ffn(i):
            outs = [[psum.get() for _ in range(2)] for _ in range(2)]
            held = []

            def second(u, last_one):
                g, dg = held.pop(0)
                W.still = last_one
                if last_one:
                    got = [W.next(f"ffn_o{i}", 2 * u + e) for e in range(2)]
                for t, e in ((0, 0), (0, 1), (1, 0), (1, 1)) if last_one else ((0, 0), (1, 0), (0, 1), (1, 1)):
                    if last_one:
                        w, hi, lo, tw = got[e]
                    elif t == 0:
                        w, hi, lo, tw = W.next(f"ffn_o{i}", 2 * u + e)
                    k0 = u == 0 and e == 0
                    k1 = last_one and e == 1
                    if True:
                        c = slice(e * 256 + t * 128, e * 256 + (t + 1) * 128)
                        cl = slice(512 + e * 256 + t * 128, 512 + e * 256 + (t + 1) * 128)
                        for cb in range(2):
                            cs = slice(cb * 512, (cb + 1) * 512)
                            last = mm3([tw, dg, outs[t][cb].last], outs[t][cb].ap, (g.ap[:, c], g.ap[:, cl]),
                                       (hi[:, cs], lo[:, cs]), k0, k1, k1 or (t == 1 and cb == 1))
                            if k1:
                                outs[t][cb].free = resid(1, i, t, cb, outs[t][cb], last)
                    if t == 1 and not last_one:
                        W.done(w, last)
                if last_one:
                    W.done(got[0][0], last)
                    W.done(got[1][0], last)
                g.free = [last]

            for u in range(11):
                hold = {}
                if i and u == 8:
                    final.extend([rows("ln", 6144, 1024), rows("ln", 7168, 1024)])

                def eva(j, n, b, last):
                    s = wk.get()
                    t1s = [A.op([last, s.last, t_cols], ac.activation, s.ap[:, q * 256:(q + 1) * 256],
                                b.ap[:, q * 256:(q + 1) * 256], ACT.Identity, bias=K("fconv_b", i * 22 + 2 * u + q),
                                scale=K("fconv_w", i * 66 + 44 + 2 * u + q)) for q in range(2)]
                    fr = [t1s, t1s]
                    for j2 in (1, 0):
                        sh = 2 - j2
                        for q in range(2):
                            o = s.ap[:, q * 256:(q + 1) * 256]
                            fr[q] = V.op([fr[q]], ve.scalar_tensor_tensor, o[:, sh:256],
                                         b.ap[:, q * 256:(q + 1) * 256 - sh],
                                         K("fconv_w", i * 66 + 22 * j2 + 2 * u + q), o[:, sh:256], MUL, ADD)

                    def gelu():
                        hold["a"] = s, A.op(fr, ac.activation, s.ap, s.ap, ACT.Gelu_apprx_tanh)

                    W.soon.append(gelu)
                    return fr

                def evb(j, n, b, last):
                    s, t1 = hold["a"]
                    g = gp.get()
                    t2 = V.op([last, t1], ve.tensor_tensor, s.ap, s.ap, b.ap, MUL)
                    d = split(s.ap, g.ap[:, 0:512], g.ap[:, 512:1024], [t2, g.last], pool=True)
                    s.free = [d[1]]
                    held.append((g, d))
                    return [t2]

                proj_b(XT, 8, f"ffn_a{i}", 2 * u, 2, eva, u == 0)
                proj_b(XT, 8, f"ffn_b{i}", 2 * u, 2, evb)
                if u:
                    second(u - 1, False)
            second(10, True)

        modulated(0, 0, d_x)
        gn = W.beside(gain("norm_final", 0, False), 0.7)
        at[0] = 0
        cqf = take(1024)
        cq = grid(cqf, 2)
        qT, kT = grid(take(2048), 8), grid(take(2048), 8)
        qrf = take(1024)
        qr, kr, vv = grid(qrf, 4), take(256), grid(take(2048), 2)
        CT, OT = Parts(ra, 0, 4), Parts(ra, 2048, 8)

        cs4 = tiny(4)
        d_cq = [None, None]

        def ev_cq(t, cb, b, last):
            t1 = None
            s = wk.get()
            for c in range(2):
                t1 = A.op([last, s.last], ac.activation, s.ap[:, c * 256:(c + 1) * 256],
                          b.ap[:, c * 256:(c + 1) * 256], ACT.Square,
                          accum_out=cs4[:, 2 * t + c:2 * t + c + 1])
            s.free = [t1]
            t1 = rsqrt(cs4[:, 2 * t:2 * t + 2], cs4[:, 2 * t:2 * t + 2], 2, 1.0 / 256, 1e-6, [t1])
            for c in range(2):
                t2 = V.op([t1], ve.tensor_scalar, cq[:, t, c * 256:(c + 1) * 256], b.ap[:, c * 256:(c + 1) * 256],
                          cs4[:, 2 * t + c:2 * t + c + 1], None, MUL)
            d_cq[t] = t2
            return [t2]

        proj_a(XT, 8, "mla_c", 0, 1, ev_cq)

        def rope(o, b, last):
            s = wk.get()
            t1 = V.op([last, t_tab, s.last], ve.tensor_tensor, s.ap[:, 0:256], b.ap[:, 0:256], cosT, MUL)
            t2 = V.op([last, t_tab], ve.tensor_tensor, s.ap[:, 256:512], b.ap[:, 256:512], sinT, MUL)
            t3 = G.op([t1, t2], po.tensor_tensor, o, s.ap[:, 0:256], s.ap[:, 256:512], ADD)
            s.free = [t3]
            return t2, t3

        d_kr = []

        def ev_kr(j, n, b, last):
            t2, t3 = rope(kr, b, last)
            d_kr.append(t3)
            return [t2]

        proj_b(XT, 8, "mla_kr", 0, 2, ev_kr)
        transposed(lambda t, k: cq[:, t, k * 128:(k + 1) * 128], d_cq, CT, 4,
                   lambda k: K("q_norm", k) if k < 2 else K("kv_norm", k - 2), order=(2, 0))
        d_q, d_k, d_qr, d_v = [None] * 8, [None] * 8, [None] * 4, {}

        def ev_k(j, n, b, last):
            t1 = copy(kT[:, j:j + 2, :], grid(b.ap, 2), [last])
            d_k[j] = d_k[j + 1] = t1
            return [t1]

        def ev_v(t, cb, b, last):
            d_v[t, cb] = copy(vv[:, t, cb * 512:(cb + 1) * 512], b.ap, [last])
            return [d_v[t, cb]]

        proj_a(CT.part(2, 4), 2, "mla_uv", 0, 2, ev_v)

        def ev_q(j, n, b, last):
            g, r = j // 8, j % 8
            if r < 4:
                h = 4 * g + r
                t1 = copy(qT[:, h:h + 2, :], grid(b.ap, 2), [last])
                d_q[h] = d_q[h + 1] = t1
                return [t1]
            p = 2 * g + (r - 4) // 2
            t2, t3 = rope(qr[:, p, :], b, last)
            d_qr[p] = t3
            return [t2]

        def score2(h, t, n, b):
            r = slice(64 * (h % 2), 64 * (h % 2) + 64)
            mm([d_q[h], d_k[h], b.last], b.ap[:, 0:n], qT[:, h, t * 128:(t + 1) * 128], kT[:, h, 0:n], True, False)
            return mm([d_qr[h // 2], d_kr], b.ap[:, 0:n], qr[r, h // 2, t * 128:(t + 1) * 128], kr[r, 0:n],
                      False, True, True)

        def bias2(h, t, n, b, p, toks_):
            return V.op(toks_, ve.scalar_tensor_tensor, p, b.ap[:, 0:n], 192.0 ** -0.5, C("cm", 256 - n, 256),
                        MUL, ADD)

        def fin2(k, b, last):
            OT.dep[k] = split(b.ap[:, 0:256], OT.hi[k], OT.lo[k], [last, extra_end])
            return OT.dep[k]

        def val2(j, h):
            return d_v[j, h // 4], vv[:, j, h * 128:(h + 1) * 128]

        extra_end = []
        mla = attention(score2, bias2, val2, 128, fin2, lambda h: d_qr[h // 2] is not None)
        for g in range(2):
            proj_b(CT.part(2, 4), 2, "mla_uk", g, 4, lambda j, n, b, l: ev_k(4 * g + j, n, b, l))
            proj_b(CT.part(0, 2), 2, "mla_uq", 2 * g, 8, lambda j, n, b, l: ev_q(8 * g + j, n, b, l))
            if g == 0:
                mt = W.beside(mla, MLA_PACE)

        def with_heads(task):

            def before(cb, q):
                while cb == 0 and (OT.dep[2 * q] is None or OT.dep[2 * q + 1] is None):
                    next(task[0])
                    W.step(SHARE)
            return before

        proj_a(OT, 8, "mla_o", 0, 2, lambda t, cb, b, l: resid(0, 0, t, cb, b, l), True,
               with_heads(mt))
        mla_end = (P.sem, P.count)
        d1 = layer_norm()
        mod[1] = MOD_PACE[4]
        modulated(0, 1, d1)
        W.pool = POOL_PART[4]
        gn = W.beside(gain("ln", 0, True), 0.7)
        more_raw(cqf, [mla_end])
        more_raw(qrf, [mla_end])
        extra = parts_.add(ra[:, 4096:6144], [mla_end])
        ffn(0)
        parts_.spots.remove(extra)
        d2 = layer_norm()

        mod[1] = MOD_PACE[5]
        modulated(1, 0, d2)
        W.pool = POOL_PART[5]
        gn = W.beside(gain("ln", 2048, True), 0.7)

        def ev_q3(j, n, b, last):
            t1 = A.op([last], ac.activation, qT[:, j:j + 2, :], grid(b.ap, 2), ACT.Copy, scale=128.0 ** -0.5)
            d_q[j] = d_q[j + 1] = t1
            return [t1]

        def score3(h, t, n, b):
            return mm([d_q[h], d_k[h], b.last], b.ap[:, 0:n], qT[:, h, t * 128:(t + 1) * 128], kT[:, h, 0:n],
                      True, True, True)

        def bias3(h, t, n, b, p, toks_):
            return V.op([toks_, t_dist], ve.scalar_tensor_tensor, p, dist[:, t, 0:n], -(2.0 ** -(h + 1)),
                        b.ap[:, 0:n], MUL, ADD)

        proj_a(XT, 8, "moba_v", 0, 2, ev_v)
        extra_end.append(extra.free)
        moba = W.beside(attention(score3, bias3, val2, 128, fin2, lambda h: d_k[h] is not None), MOBA_PACE)
        d_k[0:8] = [None] * 8
        OT.dep[0:8] = [None] * 8
        for h in range(0, 8, 2):
            proj_b(XT, 8, "moba_q", h, 2, lambda j, n, b, l: ev_q3(h + j, n, b, l))
            proj_b(XT, 8, "moba_k", h, 2, lambda j, n, b, l: ev_k(h + j, n, b, l))
        proj_a(OT, 8, "moba_o", 0, 2, lambda t, cb, b, l: resid(0, 1, t, cb, b, l), True,
               with_heads(moba))
        d1 = layer_norm()
        mod[1] = MOD_PACE[6]
        modulated(1, 1, d1)
        gn = W.beside(gain("ln", 4096, True), 0.7)
        parts_.add(ra[:, 4096:6144], [(P.sem, P.count)])
        ffn(1)
        ln_finish(1, 704)
        final_gain(G, po, 1, 704, 1024)
        final_gain(V, ve, 1, 0, 704)
        S.wait(sent[-1:])

        block = ctx.enter_context(nc.Block())

        @block.sync
        def _(eng):
            S.emit(eng)

        @block.gpsimd
        def _(eng):
            G.emit(eng)

        @block.scalar
        def _(eng):
            A.emit(eng)

        @block.vector
        def _(eng):
            V.emit(eng)

        @block.tensor
        def _(eng):
            P.emit(eng)


def constants():
    c = np.zeros((128, NCONST), np.float32)

    def put(name, a):
        c[:a.shape[0], CONST_AT[name][0]:CONST_AT[name][0] + a.shape[1]] = a

    put("ident", np.eye(128, dtype=np.float32))
    put("ones", np.ones((128, 256), np.float32))
    sel = np.zeros((4, 4, 128), np.float32)
    for h in range(4):
        sel[h, h] = 1.0
    d = np.maximum(255 - np.arange(383), 0)
    large = 16 + (np.log(np.maximum(d, 1).astype(np.float32) / np.float32(16)) / np.log(8.0) * 16).astype(np.int32)
    bucket = np.where(d < 16, d, np.minimum(large, 31))
    oh = np.zeros((32, 384), np.float32)
    oh[bucket, np.arange(383)] = 1.0
    i = np.arange(128)
    up = np.where(i[None, :] > i[:, None], -BIG, 0.0).astype(np.float32)
    z = np.zeros((128, 128), np.float32)
    put("cm", np.concatenate([z, up], 1))
    put("cmT", np.concatenate([up.T, z], 1))
    return c, sel.reshape(4, 512), oh


def pack_b(w):
    nk, nb = w.shape[0] // 128, w.shape[1] // 128
    per = 8 // nk
    nu = -(-nb // per)
    out = np.zeros((nu, 128, per, nk, 128), w.dtype)
    for j in range(nb):
        out[j // per, :, j % per] = w[:, j * 128:(j + 1) * 128].reshape(nk, 128, 128).transpose(1, 0, 2)
    return out.reshape(nu, 128, 1024)


def pack_a(w):
    nk, ncb = w.shape[0] // 128, w.shape[1] // 512
    return w.reshape(nk // 2, 2, 128, ncb, 512).transpose(3, 0, 2, 1, 4).reshape(ncb * nk // 2, 128, 1024)


def layout(I):
    f = np.float32
    a = {k: np.asarray(v) for k, v in I.items()}
    o = {}
    o["x"] = a["x"][0]
    o["pT"] = np.ascontiguousarray(a["p"][0, 0].T)
    o["rel_bias"] = a["rel_bias"]
    o["pos_r"] = a["positions_2"].reshape(1, 256)
    o["pos_c"] = np.ascontiguousarray(a["positions_2"].reshape(2, 128).T)
    o["consts"], o["sel"], o["onehot"] = constants()
    c = np.zeros((128, NCOL), f)

    def put(name, m):
        c[:m.shape[0], COL_AT[name][0]:COL_AT[name][0] + m.shape[1]] = m

    def col(v):
        return v.reshape(-1, 128).T

    put("norm_in", col(a["norm_in"][0]))
    put("conv_w", col(a["conv_w"][0].reshape(-1)))
    put("fconv_w", col(a["ffn_conv_w_2"].reshape(-1)))
    put("fconv_b", col(a["ffn_conv_b_2"].reshape(-1)))
    put("q_norm", col(a["mla_q_norm_2"][0]))
    put("kv_norm", col(a["mla_kv_norm_2"][0]))
    put("mod_b", col(a["mod_b_2"].reshape(-1)))
    put("c", col(a["c_2"][0]))
    put("b_gate", a["b_gate"][0].reshape(2, 4).T)
    inv = (10000.0 ** (-np.arange(32, dtype=f) / f(32))).astype(f)
    put("inv_freq", np.tile(inv, 4)[:, None])
    put("nf", col(a["norm_final"]))
    put("ln", col(np.stack([a["ln_g_2"], a["ln_b_2"]], 2).reshape(-1)))
    put("sign", np.tile(np.repeat(np.array([-1.0, 1.0], f), 32), 2)[:, None])
    o["cols"] = c
    w = a["w_in"][0]
    cut = np.cumsum([0, 512, 512, 1024, 1024, 1024, 8, 512, 512, 512, 512, 512, 64, 8])
    mq, mk, m_v, mo, mz, mif, aq, ak, a_v, az, iq, ik, iw = (w[:, cut[i]:cut[i + 1]] for i in range(13))
    o["w_iq"] = pack_b(np.concatenate([iq, ik, ik], 1))
    o["w_mqk"] = pack_b(np.concatenate([mq, mk], 1))
    o["w_mv"], o["w_av"] = pack_a(m_v), pack_a(a_v)
    o["w_aqk"], o["w_az"] = pack_b(np.concatenate([aq, ak], 1)), pack_b(az)
    g = np.zeros((1, 128, 8, 96), f)
    for at, m in ((0, mif[:, 0:4]), (32, mif[:, 4:8]), (64, iw)):
        g[0, :, :, at:at + m.shape[1]] = m.reshape(8, 128, -1).transpose(1, 0, 2)
    o["w_g"] = g.reshape(1, 128, 768)
    o["w_moz"] = pack_a(np.concatenate([mo[:, :512], mz[:, :512], mo[:, 512:], mz[:, 512:]], 1))
    o["w_out"] = pack_a(a["w_out"][0])
    o["w_ple"] = pack_a(a["w_ple"][0])
    o["w_gate"] = pack_a(a["w_ple_gate"][0])
    o["m_norm"], o["norm_final"] = a["m_norm"], a["norm_final"].reshape(1, -1)
    o["mod_b"] = a["mod_b_2"]
    o["mod_w"] = np.ascontiguousarray(a["mod_w_2"].reshape(2, 8, 128, 6, 1024).transpose(0, 3, 1, 2, 4)).reshape(
        96, 128, 1024)
    o["ln"] = np.ascontiguousarray(np.stack([a["ln_g_2"], a["ln_b_2"]], 2).reshape(4, 2048))
    for i in range(2):
        o[f"ffn_a{i}"] = pack_b(a["ffn_w_in_2"][i][:, 0:2816])
        o[f"ffn_b{i}"] = pack_b(a["ffn_w_in_2"][i][:, 2816:])
        o[f"ffn_o{i}"] = a["ffn_w_out_2"][i].reshape(22, 128, 1024)
    w = a["mla_w_in_2"][0]
    o["mla_c"] = pack_a(w[:, 0:512])
    r, s = w[:, 512:576], np.concatenate([w[:, 544:576], w[:, 512:544]], 1)
    o["mla_kr"] = pack_b(np.concatenate([r, r, s, s], 1))
    w = a["mla_w_uq_2"][0].reshape(256, 8, 192)
    parts = []
    for g in range(2):
        parts.append(w[:, 4 * g:4 * g + 4, 0:128].reshape(256, 512))
        for j in (2 * g, 2 * g + 1):
            r = w[:, 2 * j:2 * j + 2, 128:192]
            parts += [r.reshape(256, 128), np.concatenate([r[:, :, 32:], r[:, :, :32]], 2).reshape(256, 128)]
    o["mla_uq"] = pack_b(np.concatenate(parts, 1))
    w = a["mla_w_ukv_2"][0].reshape(256, 8, 256)
    o["mla_uk"] = pack_b(w[:, :, 0:128].reshape(256, 1024))
    o["mla_uv"] = pack_a(w[:, :, 128:256].reshape(256, 1024))
    o["mla_o"] = pack_a(a["mla_w_o_2"][0])
    w = a["moba_w_in_2"][0]
    o["moba_q"], o["moba_k"] = pack_b(w[:, 0:1024]), pack_b(w[:, 1024:2048])
    o["moba_v"] = pack_a(w[:, 2048:3072])
    o["moba_o"] = pack_a(a["moba_w_o_2"][0])
    return {k: np.ascontiguousarray(v) for k, v in o.items()}


def kernel(**inputs):
    import concourse.bacc as bacc
    from concourse.bass_utils import run_bass_kernel_spmd

    nc = bacc.Bacc("TRN2", target_bir_lowering=False, num_devices=1)
    arrays = {f"in_{k}": v for k, v in layout(inputs).items()}
    D = {k[3:]: nc.dram_tensor(k, v.shape, mybir.dt.from_np(v.dtype), kind="ExternalInput").ap()
         for k, v in arrays.items()}
    out = nc.dram_tensor("out_0", (256, 1024), mybir.dt.float32, kind="ExternalOutput").ap()
    build(nc, D, out)
    r = run_bass_kernel_spmd(nc, [arrays], core_ids=[0])
    return r.results[0]["out_0"].reshape(1, 256, 1024)
```
